# Optimizing a Trainium2 kernel written in Bass

```python
import math
import jax, jax.numpy as jnp
from jax import lax
import numpy as np

D_MODEL = 1024
BATCH = 1
SEQ = 512
DEPTH = 2

N_MEM = 256
HEAD_DIM = 64
MIX_WIDTH = 3 * D_MODEL // 4
MIX_HEADS = MIX_WIDTH // HEAD_DIM
MEM_HEADS = 4
MEM_WIDTH = MEM_HEADS * HEAD_DIM
NSA_KV_GROUPS = 4
NSA_GROUP_SIZE = MIX_HEADS // NSA_KV_GROUPS
KV_WIDTH = NSA_KV_GROUPS * HEAD_DIM
CMP_BLOCK = 32
CMP_STRIDE = 16
CMP_HIDDEN = 2 * HEAD_DIM
SEL_BLOCK = 64
SEL_TOPN = 16
WINDOW = 512
NSA_Q_BLOCK = 64
FORCE_SCORE = 1.0e4
NSA_IN = MIX_WIDTH + 6 * KV_WIDTH + 3 * MIX_HEADS + MEM_WIDTH
DECAY_LORA = 64
ICLR_LORA = 64
GATE_LORA = 160
RW_SHIFT = 3 * MIX_WIDTH + DECAY_LORA + ICLR_LORA + GATE_LORA
RW_IN = RW_SHIFT + MEM_WIDTH
GN_EPS = 64e-5
FFN_HIDDEN = -(-8 * D_MODEL // (3 * 256)) * 256
N_NSA = (DEPTH + 1) // 2
N_RWKV = DEPTH // 2
RMS_EPS = 1e-6
NEG_INF = -1e30


def _rmsnorm(x, g):
    xf = x.astype(jnp.float32)
    y = xf * lax.rsqrt(jnp.mean(xf * xf, axis=-1, keepdims=True) + RMS_EPS)
    return (y * g.astype(jnp.float32)).astype(x.dtype)

def _split(x, sizes):
    idx = [int(i) for i in np.cumsum(sizes)[:-1]]
    return jnp.split(x, idx, axis=-1)

def _alibi_slopes(n):
    def pow2(m):
        start = 2.0 ** (-8.0 / m)
        return [start ** (i + 1) for i in range(m)]
    c = 2 ** int(math.floor(math.log2(n)))
    s = pow2(c)
    if c < n:
        s = s + pow2(2 * c)[0::2][: n - c]
    return np.asarray(s, dtype=np.float32)

def _masked_softmax(s, mask):
    p = jax.nn.softmax(jnp.where(mask, s, NEG_INF), axis=-1)
    return p * mask

def _compress(kv, pos, w1, w2):
    S = kv.shape[1]
    n_cmp = (S - CMP_BLOCK) // CMP_STRIDE + 1
    idx = jnp.arange(n_cmp)[:, None] * CMP_STRIDE + jnp.arange(CMP_BLOCK)[None, :]
    blocks = kv[:, idx] + pos[None, None, :, None, :]
    hid = jax.nn.gelu(jnp.einsum('bnlgd,lde->bnge', blocks, w1))
    return jnp.einsum('bnge,ed->bngd', hid, w2)

def _nsa_mixer(h, w_in, gate_b, cmp_pos, cmp_w1, cmp_w2):
    B, S, _ = h.shape
    G, R, Dh, QB = NSA_KV_GROUPS, NSA_GROUP_SIZE, HEAD_DIM, NSA_Q_BLOCK
    proj = h @ w_in
    q, kc, vc, ks, vs, kw, vw, gl, q_mem = _split(
        proj, [MIX_WIDTH] + [KV_WIDTH] * 6 + [3 * MIX_HEADS, MEM_WIDTH])
    q = q.reshape(B, S, G, R, Dh)
    kc, vc, ks, vs, kw, vw = (t.reshape(B, S, G, Dh) for t in (kc, vc, ks, vs, kw, vw))
    gates = jax.nn.sigmoid(gl + gate_b).reshape(B, S, 3, G, R)

    kc_b = _compress(kc, cmp_pos[0], cmp_w1[0], cmp_w2[0])
    vc_b = _compress(vc, cmp_pos[1], cmp_w1[1], cmp_w2[1])
    n_cmp = kc_b.shape[1]
    n_blk = S // SEL_BLOCK
    n_sel = min(SEL_TOPN, n_blk)
    ks_blk = ks.reshape(B, n_blk, SEL_BLOCK, G, Dh).transpose(0, 3, 1, 2, 4)
    vs_blk = vs.reshape(B, n_blk, SEL_BLOCK, G, Dh).transpose(0, 3, 1, 2, 4)
    kw_pad = jnp.pad(kw, ((0, 0), (WINDOW, 0), (0, 0), (0, 0)))
    vw_pad = jnp.pad(vw, ((0, 0), (WINDOW, 0), (0, 0), (0, 0)))

    slopes = jnp.asarray(_alibi_slopes(MIX_HEADS).reshape(G, R))[None, :, :, None, None]
    cmp_start = jnp.arange(n_cmp) * CMP_STRIDE
    cmp_end = cmp_start + CMP_BLOCK - 1
    sel_start = jnp.arange(n_blk) * SEL_BLOCK
    overlap = ((cmp_start[:, None] <= sel_start[None, :] + SEL_BLOCK - 1)
               & (cmp_end[:, None] >= sel_start[None, :])).astype(jnp.float32)
    blk_ids = jnp.arange(n_blk)
    b_idx = jnp.arange(B)[:, None, None, None]
    g_idx = jnp.arange(G)[None, :, None, None]
    scale = HEAD_DIM ** -0.5

    def chunk(c0):
        t = c0 + jnp.arange(QB)
        qc = lax.dynamic_slice_in_dim(q, c0, QB, axis=1)
        dist_c = t[:, None] - cmp_end[None, :]
        s_c = jnp.einsum('bqgrd,bngd->bgrqn', qc, kc_b).astype(jnp.float32) * scale \
            - slopes * dist_c.astype(jnp.float32)
        p_c = _masked_softmax(s_c, dist_c >= 0)
        o_c = jnp.einsum('bgrqn,bngd->bqgrd', p_c.astype(vc_b.dtype), vc_b)
        imp = jnp.einsum('bgrqn,nj->bgqj', p_c, overlap)
        tb = (t // SEL_BLOCK)[:, None]
        valid = blk_ids[None, :] <= tb
        forced = (blk_ids[None, :] == 0) | (blk_ids[None, :] == tb) | (blk_ids[None, :] == tb - 1)
        score = jnp.where(valid, jnp.where(forced, FORCE_SCORE, imp), -jnp.inf)
        top_s, top_i = lax.top_k(score, n_sel)
        kg = ks_blk[b_idx, g_idx, top_i].reshape(B, G, QB, n_sel * SEL_BLOCK, Dh)
        vg = vs_blk[b_idx, g_idx, top_i].reshape(B, G, QB, n_sel * SEL_BLOCK, Dh)
        pos = (top_i[..., None] * SEL_BLOCK + jnp.arange(SEL_BLOCK)).reshape(B, G, QB, -1)
        ok = jnp.broadcast_to(jnp.isfinite(top_s)[..., None],
                              (B, G, QB, n_sel, SEL_BLOCK)).reshape(B, G, QB, -1)
        dist_s = t[None, None, :, None] - pos
        mask_s = ok & (dist_s >= 0)
        s_s = jnp.einsum('bqgrd,bgqkd->bgrqk', qc, kg).astype(jnp.float32) * scale \
            - slopes * dist_s[:, :, None].astype(jnp.float32)
        p_s = _masked_softmax(s_s, mask_s[:, :, None])
        o_s = jnp.einsum('bgrqk,bgqkd->bqgrd', p_s.astype(vg.dtype), vg)
        kwc = lax.dynamic_slice_in_dim(kw_pad, c0, WINDOW + QB, axis=1)
        vwc = lax.dynamic_slice_in_dim(vw_pad, c0, WINDOW + QB, axis=1)
        kp = c0 - WINDOW + jnp.arange(WINDOW + QB)
        dist_w = t[:, None] - kp[None, :]
        mask_w = (kp[None, :] >= 0) & (dist_w >= 0) & (dist_w < WINDOW)
        s_w = jnp.einsum('bqgrd,bkgd->bgrqk', qc, kwc).astype(jnp.float32) * scale \
            - slopes * dist_w.astype(jnp.float32)
        p_w = _masked_softmax(s_w, mask_w)
        o_w = jnp.einsum('bgrqk,bkgd->bqgrd', p_w.astype(vwc.dtype), vwc)
        gc = lax.dynamic_slice_in_dim(gates, c0, QB, axis=1)[..., None]
        return gc[:, :, 0] * o_c + gc[:, :, 1] * o_s + gc[:, :, 2] * o_w

    starts = jnp.arange(S // QB) * QB
    o = lax.map(chunk, starts)
    o = jnp.moveaxis(o, 0, 1).reshape(B, S, MIX_WIDTH)
    return o, q_mem

def _wkv7_scan(r, w, k, v, a, b):
    B, S, H, N = r.shape

    def step(state, inp):
        r_t, w_t, k_t, v_t, a_t, b_t = inp
        sa = jnp.einsum('bhvk,bhk->bhv', state, a_t)
        state = state * w_t[:, :, None, :] + sa[..., None] * b_t[:, :, None, :] \
            + v_t[..., None] * k_t[:, :, None, :]
        return state, jnp.einsum('bhvk,bhk->bhv', state, r_t)

    xs = tuple(jnp.moveaxis(t, 1, 0) for t in (r, w, k, v, a, b))
    s0 = jnp.zeros((B, H, N, N), jnp.float32)
    _, y = lax.scan(step, s0, xs)
    return jnp.moveaxis(y, 0, 1)

def _rwkv7_mixer(h, w_in, mu, w0, w2, a0, a2, g2, k_k, k_a, r_k, lnx_w, lnx_b):
    B, S, _ = h.shape
    H, N = MIX_HEADS, HEAD_DIM
    proj = h @ w_in
    z, q_mem = proj[..., :RW_SHIFT], proj[..., RW_SHIFT:]
    z_prev = jnp.pad(z, ((0, 0), (1, 0), (0, 0)))[:, :-1]
    z = z + (z_prev - z) * mu
    r, k, v, zw, za, zg = _split(z, [MIX_WIDTH] * 3 + [DECAY_LORA, ICLR_LORA, GATE_LORA])
    w_log = -jax.nn.softplus(-(w0 + jnp.tanh(zw) @ w2)) - 0.5
    decay = jnp.exp(-jnp.exp(w_log.astype(jnp.float32)))
    a = jax.nn.sigmoid(a0 + za @ a2)
    g = jax.nn.sigmoid(zg) @ g2
    kk = (k * k_k).astype(jnp.float32).reshape(B, S, H, N)
    kk = kk / jnp.maximum(jnp.sqrt(jnp.sum(kk * kk, axis=-1, keepdims=True)), 1e-12)
    k = k * (1 + (a - 1) * k_a)

    def heads(t):
        return t.astype(jnp.float32).reshape(B, S, H, N)

    rh, wh, kh, vh, ah = heads(r), heads(decay), heads(k), heads(v), heads(a)
    y = _wkv7_scan(rh, wh, kh, vh, -kk, kk * ah)
    mean = jnp.mean(y, axis=-1, keepdims=True)
    var = jnp.mean(jnp.square(y - mean), axis=-1, keepdims=True)
    y = ((y - mean) * lax.rsqrt(var + GN_EPS)).reshape(B, S, MIX_WIDTH)
    y = y * lnx_w.astype(jnp.float32) + lnx_b.astype(jnp.float32)
    bonus = jnp.sum(rh * kh * r_k.astype(jnp.float32), axis=-1, keepdims=True) * vh
    out = (y + bonus.reshape(B, S, MIX_WIDTH)) * g.astype(jnp.float32)
    return out.astype(h.dtype), q_mem

def _mem_attention(q_mem, mem_n, w_kv):
    B, S, _ = q_mem.shape
    M = mem_n.shape[1]
    k, v = jnp.split(mem_n @ w_kv, 2, axis=-1)
    q = q_mem.reshape(B, S, MEM_HEADS, HEAD_DIM)
    k = k.reshape(B, M, MEM_HEADS, HEAD_DIM)
    v = v.reshape(B, M, MEM_HEADS, HEAD_DIM)
    s = jnp.einsum('bshd,bmhd->bhsm', q, k).astype(jnp.float32) * (HEAD_DIM ** -0.5)
    p = jax.nn.softmax(s, axis=-1).astype(v.dtype)
    return jnp.einsum('bhsm,bmhd->bshd', p, v).reshape(B, S, MEM_WIDTH)

def _swiglu(h, w_in, w_out):
    gate, up = jnp.split(h @ w_in, 2, axis=-1)
    return (jax.nn.silu(gate) * up) @ w_out

def first_inputs(seed: int = 0) -> dict:
    key = jax.random.key(seed)
    ks = jax.random.split(key, 32)
    f32 = jnp.float32

    def nrm(k, shape, scale):
        return jax.random.normal(k, shape, f32) * scale

    D = D_MODEL
    return {
        'x': nrm(ks[0], (BATCH, SEQ, D), 1.0),
        'mem': nrm(ks[1], (BATCH, N_MEM, D), 1.0),
        'norm1': 1.0 + nrm(ks[2], (DEPTH, D), 0.05),
        'norm_mem': 1.0 + nrm(ks[3], (DEPTH, D), 0.05),
        'w_mem_kv': nrm(ks[4], (DEPTH, D, 2 * MEM_WIDTH), D ** -0.5),
        'w_o': nrm(ks[5], (DEPTH, MIX_WIDTH + MEM_WIDTH, D), (MIX_WIDTH + MEM_WIDTH) ** -0.5),
        'norm2': 1.0 + nrm(ks[6], (DEPTH, D), 0.05),
        'w_ffn_in': nrm(ks[7], (DEPTH, D, 2 * FFN_HIDDEN), D ** -0.5),
        'w_ffn_out': nrm(ks[8], (DEPTH, FFN_HIDDEN, D), FFN_HIDDEN ** -0.5),
        'nsa_w_in': nrm(ks[9], (N_NSA, D, NSA_IN), D ** -0.5),
        'nsa_gate_b': nrm(ks[10], (N_NSA, 3 * MIX_HEADS), 0.1),
        'nsa_cmp_pos': nrm(ks[11], (N_NSA, 2, CMP_BLOCK, HEAD_DIM), 0.1),
        'nsa_cmp_w1': nrm(ks[12], (N_NSA, 2, CMP_BLOCK, HEAD_DIM, CMP_HIDDEN), (CMP_BLOCK * HEAD_DIM) ** -0.5),
        'nsa_cmp_w2': nrm(ks[13], (N_NSA, 2, CMP_HIDDEN, HEAD_DIM), CMP_HIDDEN ** -0.5),
        'rw_w_in': nrm(ks[14], (N_RWKV, D, RW_IN), D ** -0.5),
        'rw_mu': jax.random.uniform(ks[15], (N_RWKV, RW_SHIFT), f32),
        'rw_w0': jax.random.uniform(ks[16], (N_RWKV, MIX_WIDTH), f32, -5.0, 1.0),
        'rw_w2': nrm(ks[17], (N_RWKV, DECAY_LORA, MIX_WIDTH), 0.1 * DECAY_LORA ** -0.5),
        'rw_a0': nrm(ks[18], (N_RWKV, MIX_WIDTH), 0.5),
        'rw_a2': nrm(ks[19], (N_RWKV, ICLR_LORA, MIX_WIDTH), 0.3 * ICLR_LORA ** -0.5),
        'rw_g2': nrm(ks[20], (N_RWKV, GATE_LORA, MIX_WIDTH), GATE_LORA ** -0.5),
        'rw_k_k': 0.85 + nrm(ks[21], (N_RWKV, MIX_WIDTH), 0.05),
        'rw_k_a': 1.0 + nrm(ks[22], (N_RWKV, MIX_WIDTH), 0.05),
        'rw_r_k': nrm(ks[23], (N_RWKV, MIX_HEADS, HEAD_DIM), 0.1),
        'rw_lnx_w': 1.0 + nrm(ks[24], (N_RWKV, MIX_WIDTH), 0.05),
        'rw_lnx_b': nrm(ks[25], (N_RWKV, MIX_WIDTH), 0.02),
        'final_norm': 1.0 + nrm(ks[26], (D,), 0.05),
    }

def first_block(x, mem, norm1, norm_mem, w_mem_kv, w_o, norm2, w_ffn_in, w_ffn_out,
              nsa_w_in, nsa_gate_b, nsa_cmp_pos, nsa_cmp_w1, nsa_cmp_w2,
              rw_w_in, rw_mu, rw_w0, rw_w2, rw_a0, rw_a2, rw_g2, rw_k_k, rw_k_a, rw_r_k,
              rw_lnx_w, rw_lnx_b, final_norm):
    for i in range(DEPTH):
        j = i // 2
        hn = _rmsnorm(x, norm1[i])
        mn = _rmsnorm(mem, norm_mem[i])
        if i % 2 == 0:
            mix, q_mem = _nsa_mixer(hn, nsa_w_in[j], nsa_gate_b[j], nsa_cmp_pos[j],
                                    nsa_cmp_w1[j], nsa_cmp_w2[j])
        else:
            mix, q_mem = _rwkv7_mixer(hn, rw_w_in[j], rw_mu[j], rw_w0[j], rw_w2[j], rw_a0[j],
                                      rw_a2[j], rw_g2[j], rw_k_k[j], rw_k_a[j], rw_r_k[j],
                                      rw_lnx_w[j], rw_lnx_b[j])
        cross = _mem_attention(q_mem, mn, w_mem_kv[i])
        x = x + jnp.concatenate([mix, cross], axis=-1) @ w_o[i]
        x = x + _swiglu(_rmsnorm(x, norm2[i]), w_ffn_in[i], w_ffn_out[i])
    return _rmsnorm(x, final_norm)


DEPTH_2 = 1

MEM_LEN = 256
D_MIX = D_MODEL
SSD_DIM = D_MIX // 2
SSD_HEAD_DIM = 64
SSD_HEADS = SSD_DIM // SSD_HEAD_DIM
SSD_GROUPS = 2
SSD_STATE = 64
CONV_K = 4
CHUNK = 128
SB_DIM = D_MIX - SSD_DIM
SB_HEAD_DIM = 64
SB_HEADS = SB_DIM // SB_HEAD_DIM
Q_BLOCK = 128
XA_HEADS = 4
XA_HEAD_DIM = 128
XA_DIM = XA_HEADS * XA_HEAD_DIM
D_FF = 4 * D_MODEL
EPS = 1e-5
GN = SSD_GROUPS * SSD_STATE
CONV_DIM = SSD_DIM + 2 * GN
IN_DIM = SSD_DIM + CONV_DIM + SSD_HEADS + 3 * SB_DIM


def rmsnorm(x, g):
    xf = x.astype(jnp.float32)
    y = xf * lax.rsqrt(jnp.mean(xf * xf, axis=-1, keepdims=True) + EPS)
    return (y * g.astype(jnp.float32)).astype(x.dtype)

def causal_dwconv(x, w, b):
    y = lax.conv_general_dilated(
        x, w.astype(x.dtype)[:, None, :], window_strides=(1,), padding=[(CONV_K - 1, 0)],
        dimension_numbers=("NWC", "WIO", "NWC"), feature_group_count=x.shape[-1])
    return y + b.astype(x.dtype)

def ssd_chunked(xh, dt, a, bm, cm):
    b, s, h, p = xh.shape
    g, n = bm.shape[-2:]
    e = h // g
    nc = s // CHUNK
    x_c = (xh * dt[..., None]).reshape(b, nc, CHUNK, g, e, p)
    a_c = (dt * a).reshape(b, nc, CHUNK, g, e)
    b_c = bm.reshape(b, nc, CHUNK, g, n)
    c_c = cm.reshape(b, nc, CHUNK, g, n)
    a_cum = jnp.cumsum(a_c, axis=2)
    seg = a_cum[:, :, :, None] - a_cum[:, :, None, :]
    causal = jnp.tril(jnp.ones((CHUNK, CHUNK), dtype=bool))[:, :, None, None]
    decay = jnp.exp(jnp.where(causal, seg, -jnp.inf))
    cb = jnp.einsum("bclgn,bcsgn->bclsg", c_c, b_c)
    y_diag = jnp.einsum("bclsg,bclsge,bcsgep->bclgep", cb, decay, x_c)
    decay_states = jnp.exp(a_cum[:, :, -1:] - a_cum)
    states = jnp.einsum("bclgn,bclge,bclgep->bcgepn", b_c, decay_states, x_c)
    chunk_decay = jnp.exp(a_cum[:, :, -1])

    def step(prev, inp):
        st, dec = inp
        return prev * dec[..., None, None] + st, prev

    init = jnp.zeros((b, g, e, p, n), jnp.float32)
    _, prev_states = lax.scan(step, init, (jnp.swapaxes(states, 0, 1), jnp.swapaxes(chunk_decay, 0, 1)))
    prev_states = jnp.swapaxes(prev_states, 0, 1)
    y_off = jnp.einsum("bclgn,bcgepn,bclge->bclgep", c_c, prev_states, jnp.exp(a_cum))
    return (y_diag + y_off).reshape(b, s, h, p)

def stick_breaking_attention(q, k, v):
    s_len, dh = q.shape[2], q.shape[3]
    scale = 1.0 / math.sqrt(dh)
    outs = []
    for i in range(s_len // Q_BLOCK):
        start = i * Q_BLOCK
        end = start + Q_BLOCK
        qb = q[:, :, start:end].astype(jnp.float32)
        kb = k[:, :, :end].astype(jnp.float32)
        vb = v[:, :, :end].astype(jnp.float32)
        logits = jnp.einsum("bhqd,bhkd->bhqk", qb, kb) * scale
        t_pos = start + jnp.arange(Q_BLOCK)[:, None]
        s_pos = jnp.arange(end)[None, :]
        mask = s_pos < t_pos
        log_stay = jnp.where(mask, jax.nn.log_sigmoid(-logits), 0.0)
        log_beta = jax.nn.log_sigmoid(logits)
        later = lax.cumsum(log_stay, axis=3, reverse=True) - log_stay
        w = jnp.where(mask, jnp.exp(log_beta + later), 0.0)
        outs.append(jnp.einsum("bhqk,bhkd->bhqd", w, vb))
    return jnp.concatenate(outs, axis=2)

def hybrid_mixer(hn, w_in, conv_w, conv_b, dt_bias, a_log, d_skip, ssd_norm_g, sb_norm_g, w_out):
    b, s, _ = hn.shape
    proj = hn @ w_in.astype(hn.dtype)
    z, xbc, dt_raw, qkv = jnp.split(
        proj, [SSD_DIM, SSD_DIM + CONV_DIM, SSD_DIM + CONV_DIM + SSD_HEADS], axis=-1)
    xbc = jax.nn.silu(causal_dwconv(xbc, conv_w, conv_b))
    xs, bm, cm = jnp.split(xbc, [SSD_DIM, SSD_DIM + GN], axis=-1)
    dt = jax.nn.softplus(dt_raw.astype(jnp.float32) + dt_bias.astype(jnp.float32))
    a = -jnp.exp(a_log.astype(jnp.float32))
    xh = xs.astype(jnp.float32).reshape(b, s, SSD_HEADS, SSD_HEAD_DIM)
    y = ssd_chunked(xh, dt, a,
                    bm.astype(jnp.float32).reshape(b, s, SSD_GROUPS, SSD_STATE),
                    cm.astype(jnp.float32).reshape(b, s, SSD_GROUPS, SSD_STATE))
    y = y + d_skip.astype(jnp.float32)[:, None] * xh
    y = y.reshape(b, s, SSD_DIM) * jax.nn.silu(z.astype(jnp.float32))
    y_ssd = rmsnorm(y, ssd_norm_g)
    q, k, v = jnp.split(qkv, 3, axis=-1)
    to_heads = lambda t: t.reshape(b, s, SB_HEADS, SB_HEAD_DIM).transpose(0, 2, 1, 3)
    o = stick_breaking_attention(to_heads(q), to_heads(k), to_heads(v))
    y_sb = rmsnorm(o.transpose(0, 2, 1, 3).reshape(b, s, SB_DIM), sb_norm_g)
    y_all = jnp.concatenate([y_ssd, y_sb], axis=-1).astype(hn.dtype)
    return y_all @ w_out.astype(hn.dtype)

def memory_cross_attention(hn, mem, g_mem, w_q, w_k, w_v, w_o):
    b, s, _ = hn.shape
    m = rmsnorm(mem, g_mem)
    q = (hn @ w_q.astype(hn.dtype)).reshape(b, s, XA_HEADS, XA_HEAD_DIM).astype(jnp.float32)
    k = (m @ w_k.astype(m.dtype)).reshape(b, -1, XA_HEADS, XA_HEAD_DIM).astype(jnp.float32)
    v = (m @ w_v.astype(m.dtype)).reshape(b, -1, XA_HEADS, XA_HEAD_DIM).astype(jnp.float32)
    logits = jnp.einsum("bshd,bmhd->bhsm", q, k) * (1.0 / math.sqrt(XA_HEAD_DIM))
    p = jax.nn.softmax(logits, axis=-1)
    o = jnp.einsum("bhsm,bmhd->bshd", p, v).reshape(b, s, XA_DIM).astype(hn.dtype)
    return o @ w_o.astype(hn.dtype)

def sqrelu_mlp(hn, w1, w2):
    u = hn @ w1.astype(hn.dtype)
    u = jnp.square(jax.nn.relu(u))
    return u @ w2.astype(hn.dtype)

def second_inputs(seed: int = 0) -> dict:
    key = jax.random.key(seed)
    ks = jax.random.split(key, 24)
    f32 = jnp.float32
    nrm = lambda k, shape, fan_in: jax.random.normal(k, shape, f32) * (fan_in ** -0.5)
    gain = lambda k, shape: 1.0 + 0.02 * jax.random.normal(k, shape, f32)
    u = jax.random.uniform(ks[5], (DEPTH_2, SSD_HEADS), f32)
    dt0 = jnp.exp(u * (math.log(0.1) - math.log(0.001)) + math.log(0.001))
    dt_bias = dt0 + jnp.log(-jnp.expm1(-dt0))
    a_log = jnp.log(jax.random.uniform(ks[6], (DEPTH_2, SSD_HEADS), f32, minval=1.0, maxval=16.0))
    return {
        "x": jax.random.normal(ks[0], (BATCH, SEQ, D_MODEL), f32),
        "mem": jax.random.normal(ks[1], (BATCH, MEM_LEN, D_MODEL), f32),
        "norm_mix_g": gain(ks[2], (DEPTH_2, D_MODEL)),
        "w_in": nrm(ks[3], (DEPTH_2, D_MODEL, IN_DIM), D_MODEL),
        "conv_w": 0.5 * jax.random.normal(ks[4], (DEPTH_2, CONV_K, CONV_DIM), f32),
        "conv_b": 0.02 * jax.random.normal(ks[7], (DEPTH_2, CONV_DIM), f32),
        "dt_bias": dt_bias,
        "a_log": a_log,
        "d_skip": 1.0 + 0.1 * jax.random.normal(ks[8], (DEPTH_2, SSD_HEADS), f32),
        "ssd_norm_g": gain(ks[9], (DEPTH_2, SSD_DIM)),
        "sb_norm_g": gain(ks[10], (DEPTH_2, SB_DIM)),
        "w_out": nrm(ks[11], (DEPTH_2, D_MIX, D_MODEL), D_MIX),
        "norm_xa_g": gain(ks[12], (DEPTH_2, D_MODEL)),
        "norm_mem_g": gain(ks[13], (DEPTH_2, D_MODEL)),
        "w_xq": nrm(ks[14], (DEPTH_2, D_MODEL, XA_DIM), D_MODEL),
        "w_xk": nrm(ks[15], (DEPTH_2, D_MODEL, XA_DIM), D_MODEL),
        "w_xv": nrm(ks[16], (DEPTH_2, D_MODEL, XA_DIM), D_MODEL),
        "w_xo": nrm(ks[17], (DEPTH_2, XA_DIM, D_MODEL), XA_DIM),
        "norm_ff_g": gain(ks[18], (DEPTH_2, D_MODEL)),
        "w_ff1": nrm(ks[19], (DEPTH_2, D_MODEL, D_FF), D_MODEL),
        "w_ff2": nrm(ks[20], (DEPTH_2, D_FF, D_MODEL), D_FF),
        "final_g": gain(ks[21], (D_MODEL,)),
    }

def second_block(x, mem, norm_mix_g, w_in, conv_w, conv_b, dt_bias, a_log, d_skip, ssd_norm_g,
              sb_norm_g, w_out, norm_xa_g, norm_mem_g, w_xq, w_xk, w_xv, w_xo,
              norm_ff_g, w_ff1, w_ff2, final_g):
    h = x
    for l in range(DEPTH_2):
        h = h + hybrid_mixer(rmsnorm(h, norm_mix_g[l]), w_in[l], conv_w[l], conv_b[l], dt_bias[l],
                             a_log[l], d_skip[l], ssd_norm_g[l], sb_norm_g[l], w_out[l])
        h = h + memory_cross_attention(rmsnorm(h, norm_xa_g[l]), mem, norm_mem_g[l],
                                       w_xq[l], w_xk[l], w_xv[l], w_xo[l])
        h = h + sqrelu_mlp(rmsnorm(h, norm_ff_g[l]), w_ff1[l], w_ff2[l])
    return rmsnorm(h, final_g)


def setup_inputs(seed=0):
    out = dict(first_inputs(seed))
    for name, value in second_inputs(seed + 1).items():
        if name != "x":
            out[name + "_2"] = value
    return out


def reference(
    x, mem, norm1, norm_mem, w_mem_kv, w_o, norm2, w_ffn_in, w_ffn_out, nsa_w_in, nsa_gate_b,
    nsa_cmp_pos, nsa_cmp_w1, nsa_cmp_w2, rw_w_in, rw_mu, rw_w0, rw_w2, rw_a0, rw_a2, rw_g2,
    rw_k_k, rw_k_a, rw_r_k, rw_lnx_w, rw_lnx_b, final_norm, mem_2, norm_mix_g_2, w_in_2,
    conv_w_2, conv_b_2, dt_bias_2, a_log_2, d_skip_2, ssd_norm_g_2, sb_norm_g_2, w_out_2,
    norm_xa_g_2, norm_mem_g_2, w_xq_2, w_xk_2, w_xv_2, w_xo_2, norm_ff_g_2, w_ff1_2, w_ff2_2,
    final_g_2,
):
    x = first_block(
        x, mem, norm1, norm_mem, w_mem_kv, w_o, norm2, w_ffn_in, w_ffn_out, nsa_w_in,
        nsa_gate_b, nsa_cmp_pos, nsa_cmp_w1, nsa_cmp_w2, rw_w_in, rw_mu, rw_w0, rw_w2, rw_a0,
        rw_a2, rw_g2, rw_k_k, rw_k_a, rw_r_k, rw_lnx_w, rw_lnx_b, final_norm,
    )
    return second_block(
        x, mem_2, norm_mix_g_2, w_in_2, conv_w_2, conv_b_2, dt_bias_2, a_log_2, d_skip_2,
        ssd_norm_g_2, sb_norm_g_2, w_out_2, norm_xa_g_2, norm_mem_g_2, w_xq_2, w_xk_2, w_xv_2,
        w_xo_2, norm_ff_g_2, w_ff1_2, w_ff2_2, final_g_2,
    )


_drawn_inputs = setup_inputs


def setup_inputs(seed=0):
    import zlib

    import numpy as np

    out = dict(_drawn_inputs(seed))
    spreads = {}
    factors = {'norm_mem': 7.57,
     'rw_w2': 8.0,
     'rw_k_k': 2.924,
     'rw_lnx_b': 5.107,
     'norm_mix_g_2': 2.809,
     'conv_b_2': 4.397,
     'ssd_norm_g_2': 6.049,
     'sb_norm_g_2': 5.12,
     'norm_xa_g_2': 8.0,
     'norm_mem_g_2': 8.0,
     'norm_ff_g_2': 10.319,
     'final_g_2': 8.081}
    for name, (base, spread) in spreads.items():
        noise = np.random.default_rng([zlib.crc32(name.encode()), seed]).standard_normal(out[name].shape)
        drawn = base * np.exp(spread * noise) if base else spread * noise
        out[name] = __import__('jax').numpy.asarray(drawn.astype(out[name].dtype))
    for name, factor in factors.items():
        out[name] = (out[name] * factor).astype(out[name].dtype)
    return out
```

```python
import math
from contextlib import ExitStack

import numpy as np
import concourse.bass as bass
from concourse import mybir

F32 = mybir.dt.float32
ALU = mybir.AluOpType
ACT = mybir.ActivationFunctionType
AX = mybir.AxisListType

P = 128
D = 1024
KC = D // P
S = 512
TT = S // P
M = 256
HD = 64
NEG = -1.0e30

H1 = 12
G1 = 4
R1 = H1 // G1
MIX = H1 * HD
KV = G1 * HD
CB, CS = 32, 16
NCMP = (S - CB) // CS + 1
FH = 2816
FT = FH // P
SLOT = 3 * MIX + 64 + 64 + 160
DECAY = math.exp(-0.5)
CH = 64
NCH = S // CH
JP = H1 // 2
SD = 512
SH = 8
SG = 2
XH = 4
FF = 4096
FFT = FF // P
EPS1, EPS2, EPS_GN = 1e-6, 1e-5, 64e-5

NSLOT = 4
NBANK = 4


def alibi_slopes(n):
    def pow2(m):
        start = 2.0 ** (-8.0 / m)
        return [start ** (i + 1) for i in range(m)]
    c = 2 ** int(math.floor(math.log2(n)))
    s = pow2(c)
    if c < n:
        s = s + pow2(2 * c)[0::2][: n - c]
    return [float(np.float32(v)) for v in s]


class Steps:

    def __init__(self, sem, *names):
        self.sem, self.names = sem, names

    def at(self, name, rnd):
        return rnd * len(self.names) + self.names.index(name) + 1


class Tile:

    def __init__(self, n, eng, order):
        self.n, self.bank, self.eng, self.order = n, n % NBANK, eng, order


def block_stack(nc, a, out, upto=None):
    ctx = ExitStack()
    with ctx:
        def sb(name, shape):
            return ctx.enter_context(nc.sbuf_tensor(name, shape, F32))

        def sem(name):
            return ctx.enter_context(nc.semaphore(name))

        xT = sb("xT", [P, KC, S])
        hT = sb("hT", [P, KC, S])
        wring = sb("wring", [P, NSLOT, 4096])
        arena = sb("arena", [P, 48 * S])
        ident = sb("ident", [P, P])
        ones = sb("ones", [P, P])
        nones = sb("nones", [P, P])
        blockones = sb("blockones", [P, P])
        eye2 = sb("eye2", [P, HD])
        dist = sb("dist", [P, S])
        distc = sb("distc", [P, TT, NCMP])
        keep = dist
        triu = sb("triu", [P, P])
        masks = sb("masks", [P, 4 * P])
        causal = masks[:, 0:P]
        level = masks[:, P:4 * P].rearrange("p (l n) -> p l n", l=6)
        triu_s, ntril = masks[:, 0:P], masks[:, P:2 * P]
        hide_gt, hide_ge = masks[:, 2 * P:3 * P], masks[:, 3 * P:4 * P]
        qscale = sb("qscale", [P, 6])
        cols = sb("cols", [P, 320])
        ncols = sb("ncols", [P, 16])
        omu = sb("omu", [P, 21])
        eps = sb("eps", [P, 5])
        bcast = sb("bcast", [P, 60])
        dskip = sb("dskip", [P, 4])
        cmp_w2 = sb("cmp_w2", [P, 2, HD])
        stat = sb("stat", [P, 2, 4])
        rsb = sb("rsb", [P, S])
        gates = sb("gates", [P, TT, 36])
        small = sb("small", [P, 6, 32])
        bank = [ctx.enter_context(nc.psum_tensor(f"bank{i}", [P, S], F32)) for i in range(8)]

        def blk(first, n=1, width=S):
            v = arena[:, first * S:first * S + n * width]
            return v.rearrange("p (n w) -> p n w", n=n)

        rows = blk(30)[:, 0, 0:3 * P].rearrange("p (j n) -> p j n", j=3)

        landed = [sem(f"landed{i}") for i in range(NSLOT)]
        panel_read = sem("panel_read")
        acc_full = sem("acc_full")
        evac_v = sem("evac_v")
        evac_a = sem("evac_a")
        consts = sem("consts")
        vec_in = sem("vec_in")
        cols_ready = sem("cols_ready")
        squared = sem("squared")
        rooted = sem("rooted")
        normed = sem("normed")
        chain_v = sem("chain_v")
        chain_a = sem("chain_a")
        chain_p = sem("chain_p")
        gates_ready = sem("gates_ready")
        gate_exp_in = sem("gate_exp_in")
        gate_exp = sem("gate_exp")
        gelu_in = sem("gelu_in")
        gelu_exp = sem("gelu_exp")
        gelu_out = sem("gelu_out")
        cmp_ready = sem("cmp_ready")
        att_scores = sem("att_scores")
        att_max = sem("att_max")
        att_exp = sem("att_exp")
        att_weight = sem("att_weight")
        att_turned = sem("att_turned")
        att_copied = sem("att_copied")
        att_pv = sem("att_pv")
        att_out = sem("att_out")
        shifted = sem("shifted")
        lora_pre = sem("lora_pre")
        lora_mid = sem("lora_mid")
        lora_in = sem("lora_in")
        rp_a = sem("rp_a")
        rp_v = sem("rp_v")
        rp_p = sem("rp_p")
        rc_t = sem("rc_t")
        rc_v = sem("rc_v")
        rc_a = sem("rc_a")
        rc_p = sem("rc_p")
        gn_v = sem("gn_v")
        gn_a = sem("gn_a")
        sd_v = sem("sd_v")
        sd_a = sem("sd_a")
        sc_t = sem("sc_t")
        sc_v = sem("sc_v")
        sc_a = sem("sc_a")
        conv_a = sem("conv_a")
        conv_v = sem("conv_v")
        sb_t = sem("sb_t")
        sb_v = sem("sb_v")
        sb_a = sem("sb_a")
        sb_pv = sem("sb_pv")
        sb_out = sem("sb_out")
        out_sent = sem("out_sent")

        tiles, order = [], {"v": 0, "a": 0}

        def tile(eng):
            t = Tile(len(tiles), eng, order[eng])
            order[eng] += 1
            tiles.append(t)
            return t

        panels = []

        def panel(*parts):
            p = {"slot": len(panels) % NSLOT, "n": len(panels), "until": None}
            before = panels[-NSLOT]["level"] if len(panels) >= NSLOT else 0
            p["parts"] = [(f(wring[:, p["slot"], :]), src) for f, src in parts]
            p["level"] = before + 16 * len(parts)
            panels.append(p)
            return p

        def columns(w, c0, n, k=KC):
            p = panel((lambda s: s[:, 0:k * n].rearrange("p (k n) -> p k n", k=k),
                       w[0:k * P, c0:c0 + n].rearrange("(k p) n -> p k n", p=P)))
            p["v"] = wring[:, p["slot"], 0:k * n].rearrange("p (k n) -> p k n", k=k)
            return p

        def until_tile(p, t):
            p["until"] = (acc_full, t.n + 1)

        vec = {}
        vec_dmas = []
        nrow = [0]

        def vrow(name, src, n):
            vec[name] = nrow[0]
            r = 0
            while r < n:
                j, o = divmod(nrow[0] + r, P)
                m = min(n - r, P - o)
                vec_dmas.append((rows[o:o + m, j, :], src[r:r + m, :]))
                r += m
            nrow[0] += n

        for nm in ("norm1", "norm_mem", "norm2"):
            vrow(nm, a[nm].rearrange("l (k p) -> (l k) p", p=P), 2 * KC)
        for nm in ("final_norm", "final_g_2"):
            vrow(nm, a[nm].rearrange("(k p) -> k p", p=P), KC)
        for nm in ("norm_mix_g_2", "norm_xa_g_2", "norm_mem_g_2", "norm_ff_g_2"):
            vrow(nm, a[nm].rearrange("l (k p) -> (l k) p", p=P), KC)
        for nm in ("ssd_norm_g_2", "sb_norm_g_2"):
            vrow(nm, a[nm].rearrange("l (k p) -> (l k) p", p=P), 4)
        vrow("rw_mu", a["rw_mu"][:, 0:20 * P].rearrange("l (k p) -> (l k) p", p=P), 20)
        for nm in ("rw_w0", "rw_a0", "rw_k_k", "rw_k_a", "rw_lnx_w", "rw_lnx_b"):
            vrow(nm, a[nm].rearrange("l (k p) -> (l k) p", p=P), 6)
        vrow("rw_r_k", a["rw_r_k"].rearrange("l (c two) d -> (l c) (two d)", two=2), 6)
        vrow("conv_w_2", a["conv_w_2"].rearrange("l k (c p) -> (l k c) p", p=P), 24)
        vrow("conv_b_2", a["conv_b_2"].rearrange("l (c p) -> (l c) p", p=P), 6)
        NVEC = nrow[0]
        MU20 = NVEC
        j20, o20 = divmod(MU20, P)
        vec_dmas.append((rows[o20:o20 + 1, j20, 0:32], a["rw_mu"][:, 20 * P:SLOT]))
        NROW1 = NVEC + 1 - P
        POS = 256
        vec_dmas.append((rows[0:64, 2, 0:HD], a["nsa_cmp_pos"].rearrange("z j l d -> (z j l) d")))
        vec_dmas.append((bcast[:, 0:36], a["nsa_gate_b"].rearrange("a n -> (a n)").partition_broadcast(P)))
        vec_dmas.append((bcast[:, 36:44], a["dt_bias_2"].rearrange("a n -> (a n)").partition_broadcast(P)))
        vec_dmas.append((bcast[:, 44:52], a["a_log_2"].rearrange("a n -> (a n)").partition_broadcast(P)))
        vec_dmas.append((bcast[:, 52:60], a["d_skip_2"].rearrange("a n -> (a n)").partition_broadcast(P)))
        vec_dmas.append((cmp_w2[:, :, :], a["nsa_cmp_w2"].rearrange("z j e d -> e (z j) d")))

        def col(name, j, p0=0, p1=P):
            return cols[p0:p1, vec[name] + j:vec[name] + j + 1]

        MUC = lambda j: cols[:, (vec["rw_mu"] + j if j < 20 else MU20):(vec["rw_mu"] + j if j < 20 else MU20) + 1]

        vec_tile = tile("v")

        def rows_panel(src, nt):
            p = panel((lambda s: s[:, 0:nt * D].rearrange("p (t d) -> p t d", t=nt),
                       src.rearrange("z (t p) d -> p (z t) d", p=P)))
            p["v"] = wring[:, p["slot"], 0:nt * D].rearrange("p (t d) -> p t d", t=nt)
            return p

        x_panel = rows_panel(a["x"], TT)
        x_tiles = [tile("va"[k % 2]) for k in range(KC)]
        until_tile(x_panel, x_tiles[-1])
        mem_panel = rows_panel(a["mem"], 2)
        memT = blk(40, KC, M)
        mem_tiles = [tile("va"[k % 2]) for k in range(KC // 2)]
        until_tile(mem_panel, mem_tiles[-1])

        norms = []

        def norm(src, sq, dst, gain, k, n, epscol):
            nm = dict(src=src, sq=sq, dst=dst, gain=gain, k=k, n=n, eps=epscol, j=len(norms), t=tile("a"))
            norms.append(nm)
            return nm

        def feature_tile(w, c, width, h, eng, n=S, k=KC, m=P):
            t = tile(eng)
            v = bank[t.bank][0:m, 0:n]
            mm = [(v, [(w["v"][:, kk, c:c + m], h[:, kk, 0:n], w) for kk in range(k)])]
            until_tile(w, t)
            return t, mm, v

        def token_tile(w, c, width, h, tts, eng, k=KC):
            t = tile(eng)
            v = bank[t.bank][:, 0:len(tts) * width].rearrange("p (t w) -> p t w", t=len(tts))
            mm = [(v[:, i, :], [(h[:, kk, tt * P:tt * P + P], w["v"][:, kk, c:c + width], w) for kk in range(k)])
                  for i, tt in enumerate(tts)]
            until_tile(w, t)
            return t, mm, v

        mn = blk(32, KC, M)
        kmT = [blk(44 + 2 * l, 2, M) for l in range(2)]
        vm = [blk(45 + 2 * l, 2, M) for l in range(2)]
        mem_norm, mem_jobs = [], []
        for l in range(2):
            mem_norm.append(norm(memT, mn, mn, ("norm_mem", l * KC), KC, M, 0))
            w = columns(a["w_mem_kv"][l], 0, 512)
            jobs = []
            for c in range(2):
                t, mm, v = feature_tile(w, c * P, P, mn, "va"[c], n=M)
                jobs.append((t, mm, kmT[l][:, c, :], v, 1.0))
            t, mm, v = token_tile(w, M, M, mn, range(2), "v")
            jobs.append((t, mm, vm[l][:, :, :], v, 1.0))
            mem_jobs.append(jobs)

        qT, kcT, vcT = blk(0, 6), blk(6, 2), blk(8, 2)
        ksT, kwT, qmT = blk(10, 2), blk(12, 2), blk(14, 2)
        vs, vw = blk(16, 4, KV), blk(18, 4, KV)
        n1a = norm(xT, hT, hT, ("norm1", 0), KC, S, 0)
        wn = a["nsa_w_in"][0]
        nsa_jobs = []
        slopes = alibi_slopes(H1)
        pair = lambda h: (h // 6) * 3 + h % 3
        for gp in range(2):
            w = panel(*[((lambda s, gg=gg, k=k: s[:, k * 384:k * 384 + 384].rearrange(
                              "p (r g d) -> p r g d", r=3, g=2)[:, :, gg, :]),
                         wn[k * P:k * P + P, gp * 384 + gg * 192:gp * 384 + gg * 192 + 192]
                         .rearrange("p (r d) -> p r d", r=3)) for gg in range(2) for k in range(KC)])
            w["v"] = wring[:, w["slot"], 0:KC * 384].rearrange("p (k n) -> p k n", k=KC)
            for r in range(3):
                t, mm, v = feature_tile(w, r * P, P, hT, "va"[r % 2])
                nsa_jobs.append((t, mm, qT[:, gp * 3 + r, :], v, qscale[:, gp * 3 + r:gp * 3 + r + 1]))
        w = columns(wn, MIX, 512)
        for c, dst in enumerate([kcT[:, 0, :], kcT[:, 1, :], vcT[:, 0, :], vcT[:, 1, :]]):
            t, mm, v = feature_tile(w, c * P, P, hT, "va"[c % 2])
            nsa_jobs.append((t, mm, dst, v, 1.0))
        for c0, kT_, v_ in ((MIX + 2 * KV, ksT, vs), (MIX + 4 * KV, kwT, vw)):
            w = columns(wn, c0, 512)
            for c in range(2):
                t, mm, v = feature_tile(w, c * P, P, hT, "va"[c % 2])
                nsa_jobs.append((t, mm, kT_[:, c, :], v, 1.0))
            for i in range(2):
                t, mm, v = token_tile(w, KV, KV, hT, range(2 * i, 2 * i + 2), "va"[i % 2])
                nsa_jobs.append((t, mm, v_[:, 2 * i:2 * i + 2, :], v, 1.0))
        w = columns(wn, MIX + 6 * KV, 292)
        for c in range(2):
            t, mm, v = feature_tile(w, 36 + c * P, P, hT, "va"[c % 2])
            nsa_jobs.append((t, mm, qmT[:, c, :], v, HD ** -0.5))
        gate_job = token_tile(w, 0, 36, hT, range(TT), "v")

        cmp_panels = []
        for j in range(2):
            src = a["nsa_cmp_w1"][0, j].rearrange("l d e -> d l e")
            w = panel(*[((lambda s, hf=hf: s[hf * HD:hf * HD + HD, :].rearrange("p (l e) -> p l e", l=CB)), src)
                        for hf in range(2)])
            w["v"] = wring[:, w["slot"], :].rearrange("p (l e) -> p l e", l=CB)
            cmp_panels.append(w)
        cmp_hid = [tile("v") for _ in range(2)]
        for j in range(2):
            until_tile(cmp_panels[j], cmp_hid[j])
        cmp_res = [tile("v") for _ in range(2)]
        kcb = blk(26)[:, 0, 0:2 * NCMP].rearrange("p (c n) -> p c n", c=2)
        vcb = blk(27)[0:NCMP, 0, 0:KV].rearrange("p (g d) -> p g d", g=G1)
        cbias = blk(27)[:, 0, KV:KV + 1]
        chid = blk(28)[:, 0, 0:248].rearrange("p (j n) -> p j n", j=2)
        ctmp = blk(28)[:, 0, 256:380]

        ubuf, pbuf, ptbuf = {}, {}, {}
        units = []
        att_stage = {}

        def stage_units(name, base, f):
            u0 = len(units)
            f()
            for u in units[u0:]:
                i = u["i"]
                u["U"], u["P"], u["PT"] = (blk(base + 2 * w + i % 2, 1)[:, 0, :] for w in range(3))
            att_stage[name] = (u0, len(units))

        nout = [0]

        def unit(**k):
            k["i"] = len(units)
            k["s"] = bank[4 + k["i"] % 2]
            if k.get("evac") is not None:
                nout[0] += 1
            k["nout"] = nout[0]
            units.append(k)

        def nsa_units():
            for c in range(6):
                for i in range(TT):
                    for hf in range(2):
                        h = 2 * c + hf
                        g = h // R1
                        b0 = HD * (g % 2)
                        q = qT[b0:b0 + HD, pair(h), i * P:i * P + P]
                        o = bank[7][hf * HD:hf * HD + HD, i * P:i * P + P]
                        gate = lambda br: gates[:, i, br * H1 + h:br * H1 + h + 1]
                        unit(q=q, k=kcb[b0:b0 + HD, g // 2, :], N=NCMP, D=distc[:, i, :], slope=slopes[h],
                             gate=gate(0), v=[(vcb[:, g, :], NCMP)], out=o, first=True, last=False)
                        N = (i + 1) * P
                        dd = dist[:, (TT - 1 - i) * P:S]
                        for br, kT_, v_ in ((1, ksT, vs), (2, kwT, vw)):
                            ev = None
                            if br == 2 and i == TT - 1 and hf == 1:
                                ev = (bank[7][:, :], hT[:, c, :])
                            unit(q=q, k=kT_[b0:b0 + HD, g // 2, 0:N], N=N, D=dd, slope=slopes[h], gate=gate(br),
                                 v=[(v_[:, t, g * HD:g * HD + HD], P) for t in range(i + 1)],
                                 out=o, first=False, last=(br == 2), evac=ev)

        zeros = sb("zeros", [P, M])

        def mem_units(l, qm):
            def f():
                for c in range(2):
                    for i in range(TT):
                        for hf in range(2):
                            b0 = hf * HD
                            h = 2 * c + hf
                            ev = (bank[7][:, :], hT[:, 6 + c, :]) if (i == TT - 1 and hf == 1) else None
                            unit(q=qm[b0:b0 + HD, c, i * P:i * P + P], k=kmT[l][b0:b0 + HD, c, :], N=M, D=zeros[:, :],
                                 slope=1.0, gate=None, v=[(vm[l][:, t, h * HD:h * HD + HD], P) for t in range(2)],
                                 out=bank[7][b0:b0 + HD, i * P:i * P + P], first=True, last=True, evac=ev)
            return f

        stage_units("nsa", 20, lambda: (nsa_units(), mem_units(0, qmT)()))

        def residual(w_dram, h, k, per_panel):
            jobs = []
            for c0 in range(0, D, per_panel):
                w = columns(w_dram, c0, per_panel, k)
                for c in range(per_panel // P):
                    t, mm, v = feature_tile(w, c * P, P, h, "v", k=k)
                    jobs.append((t, mm, (c0 // P) + c, v))
            return jobs

        def residual_split(w_dram, h, k):
            halves = []
            for hf in range(2):
                ts = [tile("v") for _ in range(4)]
                ps = []
                for k0 in range(0, k, 8):
                    kk = min(8, k - k0)
                    w = columns(w_dram[k0 * P:(k0 + kk) * P, :], hf * 512, 512, kk)
                    ps.append((w, k0, kk))
                halves.append((hf, ts, ps, h))
            return halves

        wo_jobs = [None, None]
        wo_jobs[0] = residual(a["w_o"][0], hT, KC, 512)
        hid = blk(0, 32)

        def swiglu(l):
            nm = norm(xT, hT, hT, ("norm2", l * KC), KC, S, 0)
            jobs = []
            wi = a["w_ffn_in"][l]
            for b in range(FT // 2):
                w = panel(*[((lambda s, o=o: s.rearrange("p (k n) -> p k n", k=KC)[:, :, o * 256:o * 256 + 256]),
                             wi[:, o * FH + b * 256:o * FH + b * 256 + 256].rearrange("(k p) n -> p k n", p=P))
                            for o in range(2)])
                w["v"] = wring[:, w["slot"], :].rearrange("p (k n) -> p k n", k=KC)
                for c in range(2):
                    jobs.append((feature_tile(w, c * P, P, hT, "a"), feature_tile(w, 256 + c * P, P, hT, "v"), 2 * b + c))
            return nm, jobs, residual_split(a["w_ffn_out"][l], hid, FT)

        ffn = [swiglu(0)]

        rT, kT7, vT7 = blk(0, 6), blk(6, 6), blk(12, 6)
        kkT, bT, bonT = blk(18, 6), blk(24, 6), blk(30, 6)
        lo, lo2, lo3, qm1 = blk(36)[:, 0, :], blk(37)[:, 0, :], blk(38)[:, 0, :], blk(39, 2)
        n1b = norm(xT, hT, hT, ("norm1", KC), KC, S, 0)
        wr = a["rw_w_in"][0]
        shift_jobs, qm1_jobs = [], []
        for b in range(5):
            w = columns(wr, b * 512, 512)
            for c in range(4):
                j = 4 * b + c
                dst = blk(j)[:, 0, :] if j < 18 else (lo if j == 18 else lo2)
                t, mm, v = feature_tile(w, c * P, P, hT, "v")
                shift_jobs.append((t, mm, dst, v, j, P))
        w = columns(wr, 2560, 288)
        t, mm, v = feature_tile(w, 0, 32, hT, "v", m=32)
        shift_jobs.append((t, mm, lo3[0:32, :], v, 20, 32))
        for c in range(2):
            t, mm, v = feature_tile(w, 32 + c * P, P, hT, "a")
            qm1_jobs.append((t, mm, qm1[:, c, :], v, HD ** -0.5))
        lora_panel = panel(
            (lambda s: s[0:64, 0:MIX], a["rw_w2"][0]),
            (lambda s: s[64:128, 0:MIX], a["rw_a2"][0]),
            (lambda s: s[:, MIX:2 * MIX], a["rw_g2"][0, 0:P, :]),
            (lambda s: s[0:32, 2 * MIX:3 * MIX], a["rw_g2"][0, P:160, :]))
        lw = wring[:, lora_panel["slot"], :]
        stage_units("mem1", 18, mem_units(1, qm1))
        rp_tiles = [dict(w=tile("a"), a=tile("a"), g=tile("a"), n=tile("v"), b=tile("v")) for _ in range(JP)]
        until_tile(lora_panel, rp_tiles[-1]["g"])
        tmp = [blk(41 + i)[:, 0, :] for i in range(4)] + [blk(45)[:, 0, :], rsb[:, :]]
        pc = sb("pc", [P, JP, NCH])
        gn_tiles = [(tile("a"), tile("a")) for _ in range(JP)]
        GA = arena[:, 36 * S:36 * S + 768].rearrange("p (j n) -> p j n", j=JP)
        GK = arena[:, 36 * S + 768:36 * S + 1536].rearrange("p (j n) -> p j n", j=JP)
        o_ = 39 * S
        tv = []
        for i in range(9):
            tv.append(arena[:, o_ + i * 384:o_ + i * 384 + 384].rearrange("p (j n) -> p j n", j=JP))
        BT, KT, VT, Tm, TTm, Ym, Xm, Um, Tn = tv
        TTn = Xm
        NALT = 3
        ALT = arena[:, o_ + 9 * 384:o_ + 9 * 384 + NALT * 384].rearrange("p (a n) -> p a n", a=NALT)
        state = sb("state", [P, JP, HD])
        wo_jobs[1] = residual(a["w_o"][1], hT, KC, 512)
        ffn.append(swiglu(1))
        n1f = norm(xT, hT, xT, ("final_norm", 0), KC, S, 0)

        mem2_panel = rows_panel(a["mem_2"], 2)
        memT2, mn2 = blk(40, KC, M), blk(36, KC, M)
        mem2_tiles = [tile("va"[k % 2]) for k in range(KC // 2)]
        until_tile(mem2_panel, mem2_tiles[-1])
        mem2_norm = norm(memT2, mn2, mn2, ("norm_mem_g_2", 0), KC, M, 1)
        kxT, vx = blk(44, 4, M), blk(46, 2)
        mem2_jobs = []
        w = columns(a["w_xk_2"][0], 0, 512)
        for c in range(4):
            t, mm, v = feature_tile(w, c * P, P, mn2, "va"[c % 2], n=M)
            mem2_jobs.append((t, mm, kxT[:, c, :], v, 1.0))
        w = columns(a["w_xv_2"][0], 0, 512)
        for i in range(2):
            t, mm, v = token_tile(w, 0, 512, mn2, [i], "va"[i % 2])
            mem2_jobs.append((t, mm, vx[:, i:i + 1, :], v, 1.0))
        n2a = norm(xT, hT, hT, ("norm_mix_g_2", 0), KC, S, 1)
        zT, xbc, q2, k2, v2 = blk(0, 4), blk(4, 6), blk(10, 4), blk(14, 4), blk(18, 4)
        wi2 = a["w_in_2"][0]
        z_jobs, conv_jobs, qkv_jobs = [], [], []
        w = columns(wi2, 0, 512)
        for c in range(4):
            t, mm, v = feature_tile(w, c * P, P, hT, "a")
            z_jobs.append((t, mm, zT[:, c, :], v))
        w = columns(wi2, 512, 512)
        for c in range(4):
            t, mm, v = feature_tile(w, c * P, P, hT, "v")
            conv_jobs.append((t, mm, xbc[:, c, :], v, c))
        w = columns(wi2, 1024, 264)
        for c in range(2):
            t, mm, v = feature_tile(w, c * P, P, hT, "v")
            conv_jobs.append((t, mm, xbc[:, 4 + c, :], v, 4 + c))
        dt_job = token_tile(w, 256, 8, hT, range(TT), "v")
        for c0, dst, sc in ((1288, q2, HD ** -0.5), (1800, k2, 1.0)):
            w = columns(wi2, c0, 512)
            for c in range(4):
                t, mm, v = feature_tile(w, c * P, P, hT, "va"[c % 2])
                qkv_jobs.append((t, mm, dst[:, c, :], v, sc))
        w = columns(wi2, 2312, 512)
        for i in range(4):
            t, mm, v = token_tile(w, 0, 512, hT, [i], "va"[i % 2])
            qkv_jobs.append((t, mm, v2[:, i:i + 1, :], v, 1.0))
        XD, Btok = blk(24, 4), blk(28)[:, 0, :]
        xd_tiles = [tile("v") for _ in range(4)]
        bt_tile = tile("a")
        ac_tile = tile("v")
        SEG = [blk(29)[:, 0, :], blk(30)[:, 0, :]]
        MM_ = [blk(31)[:, 0, :], blk(32)[:, 0, :]]
        ER = [blk(33)[:, 0, :], blk(34)[:, 0, :]]
        CT = blk(35)[:, 0, :]
        XDD = blk(22)[:, 0, :]
        SST = state[:, 0:4, :]
        yS = blk(36, 4)
        nssd = norm(yS, hT[:, 0:4, :], hT[:, 0:4, :], ("ssd_norm_g_2", 0), 4, S, 1)
        SP, WT = blk(24, 4), blk(28, 4)
        T1 = [blk(22)[:, 0, :], blk(23)[:, 0, :]]
        yB = blk(40, 4)
        nsb = norm(yB, hT[:, 4:8, :], hT[:, 4:8, :], ("sb_norm_g_2", 0), 4, S, 1)
        wout_jobs = residual(a["w_out_2"][0], hT, KC, 512)
        n2b = norm(xT, hT, hT, ("norm_xa_g_2", 0), KC, S, 1)
        qx = blk(0, 4)
        xq_jobs = []
        w = columns(a["w_xq_2"][0], 0, 512)
        for c in range(4):
            t, mm, v = feature_tile(w, c * P, P, hT, "va"[c % 2])
            xq_jobs.append((t, mm, qx[:, c, :], v, P ** -0.5))
        ox = blk(4, 4)

        def xa_units():
            for h in range(XH):
                for i in range(TT):
                    ev = (bank[7][:, :], ox[:, h, :]) if i == TT - 1 else None
                    unit(q=qx[:, h, i * P:i * P + P], k=kxT[:, h, :], N=M, D=zeros[:, :], slope=1.0, gate=None,
                         v=[(vx[:, t, h * P:h * P + P], P) for t in range(2)],
                         out=bank[7][:, i * P:i * P + P], first=True, last=True, evac=ev)

        stage_units("xa", 8, xa_units)
        wxo_jobs = residual(a["w_xo_2"][0], ox, 4, 1024)
        n2c = norm(xT, hT, hT, ("norm_ff_g_2", 0), KC, S, 1)
        ff1_jobs = []
        for b in range(8):
            w = columns(a["w_ff1_2"][0], b * 512, 512)
            for c in range(4):
                t, mm, v = feature_tile(w, c * P, P, hT, "v")
                ff1_jobs.append((t, mm, 4 * b + c, v))
        ff2_halves = residual_split(a["w_ff2_2"][0], hid, FFT)
        n2f = norm(xT, hT, hT, ("final_g_2", 0), KC, S, 1)
        out_sb = blk(0, 4, D)
        out_tiles = [tile("va"[i % 2]) for i in range(8)]

        nread = 0
        for halves in (ffn[0][2], ffn[1][2], ff2_halves):
            for hf, ts, ps, h in halves:
                for w, k0, kk in ps:
                    if w is ps[-1][0]:
                        until_tile(w, ts[-1])
                    else:
                        nread += 1
                        w["until"] = (panel_read, nread)

        def read_out(eng, ts):
            for e, s_ in (("v", evac_v), ("a", evac_a)):
                n = [t.order for t in ts if t.eng == e]
                if n:
                    eng.wait_ge(s_, max(n) + 1)

        def done(t):
            return evac_v if t.eng == "v" else evac_a

        def chained(eng, s_):
            n = [0]

            def link(ins):
                n[0] += 1
                ins.then_inc(s_, 1)
                eng.wait_ge(s_, n[0])
            return link

        RC_T = Steps(rc_t, "gram", "tok", "eye", *[x for l in range(1, 6) for x in (f"y{l}", f"t{l}")], "x", "u", "y", "s")
        RC_V = Steps(rc_v, "mask", "t0", *[f"t{l}" for l in range(1, 6)], "x", "y", "s")
        RC_A = Steps(rc_a, "tok", *[f"y{l}" for l in range(1, 6)], "u")
        SC_T = Steps(sc_t, "row", "y", "st")
        SC_V = Steps(sc_v, "seg", "xdd", "m", "ct", "y", "st")
        SC_A = Steps(sc_a, "er", "e")
        jobs_of = lambda jobs: [j[0] for j in jobs]

        block = ctx.enter_context(nc.Block())

        @block.sync
        def _(sp):
            for p in panels:
                if p["n"] >= NSLOT:
                    sp.wait_ge(*panels[p["n"] - NSLOT]["until"])
                for dst, src in p["parts"]:
                    sp.dma_start(dst, src).then_inc(landed[p["slot"]], 16)
            o = out.rearrange("z (t p) d -> p (z t) d", p=P)
            for tt in range(TT):
                read_out(sp, out_tiles[2 * tt:2 * tt + 2])
                sp.dma_start(o[:, tt, :], out_sb[:, tt, :]).then_inc(out_sent, 16)
            sp.wait_ge(out_sent, 16 * TT)

        @block.gpsimd
        def _(pool):
            link = chained(pool, chain_p)
            ms = nc.gpsimd.memset
            aff = nc.gpsimd.affine_select

            def fill(t, value, *conds):
                link(ms(t, value))
                for pat, base, cm, other in conds:
                    link(aff(out=t, in_=t, compare_op=ALU.is_ge, fill=other, base=base, pattern=pat, channel_multiplier=cm))

            link(ms(ident[:], 0.0))
            link(aff(out=ident[:], in_=ident[:], compare_op=ALU.not_equal, fill=1.0, base=0, pattern=[[-1, P]],
                     channel_multiplier=1))
            link(ms(ones[:], 1.0))
            link(ms(nones[:], -1.0))
            link(ms(rows[:], 0.0))
            for i, e in enumerate((EPS1, EPS2, EPS_GN, 1.0, 1e-24)):
                link(ms(eps[:, i:i + 1], e))
            for gp in range(2):
                for r in range(3):
                    for gg in range(2):
                        h = 3 * (2 * gp + gg) + r
                        link(ms(qscale[gg * HD:gg * HD + HD, gp * 3 + r:gp * 3 + r + 1], HD ** -0.5 / slopes[h]))
            pool.nop().then_inc(consts, 1)
            link(ms(zeros[:], 0.0))
            link(ms(blockones[:], 0.0))
            for hf in range(2):
                s_ = slice(hf * HD, hf * HD + HD)
                link(ms(blockones[s_, s_], 1.0))
                link(ms(eye2[s_, :], 0.0))
                link(aff(out=eye2[s_, :], in_=eye2[s_, :], compare_op=ALU.not_equal, fill=1.0, base=0,
                         pattern=[[-1, HD]], channel_multiplier=1))
                fill(causal[s_, 0:HD], 1.0, ([[1, HD]], -1, -1, 0.0))
                fill(causal[s_, HD:P], 1.0, ([[1, HD]], 0, -1, 0.0))
                for l in range(6):
                    m = 1 << l
                    nb = HD // (2 * m)
                    v = level[s_, l, :].rearrange("p (b o w) -> p b o w", b=nb, o=2)
                    link(ms(level[s_, l, :], 0.0))
                    link(ms(v[:, :, 1, :], 1.0))
                    for pat, base, cm in (([[-2 * m, nb], [0, m]], 0, 1), ([[2 * m, nb], [0, m]], m - 1, -1)):
                        link(aff(out=v[:, :, 1, :], in_=v[:, :, 1, :], compare_op=ALU.is_ge, fill=0.0, base=base,
                                 pattern=pat, channel_multiplier=cm))
            link(nc.gpsimd.iota(dist[:], pattern=[[1, S]], base=-(S - P), channel_multiplier=-1,
                                allow_small_or_imprecise_dtypes=True))
            link(aff(out=dist[:], in_=dist[:], compare_op=ALU.is_ge, fill=NEG, base=S - P, pattern=[[-1, S]],
                     channel_multiplier=1))
            link(nc.gpsimd.iota(distc[:], pattern=[[-P, TT], [CS, NCMP]], base=CB - 1, channel_multiplier=-1,
                                allow_small_or_imprecise_dtypes=True))
            link(aff(out=distc[:], in_=distc[:], compare_op=ALU.is_ge, fill=NEG, base=-(CB - 1),
                     pattern=[[P, TT], [-CS, NCMP]], channel_multiplier=1))
            fill(triu[:], 1.0, ([[1, P]], 0, -1, 0.0))
            link(ms(state[:], 0.0))
            pool.nop().then_inc(consts, 1)
            pool.wait_ge(att_max, att_stage["nsa"][1])
            link(ms(keep[:], 1.0))
            link(ms(keep[:, 0:S:CH], 0.0))
            pool.nop().then_inc(consts, 1)
            for c in range(NCH):
                pool.wait_ge(rc_v, RC_V.at("mask", c))
                if c:
                    pool.wait_ge(rc_t, RC_T.at("y5", c - 1))
                for l in range(6):
                    if l == NALT:
                        pool.wait_ge(rc_v, RC_V.at("t0", c))
                    if l >= NALT:
                        pool.wait_ge(rc_t, RC_T.at(("eye", "y1", "y2")[l - NALT], c))
                    nc.gpsimd.tensor_tensor(ALT[:, l % NALT, :].rearrange("p (j n) -> p j n", j=JP), GA[:, :, 0:HD],
                                            level[:, l:l + 1, :].broadcast_to([P, JP, HD]), ALU.mult).then_inc(rc_p, 1)
            pool.wait_ge(rc_p, 6 * NCH)
            fill(triu_s, 1.0, ([[1, P]], -1, -1, 0.0))
            fill(ntril, -1.0, ([[-1, P]], 0, 1, 0.0))
            fill(hide_gt, 0.0, ([[1, P]], 0, -1, NEG))
            fill(hide_ge, 0.0, ([[1, P]], -1, -1, NEG))
            pool.nop().then_inc(consts, 1)

        @block.tensor
        def _(pe):
            mm = nc.tensor.matmul
            seen = set()

            def opened(t):
                if t.n >= NBANK:
                    read_out(pe, [tiles[t.n - NBANK]])

            def arrived(w):
                if w["n"] not in seen:
                    seen.add(w["n"])
                    pe.wait_ge(landed[w["slot"]], w["level"])

            def products(t, groups):
                opened(t)
                for v, prods in groups:
                    for i, (l_, r_, w) in enumerate(prods):
                        if w is not None:
                            arrived(w)
                        last = mm(v, l_, r_, start=(i == 0), stop=(i == len(prods) - 1))
                last.then_inc(acc_full, 1)

            def turned(t, views):
                opened(t)
                for v, src in views:
                    last = nc.tensor.transpose(v, src, ident[0:src.shape[0], 0:src.shape[0]])
                last.then_inc(acc_full, 1)

            def norm_sum(nm):
                pe.wait_ge(squared, nm["j"] + 1)
                v = bank[nm["t"].bank][:, 0:nm["n"]]
                products(nm["t"], [(v, [(ones[:], nm["sq"][:, k, 0:nm["n"]], None) for k in range(nm["k"])])])

            def gemm(jobs, nm=None):
                if nm is not None:
                    pe.wait_ge(normed, nm["j"] + 1)
                for j in jobs:
                    products(j[0], j[1])

            def split_sum(halves):
                for hf, ts, ps, h in halves:
                    for t in ts:
                        opened(t)
                    for w, k0, kk in ps:
                        arrived(w)
                        for c, t in enumerate(ts):
                            for k in range(kk):
                                last = mm(bank[t.bank][:], w["v"][:, k, c * P:c * P + P], h[:, k0 + k, :],
                                          start=(k0 + k == 0), stop=(w is ps[-1][0] and k == kk - 1))
                            if w is ps[-1][0]:
                                last.then_inc(acc_full, 1)
                        if w is not ps[-1][0]:
                            last.then_inc(panel_read, 1)

            def attention(name):
                u0, u1 = att_stage[name]

                def scores(u):
                    i = u["i"]
                    if i >= 2:
                        pe.wait_ge(att_max, i - 1)
                    mm(u["s"][:, 0:u["N"]], u["q"], u["k"], start=True, stop=True).then_inc(att_scores, 1)

                def turn(u):
                    i = u["i"]
                    pe.wait_ge(att_weight, i + 1)
                    if i:
                        pe.wait_ge(att_copied, i)
                    for t, (v, kp) in enumerate(u["v"]):
                        last = nc.tensor.transpose(bank[6][0:kp, t * P:t * P + P], u["P"][:, t * P:t * P + kp], ident[:])
                    last.then_inc(att_turned, 1)

                def pv(u):
                    i = u["i"]
                    pe.wait_ge(att_copied, i + 1)
                    if i == u0 or units[i - 1].get("evac") is not None:
                        if u["nout"] - (u.get("evac") is not None) > 0:
                            pe.wait_ge(att_out, u["nout"] - (u.get("evac") is not None))
                    n = len(u["v"])
                    for t, (v, kp) in enumerate(u["v"]):
                        last = mm(u["out"], v, u["PT"][0:kp, t * P:t * P + P],
                                  start=(u["first"] and t == 0), stop=(u["last"] and t == n - 1))
                    last.then_inc(att_pv, 1)

                for i in range(u0, u1 + 2):
                    if i < u1:
                        scores(units[i])
                    if u0 <= i - 1 < u1:
                        turn(units[i - 1])
                    if u0 <= i - 2 < u1:
                        pv(units[i - 2])

            pe.wait_ge(consts, 1)
            pe.wait_ge(vec_in, 16 * len(vec_dmas))
            vb = bank[vec_tile.bank]
            turned(vec_tile, [(vb[:, 0:P], rows[:, 0, :]), (vb[:, P:2 * P], rows[:, 1, :]),
                              (vb[0:HD, POS:POS + 64], rows[0:64, 2, 0:HD])])
            arrived(x_panel)
            for k, t in enumerate(x_tiles):
                turned(t, [(bank[t.bank][:, tt * P:tt * P + P], x_panel["v"][:, tt, k * P:k * P + P]) for tt in range(TT)])
            arrived(mem_panel)
            for k, t in enumerate(mem_tiles):
                turned(t, [(bank[t.bank][:, (2 * kk + tt) * P:(2 * kk + tt) * P + P],
                            mem_panel["v"][:, tt, (2 * k + kk) * P:(2 * k + kk) * P + P]) for kk in range(2) for tt in range(2)])
            for l in range(2):
                norm_sum(mem_norm[l])
                gemm(mem_jobs[l], mem_norm[l])
            norm_sum(n1a)
            gemm(nsa_jobs, n1a)
            gemm([gate_job])
            if upto == "nsa":
                return
            read_out(pe, jobs_of(nsa_jobs))
            pe.wait_ge(cols_ready, 1)
            for j in range(2):
                w, t, src = cmp_panels[j], cmp_hid[j], (kcT, vcT)[j]
                opened(t)
                arrived(w)
                if j:
                    read_out(pe, cmp_hid[0:1])
                for b in range(2):
                    hv = (bank[t.bank], bank[6])[b][:, 0:2 * NCMP].rearrange("p (c n) -> p c n", c=2)
                    s_ = slice(b * HD, b * HD + HD)
                    for l in range(CB):
                        mm(hv, w["v"][s_, l, :], src[s_, :, l:l + CS * (NCMP - 1) + 1:CS],
                           start=(l == 0), stop=(l == CB - 1))
                for l in range(CB):
                    last = mm(bank[t.bank][:, 200:201], w["v"][0:HD, l, :], cols[0:HD, POS + j * CB + l:POS + j * CB + l + 1],
                              start=(l == 0), stop=(l == CB - 1))
                last.then_inc(acc_full, 1)
            for j in range(2):
                t = cmp_res[j]
                opened(t)
                pe.wait_ge(gelu_out, j + 1)
                hv = chid[:, j, :].rearrange("p (b c n) -> p b c n", b=2, c=2)
                if j == 0:
                    for b in range(2):
                        last = mm(bank[t.bank][b * HD:b * HD + HD, 0:2 * NCMP].rearrange("p (c n) -> p c n", c=2),
                                  cmp_w2[:, 0, :], hv[:, b], start=True, stop=True)
                else:
                    for g in range(G1):
                        last = mm(bank[t.bank][0:NCMP, g * HD:g * HD + HD], hv[:, g % 2, g // 2, :], cmp_w2[:, 1, :],
                                  start=True, stop=True)
                last.then_inc(acc_full, 1)
            read_out(pe, cmp_res)
            pe.wait_ge(consts, 2)
            attention("nsa")
            pe.wait_ge(att_out, units[att_stage["nsa"][1] - 1]["nout"])
            gemm(wo_jobs[0])

            def swiglu_pe(f):
                nm, jobs, halves = f
                norm_sum(nm)
                pe.wait_ge(normed, nm["j"] + 1)
                for g_, u_, j in jobs:
                    products(g_[0], g_[1])
                    products(u_[0], u_[1])
                read_out(pe, [jobs[-1][0][0], jobs[-1][1][0]])
                split_sum(halves)

            if upto == "wo0":
                return
            swiglu_pe(ffn[0])
            if upto == "l0":
                return
            norm_sum(n1b)
            gemm(shift_jobs, n1b)
            gemm(qm1_jobs)
            read_out(pe, jobs_of(qm1_jobs))
            attention("mem1")
            arrived(lora_panel)
            pe.wait_ge(lora_in, 2)
            for j in range(JP):
                t = rp_tiles[j]
                s_ = slice(j * P, j * P + P)
                b_ = lambda n: bank[t[n].bank][:]
                products(t["w"], [(b_("w"), [(lw[0:64, s_], lo[0:64, :], None)])])
                products(t["a"], [(b_("a"), [(lw[64:128, s_], lo[64:128, :], None)])])
                products(t["g"], [(b_("g"), [(lw[:, MIX + j * P:MIX + j * P + P], lo2, None),
                                             (lw[0:32, 2 * MIX + j * P:2 * MIX + j * P + P], lo3[0:32, :], None)])])
                pe.wait_ge(rp_a, 3 * j + 2)
                products(t["n"], [(b_("n"), [(blockones[:], tmp[3], None)])])
                pe.wait_ge(rp_v, 4 * j + 3)
                products(t["b"], [(b_("b"), [(blockones[:], tmp[4], None)])])
            if upto == "rp":
                return
            pe.wait_ge(rp_v, 4 * JP)
            halves2 = [slice(0, HD), slice(HD, P)]

            def small_mm(out_bank, lf, rf, first=True, final=True):
                for j in range(JP):
                    for hs in halves2:
                        last = mm(out_bank[hs, j * HD:j * HD + HD], lf(hs, j), rf(hs, j), start=first, stop=final)
                return last

            AR = arena[:, 0:24 * S].rearrange("p (w j t) -> p w j t", w=4, j=6)
            for c in range(NCH):
                cs = slice(c * CH, c * CH + CH)
                if c:
                    pe.wait_ge(rc_v, RC_V.at("s", c - 1))
                for w_, src in ((0, bT), (2, kT7)):
                    for j in range(JP):
                        for hs in halves2:
                            o = bank[w_ + j // 3][hs, (j % 3) * P:(j % 3) * P + P]
                            mm(o[:, 0:HD], src[hs, j, cs], AR[hs, 3, j, cs], start=True, stop=True)
                            last = mm(o[:, HD:P], src[hs, j, cs], AR[hs, 0, j, cs], start=True, stop=True)
                last.then_inc(rc_t, 1)
                for n, src in enumerate((bT, kT7, vT7)):
                    last = small_mm(bank[4 + n], lambda hs, j: src[hs, j, cs], lambda hs, j: ident[hs, hs])
                last.then_inc(rc_t, 1)
                Al = lambda l: (lambda hs, j: ALT[hs, l % NALT, j * HD:j * HD + HD])
                pe.wait_ge(rc_p, 6 * c + 1)
                small_mm(bank[7], Al(0), lambda hs, j: eye2[hs, :]).then_inc(rc_t, 1)
                cur, nxt = (Tm, TTm), (Tn, TTn)
                for l in range(1, 6):
                    pe.wait_ge(rc_p, 6 * c + l + 1)
                    pe.wait_ge(rc_v, RC_V.at(f"t{l - 1}", c))
                    small_mm(bank[0], Al(l), lambda hs, j: Tm[hs, j, :]).then_inc(rc_t, 1)
                    pe.wait_ge(rc_a, RC_A.at(f"y{l}", c))
                    if l < 5:
                        small_mm(bank[1], lambda hs, j: TTm[hs, j, :], lambda hs, j: Ym[hs, j, :])
                    small_mm(bank[2], lambda hs, j: Ym[hs, j, :], lambda hs, j: TTm[hs, j, :]).then_inc(rc_t, 1)
                pe.wait_ge(rc_a, RC_A.at("tok", c))
                for j in range(JP):
                    for hs in halves2:
                        o = bank[3][hs, j * HD:j * HD + HD]
                        mm(o, GK[hs, j, 0:HD], VT[hs, j, :], start=True, stop=False)
                        last = mm(o, kkT[hs, j, cs], state[hs, j, :], start=False, stop=True)
                last.then_inc(rc_t, 1)
                pe.wait_ge(rc_v, RC_V.at("x", c))
                small_mm(bank[4], lambda hs, j: TTm[hs, j, :], lambda hs, j: Xm[hs, j, :]).then_inc(rc_t, 1)
                pe.wait_ge(rc_a, RC_A.at("u", c))
                for j in range(JP):
                    for hs in halves2:
                        o = bank[5][hs, j * HD:j * HD + HD]
                        mm(o, state[hs, j, :], rT[hs, j, cs], start=True, stop=False)
                        mm(o, VT[hs, j, :], GK[hs, j, HD:P], start=False, stop=False)
                        last = mm(o, Um[hs, j, :], GA[hs, j, HD:P], start=False, stop=True)
                last.then_inc(rc_t, 1)
                for j in range(JP):
                    for hs in halves2:
                        o = bank[6][hs, j * HD:j * HD + HD]
                        mm(o, KT[hs, j, :], VT[hs, j, :], start=True, stop=False)
                        last = mm(o, BT[hs, j, :], Um[hs, j, :], start=False, stop=True)
                last.then_inc(rc_t, 1)
            pe.wait_ge(rc_v, RC_V.at("y", NCH - 1))
            for j in range(JP):
                t0, t1 = gn_tiles[j]
                if j == 0:
                    pe.wait_ge(rc_v, RC_V.at("s", NCH - 1))
                products(t0, [(bank[t0.bank][:], [(blockones[:], rT[:, j, :], None)])])
                pe.wait_ge(gn_a, 3 * j + 2)
                products(t1, [(bank[t1.bank][:], [(blockones[:], tmp[1], None)])])
            pe.wait_ge(gn_v, 2 * JP)
            if upto == "gn":
                return
            gemm(wo_jobs[1])
            swiglu_pe(ffn[1])
            norm_sum(n1f)
            arrived(mem2_panel)
            for k, t in enumerate(mem2_tiles):
                turned(t, [(bank[t.bank][:, (2 * kk + tt) * P:(2 * kk + tt) * P + P],
                            mem2_panel["v"][:, tt, (2 * k + kk) * P:(2 * k + kk) * P + P]) for kk in range(2) for tt in range(2)])
            norm_sum(mem2_norm)
            gemm(mem2_jobs, mem2_norm)
            norm_sum(n2a)
            if upto == "b1":
                return
            gemm(z_jobs, n2a)
            gemm(conv_jobs)
            gemm([dt_job])
            gemm(qkv_jobs)
            pe.wait_ge(conv_a, 12)
            for c, t in enumerate(xd_tiles):
                turned(t, [(bank[t.bank][:, k * P:k * P + P], xbc[:, k, c * P:c * P + P]) for k in range(4)])
            turned(bt_tile, [(bank[bt_tile.bank][:, c * P:c * P + P], xbc[:, 4, c * P:c * P + P]) for c in range(4)])
            pe.wait_ge(sd_v, 1)
            opened(ac_tile)
            mm(bank[ac_tile.bank][:, 0:32], triu[:], small[:, 1, :], start=True, stop=True)
            mm(bank[ac_tile.bank][:, 32:64], ones[:], small[:, 1, :], start=True, stop=True).then_inc(acc_full, 1)
            read_out(pe, xd_tiles + [bt_tile])
            pe.wait_ge(sd_v, 2)
            read_out(pe, [ac_tile])
            for c in range(TT):
                cs = slice(c * P, c * P + P)
                if c:
                    pe.wait_ge(sc_v, SC_V.at("st", c - 1))
                for h in range(SH):
                    mm(bank[4 + h // 4][:, (h % 4) * P:(h % 4) * P + P],
                       small[:, 1, c * 8 + h:c * 8 + h + 1].broadcast_to([P, P]), triu[:], start=True, stop=True)
                for g in range(SG):
                    gs = slice(g * HD, g * HD + HD)
                    last = mm(bank[(6, 2)[g]][:, 0:P], xbc[gs, 4, cs], xbc[gs, 5, cs], start=True, stop=True)
                last.then_inc(sc_t, 1)
                pe.wait_ge(sc_v, SC_V.at("ct", c))
                for h in range(SH):
                    g = h // 4
                    gs = slice(g * HD, g * HD + HD)
                    o = bank[(7, 1)[g]][(h % 2) * HD:(h % 2) * HD + HD, (h // 2 % 2) * P:(h // 2 % 2) * P + P]
                    last = mm(o, XD[:, c, h * HD:h * HD + HD], MM_[g][:, (h % 4) * P:(h % 4) * P + P], start=True, stop=(c == 0))
                    if c:
                        last = mm(o, SST[gs, h % 4, :], CT[gs, (h % 4) * P:(h % 4) * P + P], start=False, stop=True)
                last.then_inc(sc_t, 1)
                for g in range(SG):
                    last = mm(bank[3][g * HD:g * HD + HD, 0:256], Btok[:, c * P + g * HD:c * P + g * HD + HD],
                              XDD[:, g * 256:g * 256 + 256], start=True, stop=True)
                last.then_inc(sc_t, 1)
            pe.wait_ge(sc_v, SC_V.at("st", TT - 1))
            norm_sum(nssd)
            read_out(pe, jobs_of(qkv_jobs))
            nu = 4 * SH
            pe.wait_ge(consts, 4)

            def logits(u):
                h, js = u // 4, 3 - u % 4
                hs = slice((h % 2) * HD, (h % 2) * HD + HD)
                if u >= 2:
                    pe.wait_ge(sb_a, 3 * (u - 2) + 3)
                mm(bank[4 + u % 2][:, js * P:S], k2[hs, h // 2, js * P:js * P + P], q2[hs, h // 2, js * P:S],
                   start=True, stop=True).then_inc(sb_t, 1)

            def later(u):
                h, js = u // 4, 3 - u % 4
                b_ = bank[4 + u % 2]
                pe.wait_ge(sb_v, 2 * u + 2)
                more = dict(start=False, stop=False, skip_group_check=True)
                mm(b_[:, js * P:js * P + P], ident[:], hide_ge, **more)
                for jj in range(js + 1, 4):
                    mm(b_[:, jj * P:S], nones[:], SP[:, jj, jj * P:S], **more)
                more["stop"] = True
                mm(b_[:, js * P:S], ntril, SP[:, js, js * P:S], **more).then_inc(sb_t, 1)

            def sb_values(h):
                pe.wait_ge(sb_a, 3 * (4 * h + 3) + 3)
                if h >= 2 and h % 2 == 0:
                    pe.wait_ge(sb_out, h // 2)
                for js in range(4):
                    last = mm(bank[7][(h % 2) * HD:(h % 2) * HD + HD, js * P:S], v2[:, js, h * HD:h * HD + HD],
                              WT[:, js, js * P:S], start=(js == 0), stop=(js == 3))
                last.then_inc(sb_pv, 1)

            logits(0)
            for u in range(nu):
                if u + 1 < nu:
                    logits(u + 1)
                later(u)
                if u % 4 == 3:
                    sb_values(u // 4)
            norm_sum(nsb)
            if upto == "sb":
                return
            gemm(wout_jobs, nsb)
            norm_sum(n2b)
            gemm(xq_jobs, n2b)
            read_out(pe, jobs_of(xq_jobs))
            attention("xa")
            pe.wait_ge(att_out, units[-1]["nout"])
            gemm(wxo_jobs)
            norm_sum(n2c)
            gemm(ff1_jobs, n2c)
            read_out(pe, [ff1_jobs[-1][0]])
            split_sum(ff2_halves)
            norm_sum(n2f)
            pe.wait_ge(normed, n2f["j"] + 1)
            for i, t in enumerate(out_tiles):
                tt, kh = divmod(i, 2)
                turned(t, [(bank[t.bank][:, k * P:k * P + P], hT[:, kh * 4 + k, tt * P:tt * P + P]) for k in range(4)])

        @block.scalar
        def _(act):
            A = nc.scalar.activation
            link = chained(act, chain_a)
            act.wait_ge(consts, 1)
            for dst, src in vec_dmas:
                act.dma_start(dst, src).then_inc(vec_in, 16)

            def tile_in(t):
                act.wait_ge(acc_full, t.n + 1)

            def copy_out(t, dst, v, scale=1.0):
                tile_in(t)
                A(dst, v, ACT.Copy if isinstance(scale, float) else ACT.Identity, scale=scale).then_inc(evac_a, 1)

            def norm_root(nm):
                for k in range(nm["k"]):
                    last = A(nm["sq"][:, k, 0:nm["n"]], nm["src"][:, k, 0:nm["n"]], ACT.Square)
                last.then_inc(squared, 1)
                tile_in(nm["t"])
                v = bank[nm["t"].bank][:, 0:nm["n"]]
                r = rsb[:, 0:nm["n"]]
                if nm["j"]:
                    act.wait_ge(normed, nm["j"])
                ins = A(r, v, ACT.Ln, scale=1.0 / (nm["k"] * P), bias=eps[:, nm["eps"]:nm["eps"] + 1])
                ins.then_inc(evac_a, 1)
                act.wait_ge(evac_a, nm["t"].order + 1)
                A(r, r, ACT.Exp, scale=-0.5).then_inc(rooted, 1)

            def plain(jobs):
                for t, _, dst, v, sc in jobs:
                    if t.eng == "a":
                        copy_out(t, dst, v, sc)

            def attention(name):
                u0, u1 = att_stage[name]

                def probs(u):
                    i = u["i"]
                    if i >= 2:
                        act.wait_ge(att_turned, i - 1)
                    act.wait_ge(att_max, i + 1)
                    A(u["P"][:, 0:u["N"]], u["U"][:, 0:u["N"]], ACT.Exp, scale=u["slope"], bias=stat[:, i % 2, 1:2],
                      accum_out=stat[:, i % 2, 2:3]).then_inc(att_exp, 1)

                def copy(u):
                    i = u["i"]
                    act.wait_ge(att_turned, i + 1)
                    if i >= 2:
                        act.wait_ge(att_pv, i - 1)
                    kp = u["v"][0][1]
                    A(u["PT"][0:kp, 0:len(u["v"]) * P], bank[6][0:kp, 0:len(u["v"]) * P], ACT.Copy).then_inc(att_copied, 1)

                for i in range(u0, u1 + 1):
                    if i < u1:
                        probs(units[i])
                    if i - 1 >= u0:
                        copy(units[i - 1])

            for k, t in enumerate(x_tiles):
                if t.eng == "a":
                    copy_out(t, xT[:, k, :], bank[t.bank][:])
            for k, t in enumerate(mem_tiles):
                if t.eng == "a":
                    copy_out(t, memT[:, 2 * k:2 * k + 2, :], bank[t.bank][:].rearrange("p (k m) -> p k m", k=2))
            read_out(act, mem_tiles + x_tiles)
            for l in range(2):
                if l:
                    read_out(act, jobs_of(mem_jobs[0]))
                norm_root(mem_norm[l])
                plain(mem_jobs[l])
            norm_root(n1a)
            plain(nsa_jobs)
            act.wait_ge(gate_exp_in, 1)
            A(gates[:], gates[:], ACT.Exp, scale=-1.0).then_inc(gate_exp, 1)
            if upto == "nsa":
                return
            for j in range(2):
                act.wait_ge(gelu_in, j + 1)
                A(ctmp[:], ctmp[:], ACT.Exp, scale=-2.0 * math.sqrt(2.0 / math.pi)).then_inc(gelu_exp, 1)
            attention("nsa")

            def swiglu_act(f, jw):
                nm, jobs, halves = f
                read_out(act, jobs_of(jw))
                norm_root(nm)
                for g_, u_, j in jobs:
                    tile_in(g_[0])
                    A(hid[:, j, :], g_[2], ACT.Silu).then_inc(evac_a, 1)

            if upto == "wo0":
                return
            swiglu_act(ffn[0], wo_jobs[0])
            read_out(act, ffn[0][2][1][1])
            if upto == "l0":
                return
            norm_root(n1b)
            for t, _, dst, v, j, m in shift_jobs:
                tile_in(t)
                A(dst, v, ACT.Identity, scale=omu[0:m, j:j + 1]).then_inc(shifted, 1)
            act.wait_ge(evac_v, shift_jobs[-1][0].order + 1)
            plain(qm1_jobs)
            A(lo[0:64, :], lo[0:64, :], ACT.Tanh).then_inc(lora_in, 1)
            A(lo2, lo2, ACT.Exp, scale=-1.0)
            A(lo3[0:32, :], lo3[0:32, :], ACT.Exp, scale=-1.0).then_inc(lora_pre, 1)
            attention("mem1")
            S0 = -DECAY
            for j in range(JP):
                t = rp_tiles[j]
                tile_in(t["w"])
                if j:
                    act.wait_ge(rp_v, 4 * j)
                A(tmp[0], bank[t["w"].bank][:], ACT.Exp, scale=-1.0, bias=ncols[:, j:j + 1]).then_inc(evac_a, 1)
                tile_in(t["a"])
                A(tmp[1], bank[t["a"].bank][:], ACT.Exp, scale=-1.0, bias=ncols[:, 6 + j:7 + j]).then_inc(evac_a, 1)
                copy_out(t["g"], hT[:, j, :], bank[t["g"].bank][:])
                A(tmp[3], kT7[:, j, :], ACT.Square, scale=col("rw_k_k", j)).then_inc(rp_a, 1)
                act.wait_ge(rp_a, 3 * j + 1)
                act.nop().then_inc(rp_a, 1)
                act.wait_ge(rp_v, 4 * j + 1)
                link(A(tmp[2], tmp[2], ACT.Ln))
                A(tmp[2], tmp[2], ACT.Exp, scale=-0.5).then_inc(rp_a, 1)
                act.wait_ge(rp_v, 4 * j + 3)
                act.wait_ge(acc_full, t["b"].n + 1)
                A(tmp[4], tmp[5], ACT.Exp, scale=-S0)
                A(tmp[5], tmp[5], ACT.Exp, scale=S0)
                A(tmp[3], tmp[0], ACT.Exp, scale=S0).then_inc(rp_p, 1)
            if upto == "rp":
                return
            for c in range(NCH):
                act.wait_ge(rc_t, RC_T.at("tok", c))
                for n, dst in enumerate((BT, KT, VT)):
                    last = A(dst, bank[4 + n][:, 0:384].rearrange("p (j n) -> p j n", j=JP), ACT.Copy)
                last.then_inc(rc_a, 1)
                for l in range(1, 6):
                    act.wait_ge(rc_t, RC_T.at(f"y{l}", c))
                    A(Ym, bank[0][:, 0:384].rearrange("p (j n) -> p j n", j=JP), ACT.Copy).then_inc(rc_a, 1)
                act.wait_ge(rc_t, RC_T.at("u", c))
                A(Um, bank[4][:, 0:384].rearrange("p (j n) -> p j n", j=JP), ACT.Copy).then_inc(rc_a, 1)
            for j in range(JP):
                t0, t1 = gn_tiles[j]
                tile_in(t0)
                if j:
                    act.wait_ge(gn_v, 2 * j)
                A(tmp[0], bank[t0.bank][:], ACT.Copy, scale=-1.0 / HD).then_inc(evac_a, 1)
                act.nop().then_inc(gn_a, 1)
                act.wait_ge(gn_v, 2 * j + 1)
                A(tmp[1], rT[:, j, :], ACT.Square).then_inc(gn_a, 1)
                tile_in(t1)
                A(tmp[2], bank[t1.bank][:], ACT.Ln, scale=1.0 / HD, bias=eps[:, 2:3]).then_inc(evac_a, 1)
                act.wait_ge(evac_a, t1.order + 1)
                A(tmp[2], tmp[2], ACT.Exp, scale=-0.5).then_inc(gn_a, 1)
            if upto == "gn":
                return
            swiglu_act(ffn[1], wo_jobs[1])
            read_out(act, ffn[1][2][1][1])
            norm_root(n1f)
            for k, t in enumerate(mem2_tiles):
                if t.eng == "a":
                    copy_out(t, memT2[:, 2 * k:2 * k + 2, :], bank[t.bank][:].rearrange("p (k m) -> p k m", k=2))
            read_out(act, mem2_tiles)
            norm_root(mem2_norm)
            plain(mem2_jobs)
            act.wait_ge(normed, n1f["j"] + 1)
            norm_root(n2a)
            if upto == "b1":
                return
            for t, _, dst, v in z_jobs:
                tile_in(t)
                A(dst, v, ACT.Silu).then_inc(evac_a, 1)
            for t, _, dst, v, c in conv_jobs:
                tile_in(t)
                A(dst, v, ACT.Identity, scale=col("conv_w_2", 18 + c), bias=col("conv_b_2", c)).then_inc(conv_a, 1)
            act.wait_ge(conv_v, 6)
            for c in range(6):
                A(xbc[:, c, :], xbc[:, c, :], ACT.Silu).then_inc(conv_a, 1)
            plain(qkv_jobs)
            A(bcast[:, 44:52], bcast[:, 44:52], ACT.Exp)
            act.wait_ge(gates_ready, 2)
            link(A(small[:, 2, :], small[:, 2, :], ACT.Exp))
            A(small[:, 2, :], small[:, 2, :], ACT.Ln, bias=eps[:, 3:4]).then_inc(sd_a, 1)
            copy_out(bt_tile, Btok, bank[bt_tile.bank][:])
            act.wait_ge(sd_v, 2)
            A(small[:, 3:5, :], small[:, 3:5, :], ACT.Exp).then_inc(sd_a, 1)
            for c in range(TT):
                act.wait_ge(sc_t, SC_T.at("row", c))
                if c:
                    act.wait_ge(sc_v, SC_V.at("ct", c - 1))
                for g in range(2):
                    last = A(ER[g], bank[4 + g][:], ACT.Exp)
                last.then_inc(sc_a, 1)
                act.wait_ge(sc_v, SC_V.at("seg", c))
                for h in range(SH):
                    v = SEG[h // 4][:, (h % 4) * P:(h % 4) * P + P]
                    last = A(v, v, ACT.Exp, bias=small[:, 5, c * 8 + h:c * 8 + h + 1])
                last.then_inc(sc_a, 1)
            act.wait_ge(sd_v, 3)
            norm_root(nssd)
            for u in range(4 * SH):
                js = 3 - u % 4
                v = T1[u % 2][:, js * P:S]
                act.wait_ge(sb_v, 2 * u + 1)
                A(v, v, ACT.Exp).then_inc(sb_a, 1)
                act.wait_ge(sb_a, 3 * u + 1)
                A(v, v, ACT.Ln, bias=eps[:, 3:4]).then_inc(sb_a, 1)
                act.wait_ge(sb_t, 2 * u + 3 if u + 1 < 4 * SH else 2 * u + 2)
                if u >= 4:
                    act.wait_ge(sb_pv, u // 4)
                A(WT[:, js, js * P:S], bank[4 + u % 2][:, js * P:S], ACT.Exp).then_inc(sb_a, 1)
            act.wait_ge(sb_out, SH // 2)
            norm_root(nsb)
            read_out(act, jobs_of(wout_jobs))
            norm_root(n2b)
            plain(xq_jobs)
            attention("xa")
            read_out(act, jobs_of(wxo_jobs))
            norm_root(n2c)
            for t, _, j, v in ff1_jobs:
                tile_in(t)
                A(hid[:, j, :], v, ACT.Relu).then_inc(shifted, 1)
            read_out(act, ff2_halves[1][1])
            norm_root(n2f)
            for i, t in enumerate(out_tiles):
                if t.eng == "a":
                    tt, kh = divmod(i, 2)
                    copy_out(t, out_sb[:, tt, kh * 512:kh * 512 + 512], bank[t.bank][:])

        @block.vector
        def _(dve):
            V = nc.vector
            link = chained(dve, chain_v)

            def tile_in(t):
                dve.wait_ge(acc_full, t.n + 1)

            def copy_out(t, dst, v, scale=1.0):
                tile_in(t)
                if isinstance(scale, float) and scale == 1.0:
                    V.tensor_copy(dst, v).then_inc(evac_v, 1)
                else:
                    V.tensor_scalar(dst, v, scale, None, ALU.mult).then_inc(evac_v, 1)

            def plain(jobs):
                for t, _, dst, v, sc in jobs:
                    if t.eng == "v":
                        copy_out(t, dst, v, sc)

            def norm_apply(nm):
                dve.wait_ge(rooted, nm["j"] + 1)
                for k in range(nm["k"]):
                    last = V.scalar_tensor_tensor(nm["dst"][:, k, 0:nm["n"]], nm["src"][:, k, 0:nm["n"]],
                                                  col(nm["gain"][0], nm["gain"][1] + k), rsb[:, 0:nm["n"]], ALU.mult, ALU.mult)
                last.then_inc(normed, 1)

            def add_residual(jobs):
                for t, _, k, v in jobs:
                    tile_in(t)
                    V.tensor_tensor(xT[:, k, :], xT[:, k, :], v, ALU.add).then_inc(evac_v, 1)

            def add_split(halves):
                for hf, ts, ps, h in halves:
                    for c, t in enumerate(ts):
                        tile_in(t)
                        V.tensor_tensor(xT[:, 4 * hf + c, :], xT[:, 4 * hf + c, :], bank[t.bank][:], ALU.add).then_inc(evac_v, 1)

            def attention(name):
                u0, u1 = att_stage[name]

                def shape(u):
                    i = u["i"]
                    dve.wait_ge(att_scores, i + 1)
                    if i >= 2:
                        dve.wait_ge(att_exp, i - 1)
                    st = stat[:, i % 2, :]
                    link(V.tensor_tensor_reduce(u["U"][:, 0:u["N"]], u["s"][:, 0:u["N"]], u["D"], 1.0, -3.0e38,
                                                ALU.add, ALU.max, st[:, 0:1]))
                    V.tensor_scalar(st[:, 1:2], st[:, 0:1], -1.0e20, -u["slope"], ALU.max, ALU.mult).then_inc(att_max, 1)

                def weigh(u):
                    i = u["i"]
                    st = stat[:, i % 2, :]
                    dve.wait_ge(att_exp, i + 1)
                    link(V.tensor_scalar(st[:, 3:4], st[:, 2:3], 1.0e-30, None, ALU.max))
                    link(V.reciprocal(st[:, 3:4], st[:, 3:4]))
                    p_ = u["P"][:, 0:u["N"]]
                    if u["gate"] is None:
                        V.tensor_scalar(p_, p_, st[:, 3:4], None, ALU.mult).then_inc(att_weight, 1)
                    else:
                        V.tensor_scalar(p_, p_, st[:, 3:4], u["gate"], ALU.mult, ALU.mult).then_inc(att_weight, 1)

                def output(u):
                    if u.get("evac") is not None:
                        dve.wait_ge(att_pv, u["i"] + 1)
                        V.tensor_copy(u["evac"][1], u["evac"][0]).then_inc(att_out, 1)

                for i in range(u0, u1 + 3):
                    if i < u1:
                        shape(units[i])
                    if u0 <= i - 1 < u1:
                        weigh(units[i - 1])
                    if u0 <= i - 3 < u1:
                        output(units[i - 3])

            tile_in(vec_tile)
            vb = bank[vec_tile.bank]
            V.tensor_copy(cols[0:HD, POS:POS + 64], vb[0:HD, POS:POS + 64])
            link(V.tensor_copy(cols[:, 0:256], vb[:, 0:256]))
            for hf in range(2):
                V.tensor_copy(dskip[hf * HD:hf * HD + HD, :], bcast[hf * HD:hf * HD + HD, 52 + hf:60:2])
            V.tensor_scalar(ncols[:, 0:12], cols[:, vec["rw_w0"]:vec["rw_w0"] + 12], -1.0, None, ALU.mult)
            V.tensor_scalar(omu[:, 0:20], cols[:, vec["rw_mu"]:vec["rw_mu"] + 20], -1.0, 1.0, ALU.mult, ALU.add)
            V.tensor_scalar(omu[:, 20:21], MUC(20), -1.0, 1.0, ALU.mult, ALU.add).then_inc(cols_ready, 1)
            dve.nop().then_inc(evac_v, 1)
            for k, t in enumerate(x_tiles):
                if t.eng == "v":
                    copy_out(t, xT[:, k, :], bank[t.bank][:])
            for k, t in enumerate(mem_tiles):
                if t.eng == "v":
                    copy_out(t, memT[:, 2 * k:2 * k + 2, :], bank[t.bank][:].rearrange("p (k m) -> p k m", k=2))
            for l in range(2):
                norm_apply(mem_norm[l])
                plain(mem_jobs[l])
            norm_apply(n1a)
            plain(nsa_jobs)
            t, _, v = gate_job
            tile_in(t)
            V.tensor_tensor(gates[:], v, bcast[:, 0:36].unsqueeze(1).broadcast_to([P, TT, 36]), ALU.add).then_inc(evac_v, 1)
            dve.wait_ge(evac_v, t.order + 1)
            dve.nop().then_inc(gate_exp_in, 1)
            dve.wait_ge(gate_exp, 1)
            link(V.tensor_scalar(gates[:], gates[:], 1.0, None, ALU.add))
            link(V.reciprocal(gates[:], gates[:]))
            if upto == "nsa":
                return
            for j in range(2):
                t = cmp_hid[j]
                tile_in(t)
                h_ = chid[:, j, :]
                link(V.tensor_copy(cbias[:], bank[t.bank][:, 200:201]))
                V.tensor_scalar(h_[:, 0:62], bank[t.bank][:, 0:62], cbias[:], None, ALU.add)
                V.tensor_scalar(h_[:, 62:124], bank[6][:, 0:62], cbias[:], None, ALU.add).then_inc(evac_v, 1)
                dve.wait_ge(evac_v, t.order + 1)
                link(V.tensor_tensor(ctmp[:], h_, h_, ALU.mult))
                link(V.tensor_scalar(ctmp[:], ctmp[:], 0.044715, 1.0, ALU.mult, ALU.add))
                link(V.tensor_tensor(ctmp[:], ctmp[:], h_, ALU.mult))
                V.tensor_scalar(ctmp[:], ctmp[:], -50.0, None, ALU.max).then_inc(gelu_in, 1)
                dve.wait_ge(gelu_exp, j + 1)
                link(V.tensor_scalar(ctmp[:], ctmp[:], 1.0, None, ALU.add))
                link(V.reciprocal(ctmp[:], ctmp[:]))
                ins = V.tensor_tensor(h_, h_, ctmp[:], ALU.mult)
                ins.then_inc(gelu_out, 1)
                dve.wait_ge(gelu_out, j + 1)
            copy_out(cmp_res[0], kcb[:], bank[cmp_res[0].bank][:, 0:2 * NCMP].rearrange("p (c n) -> p c n", c=2))
            copy_out(cmp_res[1], vcb[:], bank[cmp_res[1].bank][0:NCMP, 0:KV].rearrange("p (g d) -> p g d", g=G1))
            dve.wait_ge(consts, 2)
            attention("nsa")
            add_residual(wo_jobs[0])

            def swiglu_dve(f):
                nm, jobs, halves = f
                norm_apply(nm)
                for g_, u_, j in jobs:
                    tile_in(u_[0])
                    dve.wait_ge(evac_a, g_[0].order + 1)
                    V.tensor_tensor(hid[:, j, :], hid[:, j, :], u_[2], ALU.mult).then_inc(evac_v, 1)
                add_split(halves)

            if upto == "wo0":
                return
            swiglu_dve(ffn[0])
            if upto == "l0":
                return
            norm_apply(n1b)
            for t, _, dst, v, j, m in shift_jobs:
                dve.wait_ge(shifted, j + 1)
                V.scalar_tensor_tensor(dst[:, 1:S], v[:, 0:S - 1], MUC(j)[0:m], dst[:, 1:S], ALU.mult, ALU.add).then_inc(evac_v, 1)
            dve.wait_ge(lora_pre, 1)
            V.tensor_scalar(lo3[0:32, :], lo3[0:32, :], 1.0, None, ALU.add)
            link(V.tensor_scalar(lo2, lo2, 1.0, None, ALU.add))
            V.reciprocal(lo3[0:32, :], lo3[0:32, :])
            V.reciprocal(lo2, lo2).then_inc(lora_in, 1)
            attention("mem1")
            t0_, t1_, t2_, t3_, t4_, t5_ = tmp
            dve.wait_ge(consts, 3)
            for j in range(JP):
                t = rp_tiles[j]
                tile_in(t["n"])
                V.tensor_scalar(t2_, bank[t["n"].bank][:], 1.0e-24, None, ALU.max).then_inc(evac_v, 1)
                dve.wait_ge(evac_v, t["n"].order + 1)
                dve.nop().then_inc(rp_v, 1)
                dve.wait_ge(evac_a, t["a"].order + 1)
                link(V.tensor_scalar(t1_, t1_, 1.0, None, ALU.add))
                link(V.reciprocal(t1_, t1_))
                link(V.tensor_scalar(kkT[:, j, :], kT7[:, j, :], col("rw_k_k", j), None, ALU.mult))
                dve.wait_ge(rp_a, 3 * j + 3)
                link(V.tensor_tensor(kkT[:, j, :], kkT[:, j, :], t2_, ALU.mult))
                V.tensor_tensor(bT[:, j, :], kkT[:, j, :], t1_, ALU.mult)
                link(V.tensor_scalar(t2_, t1_, -1.0, col("rw_k_a", j), ALU.add, ALU.mult))
                link(V.scalar_tensor_tensor(kT7[:, j, :], t2_, 1.0, kT7[:, j, :], ALU.add, ALU.mult))
                V.scalar_tensor_tensor(t4_, rT[:, j, :], col("rw_r_k", j), kT7[:, j, :], ALU.mult, ALU.mult).then_inc(rp_v, 1)
                link(V.tensor_scalar(t0_, t0_, 1.0, None, ALU.add))
                link(V.reciprocal(t0_, t0_))
                link(V.tensor_tensor_scan(t5_, keep[:], t0_, 0.0, ALU.mult, ALU.add))
                V.tensor_tensor(t0_, t5_, t0_, ALU.subtract).then_inc(rp_v, 1)
                tile_in(t["b"])
                V.tensor_tensor(bonT[:, j, :], vT7[:, j, :], bank[t["b"].bank][:], ALU.mult).then_inc(evac_v, 1)
                dve.wait_ge(rp_p, j + 1)
                V.tensor_tensor(bT[:, j, :], bT[:, j, :], t4_, ALU.mult)
                V.tensor_tensor(kT7[:, j, :], kT7[:, j, :], t4_, ALU.mult)
                V.tensor_tensor(rT[:, j, :], rT[:, j, :], t5_, ALU.mult)
                V.tensor_copy(pc[:, j, :], t5_[:, CH - 1:S:CH])
                V.scalar_tensor_tensor(kkT[:, j, :], kkT[:, j, :], -1.0, t3_, ALU.mult, ALU.mult).then_inc(rp_v, 1)
                dve.wait_ge(rp_v, 4 * j + 4)
            if upto == "rp":
                return
            w3 = lambda b_: b_[:, 0:384].rearrange("p (j n) -> p j n", j=JP)
            eyes = eye2[:].unsqueeze(1).broadcast_to([P, JP, HD])
            for c in range(NCH):
                cs = slice(c * CH, c * CH + CH)
                dve.wait_ge(rc_t, RC_T.at("gram", c))
                if c:
                    dve.wait_ge(rc_t, RC_T.at("s", c - 1))
                    dve.wait_ge(rc_p, 6 * c)
                cm = causal.unsqueeze(1).broadcast_to([P, 3, P])
                for dst, b0 in ((GA, 0), (GK, 2)):
                    for q_ in range(2):
                        last = V.tensor_tensor(dst[:, 3 * q_:3 * q_ + 3, :],
                                               bank[b0 + q_][:, 0:384].rearrange("p (j n) -> p j n", j=3), cm, ALU.mult)
                last.then_inc(rc_v, 1)
                dve.wait_ge(rc_p, 6 * c + 1)
                dve.wait_ge(rc_t, RC_T.at("eye", c))
                V.tensor_tensor(TTm, ALT[:, 0, :].rearrange("p (j n) -> p j n", j=JP), eyes, ALU.add)
                V.tensor_tensor(Tm, w3(bank[7]), eyes, ALU.add).then_inc(rc_v, 1)
                for l in range(1, 6):
                    dve.wait_ge(rc_t, RC_T.at(f"t{l}", c))
                    dve.wait_ge(rc_v, RC_V.at(f"t{l - 1}", c))
                    if l < 5:
                        V.tensor_tensor(Tm, Tm, w3(bank[1]), ALU.add)
                    V.tensor_tensor(TTm, TTm, w3(bank[2]), ALU.add).then_inc(rc_v, 1)
                dve.wait_ge(rc_t, RC_T.at("x", c))
                V.tensor_copy(Xm, w3(bank[3])).then_inc(rc_v, 1)
                dve.wait_ge(rc_t, RC_T.at("y", c))
                V.tensor_copy(rT[:, :, cs], w3(bank[5])).then_inc(rc_v, 1)
                dve.wait_ge(rc_t, RC_T.at("s", c))
                link(V.tensor_tensor(state[:], state[:], w3(bank[6]), ALU.add))
                V.tensor_tensor(state[:], state[:], pc[:, :, c:c + 1].broadcast_to([P, JP, HD]), ALU.mult).then_inc(rc_v, 1)
                dve.wait_ge(rc_v, RC_V.at("s", c))
            for j in range(JP):
                t0, t1 = gn_tiles[j]
                dve.wait_ge(evac_a, t0.order + 1)
                V.tensor_tensor(rT[:, j, :], rT[:, j, :], t0_, ALU.add).then_inc(gn_v, 1)
                dve.wait_ge(gn_v, 2 * j + 1)
                dve.wait_ge(gn_a, 3 * j + 3)
                link(V.scalar_tensor_tensor(rT[:, j, :], rT[:, j, :], col("rw_lnx_w", j), t2_, ALU.mult, ALU.mult))
                link(V.scalar_tensor_tensor(rT[:, j, :], rT[:, j, :], col("rw_lnx_b", j), bonT[:, j, :], ALU.add, ALU.add))
                V.tensor_tensor(hT[:, j, :], hT[:, j, :], rT[:, j, :], ALU.mult).then_inc(gn_v, 1)
            if upto == "gn":
                return
            add_residual(wo_jobs[1])
            swiglu_dve(ffn[1])
            norm_apply(n1f)
            for k, t in enumerate(mem2_tiles):
                if t.eng == "v":
                    copy_out(t, memT2[:, 2 * k:2 * k + 2, :], bank[t.bank][:].rearrange("p (k m) -> p k m", k=2))
            norm_apply(mem2_norm)
            plain(mem2_jobs)
            norm_apply(n2a)
            if upto == "b1":
                return
            for n, (t, _, dst, v, c) in enumerate(conv_jobs):
                dve.wait_ge(conv_a, n + 1)
                for s_ in (1, 2):
                    link(V.scalar_tensor_tensor(dst[:, s_:S], v[:, 0:S - s_], col("conv_w_2", 6 * (3 - s_) + c), dst[:, s_:S],
                                                ALU.mult, ALU.add))
                V.scalar_tensor_tensor(dst[:, 3:S], v[:, 0:S - 3], col("conv_w_2", c), dst[:, 3:S],
                                       ALU.mult, ALU.add).then_inc(evac_v, 1)
            dve.wait_ge(evac_v, conv_jobs[-1][0].order + 1)
            dve.nop().then_inc(conv_v, 6)
            t, _, v = dt_job
            tile_in(t)
            s8 = lambda i: small[:, i, :]
            s48 = lambda i: small[:, i, :].rearrange("p (c h) -> p c h", c=4)
            V.tensor_tensor(s48(0), v, bcast[:, 36:44].unsqueeze(1).broadcast_to([P, TT, 8]), ALU.add).then_inc(evac_v, 1)
            dve.wait_ge(evac_v, t.order + 1)
            link(V.tensor_scalar(s8(2), s8(0), -1.0, None, ALU.mult))
            link(V.tensor_tensor(s8(2), s8(2), s8(0), ALU.min))
            dve.nop().then_inc(gates_ready, 2)
            plain(qkv_jobs)
            dve.wait_ge(sd_a, 1)
            link(V.tensor_scalar(s8(0), s8(0), 0.0, None, ALU.max))
            link(V.tensor_tensor(s8(0), s8(0), s8(2), ALU.add))
            link(V.tensor_scalar(s8(2), s8(0), -1.0, None, ALU.mult))
            V.tensor_tensor(s48(1), s48(2), bcast[:, 44:52].unsqueeze(1).broadcast_to([P, TT, 8]), ALU.mult).then_inc(sd_v, 1)
            h3 = lambda v_: v_.rearrange("p (h d) -> p h d", h=8)
            for c, t in enumerate(xd_tiles):
                tile_in(t)
                V.tensor_tensor(h3(XD[:, c, :]), h3(bank[t.bank][:]),
                                small[:, 0, c * 8:c * 8 + 8].unsqueeze(2).broadcast_to([P, 8, HD]), ALU.mult).then_inc(evac_v, 1)
            tile_in(ac_tile)
            ab = bank[ac_tile.bank]
            link(V.tensor_scalar(s8(5), ab[:, 0:32], -1.0, None, ALU.mult))
            V.tensor_copy(s8(4), ab[:, 32:64])
            V.tensor_tensor(s8(3), s8(5), ab[:, 32:64], ALU.add).then_inc(evac_v, 1)
            dve.wait_ge(evac_v, ac_tile.order + 1)
            dve.nop().then_inc(sd_v, 1)
            dve.wait_ge(sd_a, 2)
            q4 = lambda v_: v_.rearrange("p (h l) -> p h l", h=4)
            dve.wait_ge(consts, 4)
            for c in range(TT):
                cs = slice(c * P, c * P + P)
                dve.wait_ge(sc_a, SC_A.at("er", c))
                for g in range(2):
                    last = V.tensor_tensor(q4(SEG[g]), q4(bank[4 + g][:]), hide_gt.unsqueeze(1).broadcast_to([P, 4, P]), ALU.add)
                last.then_inc(sc_v, 1)
                V.tensor_tensor(h3(XDD), h3(XD[:, c, :]), small[:, 3, c * 8:c * 8 + 8].unsqueeze(2).broadcast_to([P, 8, HD]),
                                ALU.mult).then_inc(sc_v, 1)
                dve.wait_ge(sc_a, SC_A.at("e", c))
                for g in range(2):
                    last = V.tensor_tensor(q4(MM_[g]), q4(SEG[g]), bank[(6, 2)[g]][:, 0:P].unsqueeze(1).broadcast_to([P, 4, P]),
                                           ALU.mult)
                last.then_inc(sc_v, 1)
                for g in range(2):
                    gs = slice(g * HD, g * HD + HD)
                    last = V.tensor_tensor(q4(CT[gs, :]), q4(ER[g][gs, :]), xbc[gs, 5, cs].unsqueeze(1).broadcast_to([HD, 4, P]),
                                           ALU.mult)
                last.then_inc(sc_v, 1)
                dve.wait_ge(sc_t, SC_T.at("y", c))
                for k in range(4):
                    last = V.scalar_tensor_tensor(yS[:, k, cs], xbc[:, k, cs], dskip[:, k:k + 1],
                                                  bank[(7, 1)[k // 2]][:, (k % 2) * P:(k % 2) * P + P],
                                                  ALU.mult, ALU.add)
                last.then_inc(sc_v, 1)
                dve.wait_ge(sc_t, SC_T.at("st", c))
                for g in range(2):
                    gs = slice(g * HD, g * HD + HD)
                    pv_ = bank[3][gs, 0:256].rearrange("p (h d) -> p h d", h=4)
                    cd = small[gs, 4, c * 8 + 4 * g:c * 8 + 4 * g + 4].unsqueeze(2).broadcast_to([HD, 4, HD])
                    if c == 0:
                        last = V.tensor_copy(SST[gs], pv_)
                    else:
                        link(V.tensor_tensor(SST[gs], SST[gs], cd, ALU.mult))
                        last = V.tensor_tensor(SST[gs], SST[gs], pv_, ALU.add)
                last.then_inc(sc_v, 1)
                dve.wait_ge(sc_v, SC_V.at("st", c))
            for k in range(4):
                last = V.tensor_tensor(yS[:, k, :], yS[:, k, :], zT[:, k, :], ALU.mult)
            last.then_inc(sd_v, 1)
            norm_apply(nssd)
            for u in range(4 * SH):
                h, js = u // 4, 3 - u % 4
                z_ = bank[4 + u % 2][:, js * P:S]
                dve.wait_ge(sb_t, 1 if u == 0 else 2 * u)
                if u >= 2:
                    dve.wait_ge(sb_v, 2 * (u - 2) + 2)
                V.tensor_scalar(T1[u % 2][:, js * P:S], z_, 80.0, None, ALU.min).then_inc(sb_v, 1)
                dve.wait_ge(sb_a, 3 * u + 2)
                if u >= 4:
                    dve.wait_ge(sb_t, 8 * (u // 4))
                link(V.tensor_tensor(SP[:, js, js * P:S], T1[u % 2][:, js * P:S], z_, ALU.max))
                dg = SP[:, js, js * P:js * P + P]
                V.tensor_tensor(dg, dg, triu_s, ALU.mult).then_inc(sb_v, 1)
                if u % 4 == 1 and u // 4 and (u // 4) % 2 == 0:
                    dve.wait_ge(sb_pv, u // 4)
                    V.tensor_copy(yB[:, u // 8 - 1, :], bank[7][:]).then_inc(sb_out, 1)
            dve.wait_ge(sb_pv, SH)
            V.tensor_copy(yB[:, 3, :], bank[7][:]).then_inc(sb_out, 1)
            norm_apply(nsb)
            if upto == "sb":
                return
            add_residual(wout_jobs)
            norm_apply(n2b)
            plain(xq_jobs)
            attention("xa")
            add_residual(wxo_jobs)
            norm_apply(n2c)
            for n, (t, _, j, v) in enumerate(ff1_jobs):
                dve.wait_ge(shifted, len(shift_jobs) + n + 1)
                V.tensor_tensor(hid[:, j, :], hid[:, j, :], v, ALU.mult).then_inc(evac_v, 1)
            add_split(ff2_halves)
            norm_apply(n2f)
            for i, t in enumerate(out_tiles):
                if t.eng == "v":
                    tt, kh = divmod(i, 2)
                    copy_out(t, out_sb[:, tt, kh * 512:kh * 512 + 512], bank[t.bank][:])


_OUT = (1, S, D)


def kernel(**inputs):
    import concourse.bacc as bacc
    from concourse.bass_utils import run_bass_kernel_spmd

    nc = bacc.Bacc("TRN2", target_bir_lowering=False, num_devices=1)
    arrays, args = {}, {}
    for name, value in inputs.items():
        v = np.ascontiguousarray(value)
        arrays[f"in_{name}"] = v
        args[name] = nc.dram_tensor(f"in_{name}", v.shape, mybir.dt.from_np(v.dtype), kind="ExternalInput").ap()
    out = nc.dram_tensor("out_x", _OUT, F32, kind="ExternalOutput").ap()
    block_stack(nc, args, out)
    r = run_bass_kernel_spmd(nc, [arrays], core_ids=[0])
    return r.results[0]["out_x"]
```

```python
import math
from contextlib import ExitStack

import numpy as np
import concourse.bass as bass
from concourse import mybir

F32 = mybir.dt.float32
F16 = mybir.dt.float16
BF16 = mybir.dt.bfloat16
ALU = mybir.AluOpType
ACT = mybir.ActivationFunctionType
AX = mybir.AxisListType

P = 128
D = 1024
KC = D // P
S = 512
TT = S // P
M = 256
HD = 64
NEG = -1.0e30

H1 = 12
G1 = 4
R1 = H1 // G1
MIX = H1 * HD
KV = G1 * HD
CB, CS = 32, 16
NCMP = (S - CB) // CS + 1
FH = 2816
FT = FH // P
SLOT = 3 * MIX + 64 + 64 + 160
DECAY = math.exp(-0.5)
CH = 64
NCH = S // CH
JP = H1 // 2
SD = 512
SH = 8
SG = 2
XH = 4
FF = 4096
FFT = FF // P
EPS1, EPS2, EPS_GN = 1e-6, 1e-5, 64e-5

NSLOT = 3
NSPLIT = 3
PANEL = 2048
AHEAD = 2
FF_SCALE = 1.0 / 8
NBANK = 4


def alibi_slopes(n):
    def pow2(m):
        start = 2.0 ** (-8.0 / m)
        return [start ** (i + 1) for i in range(m)]
    c = 2 ** int(math.floor(math.log2(n)))
    s = pow2(c)
    if c < n:
        s = s + pow2(2 * c)[0::2][: n - c]
    return [float(np.float32(v)) for v in s]


class Steps:

    def __init__(self, sem, *names):
        self.sem, self.names = sem, names

    def at(self, name, rnd):
        return rnd * len(self.names) + self.names.index(name) + 1


class Tile:

    def __init__(self, n, eng, order):
        self.n, self.bank, self.eng, self.order = n, n % NBANK, eng, order
        self.split = None


def block_stack(nc, a, out, upto=None):
    ctx = ExitStack()
    with ctx:
        def sb(name, shape, dt=F32):
            return ctx.enter_context(nc.sbuf_tensor(name, shape, dt))

        def sem(name):
            return ctx.enter_context(nc.semaphore(name))

        xT = sb("xT", [P, KC, S])
        h_hi = sb("h_hi", [P, KC, S], F16)
        h_lo = sb("h_lo", [P, KC, S], BF16)
        hT = (h_hi, h_lo)
        wring = sb("wring", [P, NSLOT, PANEL])
        w_hi = sb("w_hi", [P, NSPLIT, PANEL], F16)
        w_lo = sb("w_lo", [P, NSPLIT, PANEL], BF16)
        arena = sb("arena", [P, 54 * S])
        ntmp = sb("ntmp", [P, 2, S])
        ident = sb("ident", [P, P])
        ones = sb("ones", [P, P])
        nones = sb("nones", [P, P])
        blockones = sb("blockones", [P, P])
        eye2 = sb("eye2", [P, HD])
        dist = sb("dist", [P, S])
        distc = sb("distc", [P, TT, NCMP])
        keep = dist
        triu = sb("triu", [P, P])
        masks = sb("masks", [P, 4 * P])
        causal = masks[:, 0:P]
        level = masks[:, P:4 * P].rearrange("p (l n) -> p l n", l=6)
        triu_s, ntril = masks[:, 0:P], masks[:, P:2 * P]
        hide_gt, hide_ge = masks[:, 2 * P:3 * P], masks[:, 3 * P:4 * P]
        qscale = sb("qscale", [P, 6])
        cols = sb("cols", [P, 320])
        ncols = sb("ncols", [P, 16])
        omu = sb("omu", [P, 21])
        eps = sb("eps", [P, 5])
        bcast = sb("bcast", [P, 60])
        dskip = sb("dskip", [P, 4])
        cmp_w2 = sb("cmp_w2", [P, 2, HD])
        stat = sb("stat", [P, 3, 4, 2])
        cst = sb("cst", [P, 3, 48])
        cslope = sb("cslope", [P, 12])
        rsb = sb("rsb", [P, S])
        small = sb("small", [P, 6, 32])
        gates = small[:, :, :].rearrange("p a b -> p (a b)")[:, 0:TT * 36].rearrange("p (t n) -> p t n", t=TT)
        bank = [ctx.enter_context(nc.psum_tensor(f"bank{i}", [P, S], F32)) for i in range(8)]

        def blk(first, n=1, width=S):
            v = arena[:, first * S:first * S + n * width]
            return v.rearrange("p (n w) -> p n w", n=n)

        def parts(first, n, width=S):
            m = n * width // 2
            return tuple(arena[:, first * S + i * m:first * S + (i + 1) * m].bitcast(dt)
                         .rearrange("p (n w) -> p n w", n=n) for i, dt in enumerate((F16, BF16)))

        rows = blk(30)[:, 0, 0:3 * P].rearrange("p (j n) -> p j n", j=3)

        landed = [sem(f"landed{i}") for i in range(NSLOT)]
        panel_read = sem("panel_read")
        acc_full = sem("acc_full")
        evac_v = sem("evac_v")
        evac_a = sem("evac_a")
        consts = sem("consts")
        vec_in = sem("vec_in")
        cols_ready = sem("cols_ready")
        split_hi = sem("split_hi")
        split_lo = sem("split_lo")
        squared = sem("squared")
        norm_part = sem("norm_part")
        scaled = sem("scaled")
        cast = sem("cast")
        hid_f = sem("hid_f")
        hid_hi = sem("hid_hi")
        hid_lo = sem("hid_lo")
        cmp_s = sem("cmp_s")
        cmp_u = sem("cmp_u")
        cmp_e = sem("cmp_e")
        cmp_w = sem("cmp_w")
        cmp_t = sem("cmp_t")
        cmp_pt = sem("cmp_pt")
        cmp_ptv = sem("cmp_ptv")
        att_hi = sem("att_hi")
        mix_hi = sem("mix_hi")
        rooted = sem("rooted")
        normed = sem("normed")
        chain_v = sem("chain_v")
        chain_a = sem("chain_a")
        chain_p = sem("chain_p")
        gates_ready = sem("gates_ready")
        gate_exp_in = sem("gate_exp_in")
        gate_exp = sem("gate_exp")
        gelu_in = sem("gelu_in")
        gelu_exp = sem("gelu_exp")
        gelu_out = sem("gelu_out")
        cmp_ready = sem("cmp_ready")
        att_scores = sem("att_scores")
        att_max = sem("att_max")
        att_exp = sem("att_exp")
        att_weight = sem("att_weight")
        att_turned = sem("att_turned")
        att_copied = sem("att_copied")
        att_pv = sem("att_pv")
        att_out = sem("att_out")
        shifted = sem("shifted")
        lora_pre = sem("lora_pre")
        lora_mid = sem("lora_mid")
        lora_in = sem("lora_in")
        rp_a = sem("rp_a")
        rp_v = sem("rp_v")
        rp_p = sem("rp_p")
        rc_t = sem("rc_t")
        rc_v = sem("rc_v")
        rc_a = sem("rc_a")
        rc_p = sem("rc_p")
        gn_v = sem("gn_v")
        gn_a = sem("gn_a")
        sd_v = sem("sd_v")
        sd_a = sem("sd_a")
        sc_t = sem("sc_t")
        sc_v = sem("sc_v")
        sc_a = sem("sc_a")
        conv_a = sem("conv_a")
        conv_v = sem("conv_v")
        sb_t = sem("sb_t")
        sb_v = sem("sb_v")
        sb_a = sem("sb_a")
        sb_pv = sem("sb_pv")
        sb_out = sem("sb_out")
        out_sent = sem("out_sent")

        tiles, order = [], {"v": 0, "a": 0}

        def tile(eng):
            t = Tile(len(tiles), eng, order[eng])
            order[eng] += 1
            tiles.append(t)
            return t

        panels = []

        splits = []

        def panel(*srcs):
            p = {"slot": len(panels) % NSLOT, "n": len(panels), "until": None}
            before = panels[-NSLOT]["level"] if len(panels) >= NSLOT else 0
            p["parts"] = [(f(wring[:, p["slot"], :]), src) for f, src in srcs]
            p["level"] = before + 16 * len(srcs)
            panels.append(p)
            return p

        def split_panel(k, n, *srcs):
            p = panel(*srcs)
            p.update(m=len(splits), size=k * n, until=(split_lo, len(splits) + 1), read=None)
            sl = p["m"] % NSPLIT
            p["hi"], p["lo"] = (w_[:, sl, 0:k * n].rearrange("p (k n) -> p k n", k=k) for w_ in (w_hi, w_lo))
            splits.append(p)
            return p

        def columns(w, c0, n, k=KC):
            return split_panel(k, n, (lambda s: s[:, 0:k * n].rearrange("p (k n) -> p k n", k=k),
                                      w[0:k * P, c0:c0 + n].rearrange("(k p) n -> p k n", p=P)))

        def until_tile(p, t):
            p["read" if "m" in p else "until"] = (acc_full, t.n + 1)
            if "m" in p:
                t.split = p["m"]

        vec = {}
        vec_dmas = []
        nrow = [0]

        def vrow(name, src, n):
            vec[name] = nrow[0]
            r = 0
            while r < n:
                j, o = divmod(nrow[0] + r, P)
                m = min(n - r, P - o)
                vec_dmas.append((rows[o:o + m, j, :], src[r:r + m, :]))
                r += m
            nrow[0] += n

        for nm in ("norm1", "norm_mem", "norm2"):
            vrow(nm, a[nm].rearrange("l (k p) -> (l k) p", p=P), 2 * KC)
        for nm in ("final_norm", "final_g_2"):
            vrow(nm, a[nm].rearrange("(k p) -> k p", p=P), KC)
        for nm in ("norm_mix_g_2", "norm_xa_g_2", "norm_mem_g_2", "norm_ff_g_2"):
            vrow(nm, a[nm].rearrange("l (k p) -> (l k) p", p=P), KC)
        for nm in ("ssd_norm_g_2", "sb_norm_g_2"):
            vrow(nm, a[nm].rearrange("l (k p) -> (l k) p", p=P), 4)
        vrow("rw_mu", a["rw_mu"][:, 0:20 * P].rearrange("l (k p) -> (l k) p", p=P), 20)
        for nm in ("rw_w0", "rw_a0", "rw_k_k", "rw_k_a", "rw_lnx_w", "rw_lnx_b"):
            vrow(nm, a[nm].rearrange("l (k p) -> (l k) p", p=P), 6)
        vrow("rw_r_k", a["rw_r_k"].rearrange("l (c two) d -> (l c) (two d)", two=2), 6)
        vrow("conv_w_2", a["conv_w_2"].rearrange("l k (c p) -> (l k c) p", p=P), 24)
        vrow("conv_b_2", a["conv_b_2"].rearrange("l (c p) -> (l c) p", p=P), 6)
        NVEC = nrow[0]
        MU20 = NVEC
        j20, o20 = divmod(MU20, P)
        vec_dmas.append((rows[o20:o20 + 1, j20, 0:32], a["rw_mu"][:, 20 * P:SLOT]))
        NROW1 = NVEC + 1 - P
        POS = 256
        vec_dmas.append((rows[0:64, 2, 0:HD], a["nsa_cmp_pos"].rearrange("z j l d -> (z j l) d")))
        vec_dmas.append((bcast[:, 0:36], a["nsa_gate_b"].rearrange("a n -> (a n)").partition_broadcast(P)))
        vec_dmas.append((bcast[:, 36:44], a["dt_bias_2"].rearrange("a n -> (a n)").partition_broadcast(P)))
        vec_dmas.append((bcast[:, 44:52], a["a_log_2"].rearrange("a n -> (a n)").partition_broadcast(P)))
        vec_dmas.append((bcast[:, 52:60], a["d_skip_2"].rearrange("a n -> (a n)").partition_broadcast(P)))
        vec_dmas.append((cmp_w2[:, :, :], a["nsa_cmp_w2"].rearrange("z j e d -> e (z j) d")))

        def col(name, j, p0=0, p1=P):
            return cols[p0:p1, vec[name] + j:vec[name] + j + 1]

        MUC = lambda j: cols[:, (vec["rw_mu"] + j if j < 20 else MU20):(vec["rw_mu"] + j if j < 20 else MU20) + 1]

        vec_tile = tile("v")

        def rows_panel(src, nt):
            p = panel((lambda s: s[:, 0:nt * D].rearrange("p (t d) -> p t d", t=nt),
                       src.rearrange("z (t p) d -> p (z t) d", p=P)))
            p["v"] = wring[:, p["slot"], 0:nt * D].rearrange("p (t d) -> p t d", t=nt)
            return p

        x_panels = [rows_panel(a["x"][:, hf * M:hf * M + M, :], 2) for hf in range(2)]
        x_tiles = [tile("va"[k % 2]) for k in range(KC)]
        for p in x_panels:
            until_tile(p, x_tiles[-1])
        mem_panel = rows_panel(a["mem"], 2)
        memT = blk(40, KC, M)
        mem_tiles = [tile("va"[k % 2]) for k in range(KC // 2)]
        until_tile(mem_panel, mem_tiles[-1])

        norms, nk = [], [0, 0]

        def norm(src, dst, gain, k, n, epscol):
            nm = dict(src=src, dst=dst, gain=gain, k=k, n=n, eps=epscol, j=len(norms), b=nk[0], c=nk[1])
            nk[0] += k
            nk[1] += k * isinstance(dst, tuple)
            norms.append(nm)
            return nm

        def feature_tile(w, c, width, h, eng, n=S, k=KC, m=P):
            t = tile(eng)
            v = bank[t.bank][0:m, 0:n]
            mm = [(v, [(w[a_][:, kk, c:c + m], h[b_][:, kk, 0:n], w, kk) for kk in range(k)
                       for a_, b_ in (("hi", 0), ("hi", 1), ("lo", 0))])]
            until_tile(w, t)
            return t, mm, v

        def token_tile(w, c, width, h, tts, eng, k=KC):
            t = tile(eng)
            v = bank[t.bank][:, 0:len(tts) * width].rearrange("p (t w) -> p t w", t=len(tts))
            mm = [(v[:, i, :], [(h[b_][:, kk, tt * P:tt * P + P], w[a_][:, kk, c:c + width], w, kk) for kk in range(k)
                                for b_, a_ in ((0, "hi"), (0, "lo"), (1, "hi"))])
                  for i, tt in enumerate(tts)]
            until_tile(w, t)
            return t, mm, v

        mn = parts(32, KC, M)
        kmT = [blk(44 + 2 * l, 2, M) for l in range(2)]
        vm = [blk(45 + 2 * l, 2, M) for l in range(2)]
        mem_norm, mem_jobs = [], []
        for l in range(2):
            mem_norm.append(norm(memT, mn, ("norm_mem", l * KC), KC, M, 0))
            w = columns(a["w_mem_kv"][l], 0, M)
            jobs = []
            for c in range(2):
                t, mm, v = feature_tile(w, c * P, P, mn, "va"[c], n=M)
                jobs.append((t, mm, kmT[l][:, c, :], v, 1.0))
            w = columns(a["w_mem_kv"][l], M, M)
            t, mm, v = token_tile(w, 0, M, mn, range(2), "v")
            jobs.append((t, mm, vm[l][:, :, :], v, 1.0))
            mem_jobs.append(jobs)

        qT, kcT, vcT = blk(0, 6), blk(6, 2), blk(8, 2)
        ksT, kwT, qmT = blk(10, 2), blk(12, 2), blk(14, 2)
        vs, vw = blk(16, 4, KV), blk(18, 4, KV)
        n1a = norm(xT, hT, ("norm1", 0), KC, S, 0)
        wn = a["nsa_w_in"][0]
        nsa_jobs = []
        slopes = alibi_slopes(H1)
        pair = lambda h: (h // 6) * 3 + h % 3
        for gp in range(2):
            for r in range(3):
                w = split_panel(KC, P, *[
                    ((lambda s, gg=gg: s[:, 0:KC * P].rearrange("p (k g d) -> p k g d", k=KC, g=2)[:, :, gg, :]),
                     wn[:, (3 * (2 * gp + gg) + r) * HD:(3 * (2 * gp + gg) + r + 1) * HD].rearrange("(k p) d -> p k d", p=P))
                    for gg in range(2)])
                t, mm, v = feature_tile(w, 0, P, hT, "va"[r % 2])
                nsa_jobs.append((t, mm, qT[:, gp * 3 + r, :], v, qscale[:, gp * 3 + r:gp * 3 + r + 1]))
        for c0, dst in ((MIX, kcT), (MIX + KV, vcT), (MIX + 2 * KV, ksT), (MIX + 4 * KV, kwT), (MIX + 6 * KV + 36, qmT)):
            w = columns(wn, c0, KV)
            for c in range(2):
                t, mm, v = feature_tile(w, c * P, P, hT, "va"[c % 2])
                nsa_jobs.append((t, mm, dst[:, c, :], v, HD ** -0.5 if dst is qmT else 1.0))
        for c0, v_ in ((MIX + 3 * KV, vs), (MIX + 5 * KV, vw)):
            w = columns(wn, c0, KV)
            for i in range(2):
                t, mm, v = token_tile(w, 0, KV, hT, range(2 * i, 2 * i + 2), "va"[i % 2])
                nsa_jobs.append((t, mm, v_[:, 2 * i:2 * i + 2, :], v, 1.0))
        w = columns(wn, MIX + 6 * KV, 36)
        gate_job = token_tile(w, 0, 36, hT, range(TT), "v")

        cmp_panels = []
        for j in range(2):
            for lh in range(2):
                src = a["nsa_cmp_w1"][0, j, lh * 16:lh * 16 + 16].rearrange("l d e -> d l e")
                w = panel(*[((lambda s, hf=hf: s[hf * HD:hf * HD + HD, :].rearrange("p (l e) -> p l e", l=16)), src)
                            for hf in range(2)])
                w["v"] = wring[:, w["slot"], :].rearrange("p (l e) -> p l e", l=16)
                cmp_panels.append(w)
        cmp_hid = [tile("v") for _ in range(2)]
        for j in range(4):
            until_tile(cmp_panels[j], cmp_hid[j // 2])
        cmp_res = [tile("v") for _ in range(2)]
        kcb = blk(26)[:, 0, 0:2 * NCMP].rearrange("p (c n) -> p c n", c=2)
        vcb = blk(27)[0:NCMP, 0, 0:KV].rearrange("p (g d) -> p g d", g=G1)
        cbias = blk(27)[:, 0, KV:KV + 1]
        chid = blk(28)[:, 0, 0:248].rearrange("p (j n) -> p j n", j=2)
        ctmp = blk(28)[:, 0, 256:380]

        cmp_heads = [[6 * a_ + 3 * e + r for a_ in range(2) for r in range(3)] for e in range(2)]
        cmp_head = lambda x: cmp_heads[x // 6][x % 6]
        CU = blk(40, 3)[:, :, :].rearrange("p a w -> p (a w)")[:, 0:48 * NCMP].rearrange("p (x n) -> p x n", x=48)
        PTc = blk(28, 12)

        groups = []
        att_stage = {}
        nout = [0]

        def group(pb, ptb, **k):
            n = len(groups)
            k["n"] = n
            k["s"] = [bank[2 * (n % 2) + w] for w in range(2)]
            k["P"] = [blk(pb + 2 * (n % 3) + w)[:, 0, :] for w in range(2)]
            k["PT"] = [blk(ptb + 2 * (n % 2) + w)[:, 0, :] for w in range(2)]
            k["st"] = stat[:, n % 3, :, :]
            k["out0"] = nout[0]
            if k.get("evac") is not None:
                nout[0] += 1
            groups.append(k)

        zeros = sb("zeros", [P, M])
        att_stage["nsa"] = [0]
        for c in range(6):
            ob = bank[6 + c % 2]
            for i in range(TT):
                for hf in range(2):
                    h = 2 * c + hf
                    g = h // R1
                    b0 = HD * (g % 2)
                    q = qT[b0:b0 + HD, pair(h), i * P:i * P + P]
                    N = (i + 1) * P
                    dd = dist[:, (TT - 1 - i) * P:S]
                    o = ob[hf * HD:hf * HD + HD, i * P:i * P + P]
                    group(20, 40, slope=slopes[h], N=N, gates=gates[:, i, H1 + h:3 * H1:H1],
                          first=((ob[hf * HD:hf * HD + HD, :], vcb[:, g, :], PTc[0:NCMP, h, :]) if i == 0 else None),
                          units=[dict(q=q, k=kT_[b0:b0 + HD, g // 2, 0:N], D=dd, o=o, start=False,
                                      v=[v_[:, t, g * HD:g * HD + HD] for t in range(i + 1)])
                                 for kT_, v_ in ((ksT, vs), (kwT, vw))],
                          evac=(ob, c) if (i == TT - 1 and hf == 1) else None, ob=(i == 0 and hf == 0))

        def mem_groups(l, qm, pb, ptb):
            for c in range(2):
                ob = bank[6 + c % 2]
                for i in range(TT):
                    group(pb, ptb, slope=1.0, N=M, gates=None, first=None, ob=(i == 0),
                          units=[dict(q=qm[hf * HD:hf * HD + HD, c, i * P:i * P + P], k=kmT[l][hf * HD:hf * HD + HD, c, :],
                                      D=zeros[:, :], o=ob[hf * HD:hf * HD + HD, i * P:i * P + P], start=True,
                                      v=[vm[l][:, t, (2 * c + hf) * HD:(2 * c + hf + 1) * HD] for t in range(2)])
                                 for hf in range(2)],
                          evac=(ob, 6 + c) if i == TT - 1 else None)

        mem_groups(0, qmT, 20, 40)
        att_stage["nsa"].append(len(groups))

        def residual(w_dram, h, k):
            jobs = []
            per_panel = PANEL // k
            for c0 in range(0, D, per_panel):
                w = columns(w_dram, c0, per_panel, k)
                for c in range(per_panel // P):
                    t, mm, v = feature_tile(w, c * P, P, h, "v", k=k)
                    jobs.append((t, mm, (c0 // P) + c, v))
            return jobs

        def residual_split(w_dram, h, k):
            halves = []
            for hf in range(2):
                ts = [tile("v") for _ in range(4)]
                ps = []
                for k0 in range(0, k, 4):
                    kk = min(4, k - k0)
                    w = columns(w_dram[k0 * P:(k0 + kk) * P, :], hf * 512, 512, kk)
                    ps.append((w, k0, kk))
                halves.append((hf, ts, ps, h))
            return halves

        wo_jobs = [None, None]
        wo_jobs[0] = residual(a["w_o"][0], hT, KC)
        hid = parts(0, 32)
        hraw = [blk(32, 2), blk(34, 2)]

        def swiglu(l):
            nm = norm(xT, hT, ("norm2", l * KC), KC, S, 0)
            jobs = []
            wi = a["w_ffn_in"][l]
            for b in range(FT):
                w = split_panel(KC, 2 * P, *[
                    ((lambda s, o=o: s.rearrange("p (k n) -> p k n", k=KC)[:, :, o * P:o * P + P]),
                     wi[:, o * FH + b * P:o * FH + b * P + P].rearrange("(k p) n -> p k n", p=P)) for o in range(2)])
                jobs.append((feature_tile(w, 0, P, hT, "a"), feature_tile(w, P, P, hT, "v"), b))
            return [nm, jobs, residual_split(a["w_ffn_out"][l], hid, FT), l * FT]

        ffn = [swiglu(0)]

        rT, kT7, vT7 = blk(0, 6), blk(6, 6), blk(12, 6)
        kkT, bT, bonT = blk(18, 6), blk(24, 6), blk(30, 6)
        lo, lo2, lo3, qm1 = blk(36)[:, 0, :], blk(37)[:, 0, :], blk(38)[:, 0, :], blk(39, 2)
        n1b = norm(xT, hT, ("norm1", KC), KC, S, 0)
        ffn[0].append(n1b)
        wr = a["rw_w_in"][0]
        shift_jobs, qm1_jobs = [], []
        for b in range(10):
            w = columns(wr, b * M, M)
            for c in range(2):
                j = 2 * b + c
                dst = blk(j)[:, 0, :] if j < 18 else (lo if j == 18 else lo2)
                t, mm, v = feature_tile(w, c * P, P, hT, "v")
                shift_jobs.append((t, mm, dst, v, j, P))
        w = columns(wr, 2560, 32)
        t, mm, v = feature_tile(w, 0, 32, hT, "v", m=32)
        shift_jobs.append((t, mm, lo3[0:32, :], v, 20, 32))
        w = columns(wr, 2592, M)
        for c in range(2):
            t, mm, v = feature_tile(w, c * P, P, hT, "a")
            qm1_jobs.append((t, mm, qm1[:, c, :], v, HD ** -0.5))
        lora_panels = [panel((lambda s: s[0:64, 0:MIX], a["rw_w2"][0]),
                             (lambda s: s[64:128, 0:MIX], a["rw_a2"][0]),
                             (lambda s: s[:, MIX:2 * MIX], a["rw_g2"][0, 0:P, :])),
                       panel((lambda s: s[0:32, 0:MIX], a["rw_g2"][0, P:160, :]))]
        lw, lw2 = (wring[:, p["slot"], :] for p in lora_panels)
        att_stage["mem1"] = [len(groups)]
        mem_groups(1, qm1, 18, 24)
        att_stage["mem1"].append(len(groups))
        gT = blk(48, 6)
        rp_tiles = [dict(w=tile("a"), a=tile("a"), g=tile("a"), n=tile("v"), b=tile("v")) for _ in range(JP)]
        for p in lora_panels:
            until_tile(p, rp_tiles[-1]["g"])
        tmp = [blk(41 + i)[:, 0, :] for i in range(4)] + [blk(45)[:, 0, :], rsb[:, :]]
        pc = sb("pc", [P, JP, NCH])
        gn_tiles = [(tile("a"), tile("a")) for _ in range(JP)]
        GA = arena[:, 36 * S:36 * S + 768].rearrange("p (j n) -> p j n", j=JP)
        GK = arena[:, 36 * S + 768:36 * S + 1536].rearrange("p (j n) -> p j n", j=JP)
        o_ = 39 * S
        tv = []
        for i in range(9):
            tv.append(arena[:, o_ + i * 384:o_ + i * 384 + 384].rearrange("p (j n) -> p j n", j=JP))
        BT, KT, VT, Tm, TTm, Ym, Xm, Um, Tn = tv
        TTn = Xm
        NALT = 3
        ALT = arena[:, o_ + 9 * 384:o_ + 9 * 384 + NALT * 384].rearrange("p (a n) -> p a n", a=NALT)
        state = sb("state", [P, JP, HD])
        wo_jobs[1] = residual(a["w_o"][1], hT, KC)
        ffn.append(swiglu(1))
        n1f = norm(xT, xT, ("final_norm", 0), KC, S, 0)
        ffn[1].append(n1f)

        mem2_panel = rows_panel(a["mem_2"], 2)
        memT2, mn2 = blk(40, KC, M), parts(36, KC, M)
        mem2_tiles = [tile("va"[k % 2]) for k in range(KC // 2)]
        until_tile(mem2_panel, mem2_tiles[-1])
        mem2_norm = norm(memT2, mn2, ("norm_mem_g_2", 0), KC, M, 1)
        kxT, vx = blk(44, 4, M), blk(46, 2)
        mem2_jobs = []
        for b in range(2):
            w = columns(a["w_xk_2"][0], b * M, M)
            for c in range(2):
                t, mm, v = feature_tile(w, c * P, P, mn2, "va"[c % 2], n=M)
                mem2_jobs.append((t, mm, kxT[:, 2 * b + c, :], v, 1.0))
        for b in range(2):
            w = columns(a["w_xv_2"][0], b * M, M)
            t, mm, v = token_tile(w, 0, M, mn2, range(2), "va"[b % 2])
            mem2_jobs.append((t, mm, vx[:, :, b * M:b * M + M], v, 1.0))
        n2a = norm(xT, hT, ("norm_mix_g_2", 0), KC, S, 1)
        zT, xbc, q2, k2, v2 = blk(0, 4), blk(4, 6), blk(10, 4), blk(14, 4), blk(18, 4)
        wi2 = a["w_in_2"][0]
        z_jobs, conv_jobs, qkv_jobs = [], [], []
        for b in range(2):
            w = columns(wi2, b * M, M)
            for c in range(2):
                t, mm, v = feature_tile(w, c * P, P, hT, "a")
                z_jobs.append((t, mm, zT[:, 2 * b + c, :], v))
        for b in range(3):
            w = columns(wi2, 512 + b * M, M)
            for c in range(2):
                t, mm, v = feature_tile(w, c * P, P, hT, "v")
                conv_jobs.append((t, mm, xbc[:, 2 * b + c, :], v, 2 * b + c))
        w = columns(wi2, 1280, 8)
        dt_job = token_tile(w, 0, 8, hT, range(TT), "v")
        for c0, dst, sc in ((1288, q2, HD ** -0.5), (1800, k2, 1.0)):
            for b in range(2):
                w = columns(wi2, c0 + b * M, M)
                for c in range(2):
                    t, mm, v = feature_tile(w, c * P, P, hT, "va"[c % 2])
                    qkv_jobs.append((t, mm, dst[:, 2 * b + c, :], v, sc))
        for b in range(2):
            w = columns(wi2, 2312 + b * M, M)
            for i in range(2):
                t, mm, v = token_tile(w, 0, M, hT, range(2 * i, 2 * i + 2), "va"[i % 2])
                qkv_jobs.append((t, mm, v2[:, 2 * i:2 * i + 2, b * M:b * M + M], v, 1.0))
        XD, Btok = blk(24, 4), blk(28)[:, 0, :]
        xd_tiles = [tile("v") for _ in range(4)]
        bt_tile = tile("a")
        ac_tile = tile("v")
        SEG = [blk(29)[:, 0, :], blk(30)[:, 0, :]]
        MM_ = [blk(31)[:, 0, :], blk(32)[:, 0, :]]
        ER = [blk(33)[:, 0, :], blk(34)[:, 0, :]]
        CT = blk(35)[:, 0, :]
        XDD = blk(22)[:, 0, :]
        SST = state[:, 0:4, :]
        yS = blk(36, 4)
        nssd = norm(yS, (h_hi[:, 0:4, :], h_lo[:, 0:4, :]), ("ssd_norm_g_2", 0), 4, S, 1)
        SP, WT = blk(24, 4), blk(28, 4)
        T1 = [blk(22)[:, 0, :], blk(23)[:, 0, :]]
        yB = blk(40, 4)
        nsb = norm(yB, (h_hi[:, 4:8, :], h_lo[:, 4:8, :]), ("sb_norm_g_2", 0), 4, S, 1)
        wout_jobs = residual(a["w_out_2"][0], hT, KC)
        n2b = norm(xT, hT, ("norm_xa_g_2", 0), KC, S, 1)
        qx = blk(0, 4)
        xq_jobs = []
        for b in range(2):
            w = columns(a["w_xq_2"][0], b * M, M)
            for c in range(2):
                t, mm, v = feature_tile(w, c * P, P, hT, "va"[c % 2])
                xq_jobs.append((t, mm, qx[:, 2 * b + c, :], v, P ** -0.5))
        att_stage["xa"] = [len(groups)]
        for h in range(XH):
            ob = bank[6 + h % 2]
            for i2 in range(2):
                group(8, 14, slope=1.0, N=M, gates=None, first=None, ob=(i2 == 0),
                      units=[dict(q=qx[:, h, i * P:i * P + P], k=kxT[:, h, :], D=zeros[:, :], o=ob[:, i * P:i * P + P],
                                  start=True, v=[vx[:, t, h * P:h * P + P] for t in range(2)])
                             for i in (2 * i2, 2 * i2 + 1)],
                      evac=(ob, h) if i2 == 1 else None)
        att_stage["xa"].append(len(groups))
        wxo_jobs = residual(a["w_xo_2"][0], hT, 4)
        n2c = norm(xT, hT, ("norm_ff_g_2", 0), KC, S, 1)
        ff1_jobs = []
        for b in range(16):
            w = columns(a["w_ff1_2"][0], b * M, M)
            for c in range(2):
                t, mm, v = feature_tile(w, c * P, P, hT, "v")
                ff1_jobs.append((t, mm, 2 * b + c, v))
        ff2_halves = residual_split(a["w_ff2_2"][0], hid, FFT)
        yT = blk(36, 8)
        n2f = norm(xT, yT, ("final_g_2", 0), KC, S, 1)
        out_sb = blk(0, 4, D)
        out_tiles = [tile("va"[i % 2]) for i in range(8)]

        nread = 0
        for halves in (ffn[0][2], ffn[1][2], ff2_halves):
            for hf, ts, ps, h in halves:
                for w, k0, kk in ps:
                    if w is ps[-1][0]:
                        until_tile(w, ts[-1])
                    else:
                        nread += 1
                        w["read"] = (panel_read, nread)

        def read_out(eng, ts):
            for e, s_ in (("v", evac_v), ("a", evac_a)):
                n = [t.order for t in ts if t.eng == e]
                if n:
                    eng.wait_ge(s_, max(n) + 1)

        def done(t):
            return evac_v if t.eng == "v" else evac_a

        def splits_until(m, now):
            while m >= len(splits):
                m -= 1
            while m > now and splits[m]["n"] - splits[now]["n"] != m - now:
                m -= 1
            return m

        def chained(eng, s_):
            n = [0]

            def link(ins):
                n[0] += 1
                ins.then_inc(s_, 1)
                eng.wait_ge(s_, n[0])
            return link

        RC_T = Steps(rc_t, "gram", "tok", "eye", *[x for l in range(1, 6) for x in (f"y{l}", f"t{l}")], "x", "u", "y", "s")
        RC_V = Steps(rc_v, "mask", "t0", *[f"t{l}" for l in range(1, 6)], "x", "y", "s")
        RC_A = Steps(rc_a, "tok", *[f"y{l}" for l in range(1, 6)], "u")
        SC_T = Steps(sc_t, "row", "y", "st")
        SC_V = Steps(sc_v, "seg", "xdd", "m", "ct", "y", "st")
        SC_A = Steps(sc_a, "er", "e")
        jobs_of = lambda jobs: [j[0] for j in jobs]

        block = ctx.enter_context(nc.Block())

        @block.sync
        def _(sp):
            for p in panels:
                if p["n"] >= NSLOT:
                    sp.wait_ge(*panels[p["n"] - NSLOT]["until"])
                for dst, src in p["parts"]:
                    sp.dma_start(dst, src).then_inc(landed[p["slot"]], 16)
            o = out.rearrange("z (t p) d -> p (z t) d", p=P)
            for tt in range(TT):
                read_out(sp, out_tiles[2 * tt:2 * tt + 2])
                sp.dma_start(o[:, tt, :], out_sb[:, tt, :]).then_inc(out_sent, 16)
            sp.wait_ge(out_sent, 16 * TT)

        @block.gpsimd
        def _(pool):
            link = chained(pool, chain_p)
            ms = nc.gpsimd.memset
            aff = nc.gpsimd.affine_select

            def fill(t, value, *conds):
                link(ms(t, value))
                for pat, base, cm, other in conds:
                    link(aff(out=t, in_=t, compare_op=ALU.is_ge, fill=other, base=base, pattern=pat, channel_multiplier=cm))

            link(ms(ident[:], 0.0))
            link(aff(out=ident[:], in_=ident[:], compare_op=ALU.not_equal, fill=1.0, base=0, pattern=[[-1, P]],
                     channel_multiplier=1))
            link(ms(ones[:], 1.0))
            link(ms(nones[:], -1.0))
            link(ms(rows[:], 0.0))
            for i, e in enumerate((EPS1, EPS2, EPS_GN, 1.0, 1e-24)):
                link(ms(eps[:, i:i + 1], e))
            for gp in range(2):
                for r in range(3):
                    for gg in range(2):
                        h = 3 * (2 * gp + gg) + r
                        x = 6 * gg + 3 * gp + r
                        link(ms(cslope[:, x:x + 1], slopes[h]))
                        link(ms(qscale[gg * HD:gg * HD + HD, gp * 3 + r:gp * 3 + r + 1], HD ** -0.5 / slopes[h]))
            pool.nop().then_inc(consts, 1)
            link(ms(zeros[:], 0.0))
            link(ms(blockones[:], 0.0))
            for hf in range(2):
                s_ = slice(hf * HD, hf * HD + HD)
                link(ms(blockones[s_, s_], 1.0))
                link(ms(eye2[s_, :], 0.0))
                link(aff(out=eye2[s_, :], in_=eye2[s_, :], compare_op=ALU.not_equal, fill=1.0, base=0,
                         pattern=[[-1, HD]], channel_multiplier=1))
                fill(causal[s_, 0:HD], 1.0, ([[1, HD]], -1, -1, 0.0))
                fill(causal[s_, HD:P], 1.0, ([[1, HD]], 0, -1, 0.0))
                for l in range(6):
                    m = 1 << l
                    nb = HD // (2 * m)
                    v = level[s_, l, :].rearrange("p (b o w) -> p b o w", b=nb, o=2)
                    link(ms(level[s_, l, :], 0.0))
                    link(ms(v[:, :, 1, :], 1.0))
                    for pat, base, cm in (([[-2 * m, nb], [0, m]], 0, 1), ([[2 * m, nb], [0, m]], m - 1, -1)):
                        link(aff(out=v[:, :, 1, :], in_=v[:, :, 1, :], compare_op=ALU.is_ge, fill=0.0, base=base,
                                 pattern=pat, channel_multiplier=cm))
            link(nc.gpsimd.iota(dist[:], pattern=[[1, S]], base=-(S - P), channel_multiplier=-1,
                                allow_small_or_imprecise_dtypes=True))
            link(aff(out=dist[:], in_=dist[:], compare_op=ALU.is_ge, fill=NEG, base=S - P, pattern=[[-1, S]],
                     channel_multiplier=1))
            link(nc.gpsimd.iota(distc[:], pattern=[[-P, TT], [CS, NCMP]], base=CB - 1, channel_multiplier=-1,
                                allow_small_or_imprecise_dtypes=True))
            link(aff(out=distc[:], in_=distc[:], compare_op=ALU.is_ge, fill=NEG, base=-(CB - 1),
                     pattern=[[P, TT], [-CS, NCMP]], channel_multiplier=1))
            fill(triu[:], 1.0, ([[1, P]], 0, -1, 0.0))
            link(ms(state[:], 0.0))
            pool.nop().then_inc(consts, 1)
            pool.wait_ge(att_max, att_stage["nsa"][1])
            link(ms(keep[:], 1.0))
            link(ms(keep[:, 0:S:CH], 0.0))
            pool.nop().then_inc(consts, 1)
            for c in range(NCH):
                pool.wait_ge(rc_v, RC_V.at("mask", c))
                if c:
                    pool.wait_ge(rc_t, RC_T.at("y5", c - 1))
                for l in range(6):
                    if l == NALT:
                        pool.wait_ge(rc_v, RC_V.at("t0", c))
                    if l >= NALT:
                        pool.wait_ge(rc_t, RC_T.at(("eye", "y1", "y2")[l - NALT], c))
                    nc.gpsimd.tensor_tensor(ALT[:, l % NALT, :].rearrange("p (j n) -> p j n", j=JP), GA[:, :, 0:HD],
                                            level[:, l:l + 1, :].broadcast_to([P, JP, HD]), ALU.mult).then_inc(rc_p, 1)
            pool.wait_ge(rc_p, 6 * NCH)
            fill(triu_s, 1.0, ([[1, P]], -1, -1, 0.0))
            fill(ntril, -1.0, ([[-1, P]], 0, 1, 0.0))
            fill(hide_gt, 0.0, ([[1, P]], 0, -1, NEG))
            fill(hide_ge, 0.0, ([[1, P]], -1, -1, NEG))
            pool.nop().then_inc(consts, 1)

        @block.tensor
        def _(pe):
            mm = nc.tensor.matmul
            seen = set()

            def opened(t):
                if t.n >= NBANK:
                    read_out(pe, [tiles[t.n - NBANK]])

            def arrived(w):
                if w["n"] not in seen:
                    seen.add(w["n"])
                    if "m" in w:
                        pe.wait_ge(split_lo, w["m"] + 1)
                    else:
                        pe.wait_ge(landed[w["slot"]], w["level"])

            def products(t, sums, nm=None):
                opened(t)
                for v, prods in sums:
                    for i, p in enumerate(prods):
                        if p[2] is not None:
                            arrived(p[2])
                        if nm is not None and (nm["j"], p[3]) not in seen:
                            seen.add((nm["j"], p[3]))
                            pe.wait_ge(normed, nm["c"] + p[3] + 1)
                        last = mm(v, p[0], p[1], start=(i == 0), stop=(i == len(prods) - 1))
                last.then_inc(acc_full, 1)

            def turned(t, views):
                opened(t)
                for v, src in views:
                    last = nc.tensor.transpose(v, src, ident[0:src.shape[0], 0:src.shape[0]])
                last.then_inc(acc_full, 1)

            def norm_sum(nm, ks=None):
                for k in (range(nm["k"]) if ks is None else ks):
                    pe.wait_ge(squared, nm["b"] + k + 1)
                    mm(bank[4][:, 0:nm["n"]], ones[:], ntmp[:, k % 2, 0:nm["n"]], start=(k == 0),
                       stop=(k == nm["k"] - 1)).then_inc(norm_part, 1)

            def gemm(jobs, nm=None, then=None):
                for n, j in enumerate(jobs):
                    products(j[0], j[1], nm)
                    if then is not None and n:
                        norm_sum(then, [n - 1])
                if then is not None:
                    norm_sum(then, [len(jobs) - 1])

            def split_sum(halves, h0, then):
                for hf, ts, ps, h in halves:
                    for t in ts:
                        opened(t)
                    for w, k0, kk in ps:
                        arrived(w)
                        if hf == 0:
                            pe.wait_ge(hid_lo, h0 + k0 + kk)
                        for c, t in enumerate(ts):
                            for k in range(kk):
                                for i, (a_, b_) in enumerate((("hi", 0), ("hi", 1), ("lo", 0))):
                                    last = mm(bank[t.bank][:], w[a_][:, k, c * P:c * P + P], h[b_][:, k0 + k, :],
                                              start=(k0 + k == 0 and i == 0), stop=(w is ps[-1][0] and k == kk - 1 and i == 2))
                            if w is ps[-1][0]:
                                last.then_inc(acc_full, 1)
                        if w is not ps[-1][0]:
                            last.then_inc(panel_read, 1)
                        if hf == 1 and w is ps[0][0]:
                            norm_sum(then, range(4))
                norm_sum(then, range(4, 8))

            def attention(name):
                g0, g1 = att_stage[name]

                def scores(g):
                    n = g["n"]
                    if n >= 2:
                        pe.wait_ge(att_exp, n - 1)
                    for w, u in enumerate(g["units"]):
                        last = mm(g["s"][w][:, 0:g["N"]], u["q"], u["k"], start=True, stop=True)
                    last.then_inc(att_scores, 1)

                def turn(g):
                    n = g["n"]
                    pe.wait_ge(att_weight, n + 1)
                    if n:
                        pe.wait_ge(att_copied, n)
                    for w in range(2):
                        for t in range(g["N"] // P):
                            last = nc.tensor.transpose(bank[4 + w][:, t * P:t * P + P], g["P"][w][:, t * P:t * P + P], ident[:])
                    last.then_inc(att_turned, 1)

                def values(g):
                    n = g["n"]
                    pe.wait_ge(att_copied, n + 1)
                    if g["ob"] and g["out0"] >= 2:
                        pe.wait_ge(att_out, g["out0"] - 1)
                    more = dict(skip_group_check=True)
                    if g["first"] is not None:
                        mm(*g["first"], start=True, stop=False, **more)
                    for w, u in enumerate(g["units"]):
                        for t, v in enumerate(u["v"]):
                            last = mm(u["o"], v, g["PT"][w][:, t * P:t * P + P], start=(u["start"] and t == 0),
                                      stop=(t == len(u["v"]) - 1), **more)
                    last.then_inc(att_pv, 1)

                for i in range(g0, g1 + 3):
                    if i < g1:
                        scores(groups[i])
                    if i - 3 >= g0:
                        values(groups[i - 3])
                    if g0 <= i - 2 < g1:
                        turn(groups[i - 2])

            pe.wait_ge(consts, 1)
            pe.wait_ge(vec_in, 16 * len(vec_dmas))
            vb = bank[vec_tile.bank]
            turned(vec_tile, [(vb[:, 0:P], rows[:, 0, :]), (vb[:, P:2 * P], rows[:, 1, :]),
                              (vb[0:HD, POS:POS + 64], rows[0:64, 2, 0:HD])])
            arrived(x_panels[0])
            arrived(x_panels[1])
            for k, t in enumerate(x_tiles):
                turned(t, [(bank[t.bank][:, tt * P:tt * P + P], x_panels[tt // 2]["v"][:, tt % 2, k * P:k * P + P]) for tt in range(TT)])
            arrived(mem_panel)
            for k, t in enumerate(mem_tiles):
                turned(t, [(bank[t.bank][:, (2 * kk + tt) * P:(2 * kk + tt) * P + P],
                            mem_panel["v"][:, tt, (2 * k + kk) * P:(2 * k + kk) * P + P]) for kk in range(2) for tt in range(2)])
            for l in range(2):
                norm_sum(mem_norm[l])
                gemm(mem_jobs[l], mem_norm[l])
            norm_sum(n1a)
            gemm(nsa_jobs, n1a)
            gemm([gate_job])
            if upto == "nsa":
                return
            read_out(pe, jobs_of(nsa_jobs))
            pe.wait_ge(cols_ready, 1)
            for j in range(2):
                ws, t, src = cmp_panels[2 * j:2 * j + 2], cmp_hid[j], (kcT, vcT)[j]
                opened(t)
                arrived(ws[0])
                arrived(ws[1])
                if j:
                    read_out(pe, cmp_hid[0:1])
                for b in range(2):
                    hv = (bank[t.bank], bank[6])[b][:, 0:2 * NCMP].rearrange("p (c n) -> p c n", c=2)
                    s_ = slice(b * HD, b * HD + HD)
                    for l in range(CB):
                        mm(hv, ws[l // 16]["v"][s_, l % 16, :], src[s_, :, l:l + CS * (NCMP - 1) + 1:CS],
                           start=(l == 0), stop=(l == CB - 1))
                for l in range(CB):
                    last = mm(bank[t.bank][:, 200:201], ws[l // 16]["v"][0:HD, l % 16, :],
                              cols[0:HD, POS + j * CB + l:POS + j * CB + l + 1], start=(l == 0), stop=(l == CB - 1))
                last.then_inc(acc_full, 1)
            for j in range(2):
                t = cmp_res[j]
                opened(t)
                pe.wait_ge(gelu_out, j + 1)
                hv = chid[:, j, :].rearrange("p (b c n) -> p b c n", b=2, c=2)
                if j == 0:
                    for b in range(2):
                        last = mm(bank[t.bank][b * HD:b * HD + HD, 0:2 * NCMP].rearrange("p (c n) -> p c n", c=2),
                                  cmp_w2[:, 0, :], hv[:, b], start=True, stop=True)
                else:
                    for g in range(G1):
                        last = mm(bank[t.bank][0:NCMP, g * HD:g * HD + HD], hv[:, g % 2, g // 2, :], cmp_w2[:, 1, :],
                                  start=True, stop=True)
                last.then_inc(acc_full, 1)
            read_out(pe, cmp_res)
            pe.wait_ge(consts, 2)
            for i in range(TT):
                for e in range(2):
                    for x, h in enumerate(cmp_heads[e]):
                        hs = slice(e * HD, e * HD + HD)
                        last = mm(bank[2 * i + e][:, x * NCMP:x * NCMP + NCMP], qT[hs, pair(h), i * P:i * P + P],
                                  kcb[hs, h // 6, :], start=True, stop=True)
            last.then_inc(cmp_s, 1)
            pe.wait_ge(cmp_w, 1)
            for x in range(H1):
                if x >= 8:
                    pe.wait_ge((cmp_pt, cmp_ptv)[x % 2], (x - 8) // 2 + 1)
                for i in range(TT):
                    last = nc.tensor.transpose(bank[x % 8][0:NCMP, i * P:i * P + P], CU[:, i * H1 + x, :], ident[:])
                last.then_inc(cmp_t, 1)
            pe.wait_ge(cmp_pt, 6)
            pe.wait_ge(cmp_ptv, 6)
            attention("nsa")
            pe.wait_ge(att_out, groups[att_stage["nsa"][1] - 1]["out0"] + 1)
            gemm(wo_jobs[0], then=ffn[0][0])

            def swiglu_pe(f):
                nm, jobs, halves, h0, then = f
                for g_, u_, j in jobs:
                    products(g_[0], g_[1], nm)
                    products(u_[0], u_[1])
                split_sum(halves, h0, then)

            if upto == "wo0":
                return
            swiglu_pe(ffn[0])
            if upto == "l0":
                return
            gemm(shift_jobs, n1b)
            gemm(qm1_jobs)
            read_out(pe, jobs_of(qm1_jobs))
            read_out(pe, jobs_of(shift_jobs[-4:]))
            attention("mem1")
            arrived(lora_panels[0])
            arrived(lora_panels[1])
            pe.wait_ge(lora_in, 2)
            for j in range(JP):
                t = rp_tiles[j]
                s_ = slice(j * P, j * P + P)
                b_ = lambda n: bank[t[n].bank][:]
                products(t["w"], [(b_("w"), [(lw[0:64, s_], lo[0:64, :], None)])])
                products(t["a"], [(b_("a"), [(lw[64:128, s_], lo[64:128, :], None)])])
                products(t["g"], [(b_("g"), [(lw[:, MIX + j * P:MIX + j * P + P], lo2, None),
                                             (lw2[0:32, j * P:j * P + P], lo3[0:32, :], None)])])
                pe.wait_ge(rp_a, 3 * j + 2)
                products(t["n"], [(b_("n"), [(blockones[:], tmp[3], None)])])
                pe.wait_ge(rp_v, 4 * j + 3)
                products(t["b"], [(b_("b"), [(blockones[:], tmp[4], None)])])
            if upto == "rp":
                return
            pe.wait_ge(rp_v, 4 * JP)
            halves2 = [slice(0, HD), slice(HD, P)]

            def small_mm(out_bank, lf, rf, first=True, final=True):
                for j in range(JP):
                    for hs in halves2:
                        last = mm(out_bank[hs, j * HD:j * HD + HD], lf(hs, j), rf(hs, j), start=first, stop=final)
                return last

            AR = arena[:, 0:24 * S].rearrange("p (w j t) -> p w j t", w=4, j=6)
            for c in range(NCH):
                cs = slice(c * CH, c * CH + CH)
                if c:
                    pe.wait_ge(rc_v, RC_V.at("s", c - 1))
                for w_, src in ((0, bT), (2, kT7)):
                    for j in range(JP):
                        for hs in halves2:
                            o = bank[w_ + j // 3][hs, (j % 3) * P:(j % 3) * P + P]
                            mm(o[:, 0:HD], src[hs, j, cs], AR[hs, 3, j, cs], start=True, stop=True)
                            last = mm(o[:, HD:P], src[hs, j, cs], AR[hs, 0, j, cs], start=True, stop=True)
                last.then_inc(rc_t, 1)
                for n, src in enumerate((bT, kT7, vT7)):
                    last = small_mm(bank[4 + n], lambda hs, j: src[hs, j, cs], lambda hs, j: ident[hs, hs])
                last.then_inc(rc_t, 1)
                Al = lambda l: (lambda hs, j: ALT[hs, l % NALT, j * HD:j * HD + HD])
                pe.wait_ge(rc_p, 6 * c + 1)
                small_mm(bank[7], Al(0), lambda hs, j: eye2[hs, :]).then_inc(rc_t, 1)
                cur, nxt = (Tm, TTm), (Tn, TTn)
                for l in range(1, 6):
                    pe.wait_ge(rc_p, 6 * c + l + 1)
                    pe.wait_ge(rc_v, RC_V.at(f"t{l - 1}", c))
                    small_mm(bank[0], Al(l), lambda hs, j: Tm[hs, j, :]).then_inc(rc_t, 1)
                    pe.wait_ge(rc_a, RC_A.at(f"y{l}", c))
                    if l < 5:
                        small_mm(bank[1], lambda hs, j: TTm[hs, j, :], lambda hs, j: Ym[hs, j, :])
                    small_mm(bank[2], lambda hs, j: Ym[hs, j, :], lambda hs, j: TTm[hs, j, :]).then_inc(rc_t, 1)
                pe.wait_ge(rc_a, RC_A.at("tok", c))
                for j in range(JP):
                    for hs in halves2:
                        o = bank[3][hs, j * HD:j * HD + HD]
                        mm(o, GK[hs, j, 0:HD], VT[hs, j, :], start=True, stop=False)
                        last = mm(o, kkT[hs, j, cs], state[hs, j, :], start=False, stop=True)
                last.then_inc(rc_t, 1)
                pe.wait_ge(rc_v, RC_V.at("x", c))
                small_mm(bank[4], lambda hs, j: TTm[hs, j, :], lambda hs, j: Xm[hs, j, :]).then_inc(rc_t, 1)
                pe.wait_ge(rc_a, RC_A.at("u", c))
                for j in range(JP):
                    for hs in halves2:
                        o = bank[5][hs, j * HD:j * HD + HD]
                        mm(o, state[hs, j, :], rT[hs, j, cs], start=True, stop=False)
                        mm(o, VT[hs, j, :], GK[hs, j, HD:P], start=False, stop=False)
                        last = mm(o, Um[hs, j, :], GA[hs, j, HD:P], start=False, stop=True)
                last.then_inc(rc_t, 1)
                for j in range(JP):
                    for hs in halves2:
                        o = bank[6][hs, j * HD:j * HD + HD]
                        mm(o, KT[hs, j, :], VT[hs, j, :], start=True, stop=False)
                        last = mm(o, BT[hs, j, :], Um[hs, j, :], start=False, stop=True)
                last.then_inc(rc_t, 1)
            pe.wait_ge(rc_v, RC_V.at("y", NCH - 1))
            for j in range(JP):
                t0, t1 = gn_tiles[j]
                if j == 0:
                    pe.wait_ge(rc_v, RC_V.at("s", NCH - 1))
                products(t0, [(bank[t0.bank][:], [(blockones[:], rT[:, j, :], None)])])
                pe.wait_ge(gn_a, 3 * j + 2)
                products(t1, [(bank[t1.bank][:], [(blockones[:], tmp[1], None)])])
            pe.wait_ge(gn_v, 3 * JP)
            pe.wait_ge(att_out, groups[att_stage["mem1"][1] - 1]["out0"] + 1)
            if upto == "gn":
                return
            gemm(wo_jobs[1], then=ffn[1][0])
            swiglu_pe(ffn[1])
            arrived(mem2_panel)
            for k, t in enumerate(mem2_tiles):
                turned(t, [(bank[t.bank][:, (2 * kk + tt) * P:(2 * kk + tt) * P + P],
                            mem2_panel["v"][:, tt, (2 * k + kk) * P:(2 * k + kk) * P + P]) for kk in range(2) for tt in range(2)])
            norm_sum(mem2_norm)
            gemm(mem2_jobs, mem2_norm)
            norm_sum(n2a)
            if upto == "b1":
                return
            gemm(z_jobs, n2a)
            gemm(conv_jobs)
            gemm([dt_job])
            gemm(qkv_jobs)
            pe.wait_ge(conv_a, 12)
            for c, t in enumerate(xd_tiles):
                turned(t, [(bank[t.bank][:, k * P:k * P + P], xbc[:, k, c * P:c * P + P]) for k in range(4)])
            turned(bt_tile, [(bank[bt_tile.bank][:, c * P:c * P + P], xbc[:, 4, c * P:c * P + P]) for c in range(4)])
            pe.wait_ge(sd_v, 1)
            opened(ac_tile)
            mm(bank[ac_tile.bank][:, 0:32], triu[:], small[:, 1, :], start=True, stop=True)
            mm(bank[ac_tile.bank][:, 32:64], ones[:], small[:, 1, :], start=True, stop=True).then_inc(acc_full, 1)
            read_out(pe, xd_tiles + [bt_tile])
            pe.wait_ge(sd_v, 2)
            read_out(pe, [ac_tile])
            for c in range(TT):
                cs = slice(c * P, c * P + P)
                if c:
                    pe.wait_ge(sc_v, SC_V.at("st", c - 1))
                for h in range(SH):
                    mm(bank[4 + h // 4][:, (h % 4) * P:(h % 4) * P + P],
                       small[:, 1, c * 8 + h:c * 8 + h + 1].broadcast_to([P, P]), triu[:], start=True, stop=True)
                for g in range(SG):
                    gs = slice(g * HD, g * HD + HD)
                    last = mm(bank[(6, 2)[g]][:, 0:P], xbc[gs, 4, cs], xbc[gs, 5, cs], start=True, stop=True)
                last.then_inc(sc_t, 1)
                pe.wait_ge(sc_v, SC_V.at("ct", c))
                for h in range(SH):
                    g = h // 4
                    gs = slice(g * HD, g * HD + HD)
                    o = bank[(7, 1)[g]][(h % 2) * HD:(h % 2) * HD + HD, (h // 2 % 2) * P:(h // 2 % 2) * P + P]
                    last = mm(o, XD[:, c, h * HD:h * HD + HD], MM_[g][:, (h % 4) * P:(h % 4) * P + P], start=True, stop=(c == 0))
                    if c:
                        last = mm(o, SST[gs, h % 4, :], CT[gs, (h % 4) * P:(h % 4) * P + P], start=False, stop=True)
                last.then_inc(sc_t, 1)
                for g in range(SG):
                    last = mm(bank[3][g * HD:g * HD + HD, 0:256], Btok[:, c * P + g * HD:c * P + g * HD + HD],
                              XDD[:, g * 256:g * 256 + 256], start=True, stop=True)
                last.then_inc(sc_t, 1)
            pe.wait_ge(sc_v, SC_V.at("st", TT - 1))
            norm_sum(nssd)
            read_out(pe, jobs_of(qkv_jobs))
            nu = 4 * SH
            pe.wait_ge(consts, 4)
            pe.wait_ge(rooted, nssd["j"] + 1)

            def logits(u):
                h, js = u // 4, 3 - u % 4
                hs = slice((h % 2) * HD, (h % 2) * HD + HD)
                if u >= 2:
                    pe.wait_ge(sb_a, 3 * (u - 2) + 3)
                mm(bank[4 + u % 2][:, js * P:S], k2[hs, h // 2, js * P:js * P + P], q2[hs, h // 2, js * P:S],
                   start=True, stop=True).then_inc(sb_t, 1)

            def later(u):
                h, js = u // 4, 3 - u % 4
                b_ = bank[4 + u % 2]
                pe.wait_ge(sb_v, 2 * u + 2)
                more = dict(start=False, stop=False, skip_group_check=True)
                mm(b_[:, js * P:js * P + P], ident[:], hide_ge, **more)
                for jj in range(js + 1, 4):
                    mm(b_[:, jj * P:S], nones[:], SP[:, jj, jj * P:S], **more)
                more["stop"] = True
                mm(b_[:, js * P:S], ntril, SP[:, js, js * P:S], **more).then_inc(sb_t, 1)

            def sb_values(h):
                pe.wait_ge(sb_a, 3 * (4 * h + 3) + 3)
                if h >= 2 and h % 2 == 0:
                    pe.wait_ge(sb_out, h // 2)
                for js in range(4):
                    last = mm(bank[7][(h % 2) * HD:(h % 2) * HD + HD, js * P:S], v2[:, js, h * HD:h * HD + HD],
                              WT[:, js, js * P:S], start=(js == 0), stop=(js == 3))
                last.then_inc(sb_pv, 1)

            logits(0)
            for u in range(nu):
                if u + 1 < nu:
                    logits(u + 1)
                later(u)
                if u % 4 == 3:
                    sb_values(u // 4)
            norm_sum(nsb)
            if upto == "sb":
                return
            pe.wait_ge(normed, nsb["c"] + 4)
            gemm(wout_jobs, then=n2b)
            gemm(xq_jobs, n2b)
            read_out(pe, jobs_of(xq_jobs))
            attention("xa")
            pe.wait_ge(att_out, nout[0])
            gemm(wxo_jobs, then=n2c)
            gemm(ff1_jobs, n2c)
            split_sum(ff2_halves, 2 * FT, n2f)
            pe.wait_ge(scaled, n2f["b"] + KC)
            for i, t in enumerate(out_tiles):
                tt, kh = divmod(i, 2)
                turned(t, [(bank[t.bank][:, k * P:k * P + P], yT[:, kh * 4 + k, tt * P:tt * P + P]) for k in range(4)])

        @block.scalar
        def _(act):
            A = nc.scalar.activation
            link = chained(act, chain_a)
            act.wait_ge(consts, 1)
            for dst, src in vec_dmas:
                act.dma_start(dst, src).then_inc(vec_in, 16)

            at = [0]

            def split_to(m):
                while at[0] <= m:
                    w = splits[at[0]]
                    act.wait_ge(landed[w["slot"]], w["level"])
                    if at[0] >= NSPLIT:
                        act.wait_ge(*splits[at[0] - NSPLIT]["read"])
                    A(w_hi[:, at[0] % NSPLIT, 0:w["size"]], wring[:, w["slot"], 0:w["size"]], ACT.Copy).then_inc(split_hi, 1)
                    at[0] += 1

            def tile_in(t):
                if t.split is not None:
                    split_to(splits_until(t.split + AHEAD, t.split))
                act.wait_ge(acc_full, t.n + 1)

            def copy_out(t, dst, v, scale=1.0):
                tile_in(t)
                A(dst, v, ACT.Copy if isinstance(scale, float) else ACT.Identity, scale=scale).then_inc(evac_a, 1)

            def norm_root(nm, ready=None):
                n = nm["n"]
                if nm["c"]:
                    act.wait_ge(normed, nm["c"])
                for k in range(nm["k"]):
                    if ready is not None:
                        ready(k)
                    if k >= 2:
                        act.wait_ge(norm_part, nm["b"] + k - 1)
                    A(ntmp[:, k % 2, 0:n], nm["src"][:, k, 0:n], ACT.Square).then_inc(squared, 1)
                act.wait_ge(norm_part, nm["b"] + nm["k"])
                if nm["b"]:
                    act.wait_ge(scaled, nm["b"])
                link(A(rsb[:, 0:n], bank[4][:, 0:n], ACT.Ln, scale=1.0 / (nm["k"] * P), bias=eps[:, nm["eps"]:nm["eps"] + 1]))
                A(rsb[:, 0:n], rsb[:, 0:n], ACT.Exp, scale=-0.5).then_inc(rooted, 1)
                if isinstance(nm["dst"], tuple):
                    for k in range(nm["k"]):
                        act.wait_ge(scaled, nm["b"] + k + 1)
                        A(nm["dst"][0][:, k, 0:n], ntmp[:, k % 2, 0:n], ACT.Copy).then_inc(cast, 1)

            def added(jobs):
                def ready(k):
                    t = jobs[k][0]
                    split_to(splits_until(t.split + AHEAD, t.split))
                    act.wait_ge(evac_v, t.order + 1)
                return ready

            def added_split(halves):
                def ready(k):
                    if k % 4 == 0:
                        for w, _, _ in halves[k // 4][2]:
                            split_to(splits_until(w["m"] + AHEAD, w["m"]))
                    act.wait_ge(evac_v, halves[k // 4][1][k % 4].order + 1)
                return ready

            def plain(jobs):
                for t, _, dst, v, sc in jobs:
                    split_to(splits_until(t.split + AHEAD, t.split))
                    if t.eng == "a":
                        copy_out(t, dst, v, sc)

            def attention(name):
                g0, g1 = att_stage[name]

                def probs(g):
                    n = g["n"]
                    if n >= 3:
                        act.wait_ge(att_turned, n - 2)
                    act.wait_ge(att_max, n + 1)
                    for w in range(2):
                        last = A(g["P"][w][:, 0:g["N"]], g["s"][w][:, 0:g["N"]], ACT.Exp, scale=g["slope"],
                                 bias=g["st"][:, 1, w:w + 1], accum_out=g["st"][:, 2, w:w + 1])
                    last.then_inc(att_exp, 1)

                def copy(g):
                    n = g["n"]
                    act.wait_ge(att_turned, n + 1)
                    if n >= 2:
                        act.wait_ge(att_pv, n - 1)
                    for w in range(2):
                        last = A(g["PT"][w][:, 0:g["N"]], bank[4 + w][:, 0:g["N"]], ACT.Copy)
                    last.then_inc(att_copied, 1)

                def output(g):
                    if g["evac"] is not None:
                        act.wait_ge(att_pv, g["n"] + 1)
                        A(h_hi[:, g["evac"][1], :], g["evac"][0][:], ACT.Copy).then_inc(att_hi, 1)

                for i in range(g0, g1 + 3):
                    if i < g1:
                        probs(groups[i])
                    if g0 <= i - 2 < g1:
                        copy(groups[i - 2])
                    if i - 3 >= g0:
                        output(groups[i - 3])

            for k, t in enumerate(x_tiles):
                if t.eng == "a":
                    copy_out(t, xT[:, k, :], bank[t.bank][:])
            for k, t in enumerate(mem_tiles):
                if t.eng == "a":
                    copy_out(t, memT[:, 2 * k:2 * k + 2, :], bank[t.bank][:].rearrange("p (k m) -> p k m", k=2))
            read_out(act, mem_tiles + x_tiles)
            split_to(splits_until(AHEAD, 0))
            for l in range(2):
                if l:
                    read_out(act, jobs_of(mem_jobs[0]))
                norm_root(mem_norm[l])
                plain(mem_jobs[l])
            norm_root(n1a)
            plain(nsa_jobs)
            split_to(gate_job[0].split)
            act.wait_ge(gate_exp_in, 1)
            A(gates[:], gates[:], ACT.Exp, scale=-1.0).then_inc(gate_exp, 1)
            if upto == "nsa":
                return
            for j in range(2):
                act.wait_ge(gelu_in, j + 1)
                A(ctmp[:], ctmp[:], ACT.Exp, scale=-2.0 * math.sqrt(2.0 / math.pi)).then_inc(gelu_exp, 1)
            act.wait_ge(cmp_u, 1)
            A(CU[:], CU[:], ACT.Exp).then_inc(cmp_e, 1)
            for x in range(0, H1, 2):
                act.wait_ge(cmp_t, x + 1)
                A(PTc[0:NCMP, cmp_head(x), :], bank[x % 8][0:NCMP, :], ACT.Copy).then_inc(cmp_pt, 1)
            m = wo_jobs[0][0][0].split
            split_to(splits_until(m + AHEAD, m))
            attention("nsa")

            def hidden(j, h0, tile_):
                act.wait_ge(evac_v, tile_.order + 1)
                A(hid[0][:, j, :], hraw[1][:, j % 2, :], ACT.Copy).then_inc(hid_hi, 1)

            def swiglu_act(f, jw):
                nm, jobs, halves, h0, then = f
                norm_root(nm, added(jw))
                for g_, u_, j in jobs:
                    tile_in(g_[0])
                    if j >= 2:
                        act.wait_ge(evac_v, jobs[j - 2][1][0].order + 1)
                    A(hraw[0][:, j % 2, :], g_[2], ACT.Silu).then_inc(evac_a, 1)
                    if j:
                        hidden(j - 1, h0, jobs[j - 1][1][0])
                hidden(FT - 1, h0, jobs[FT - 1][1][0])
                norm_root(then, added_split(halves))

            if upto == "wo0":
                return
            swiglu_act(ffn[0], wo_jobs[0])
            if upto == "l0":
                return
            for t, _, dst, v, j, m in shift_jobs:
                tile_in(t)
                A(dst, v, ACT.Identity, scale=omu[0:m, j:j + 1]).then_inc(shifted, 1)
            act.wait_ge(evac_v, shift_jobs[-1][0].order + 1)
            plain(qm1_jobs)
            A(lo[0:64, :], lo[0:64, :], ACT.Tanh).then_inc(lora_in, 1)
            A(lo2, lo2, ACT.Exp, scale=-1.0)
            A(lo3[0:32, :], lo3[0:32, :], ACT.Exp, scale=-1.0).then_inc(lora_pre, 1)
            attention("mem1")
            S0 = -DECAY
            for j in range(JP):
                t = rp_tiles[j]
                tile_in(t["w"])
                if j:
                    act.wait_ge(rp_v, 4 * j)
                A(tmp[0], bank[t["w"].bank][:], ACT.Exp, scale=-1.0, bias=ncols[:, j:j + 1]).then_inc(evac_a, 1)
                tile_in(t["a"])
                A(tmp[1], bank[t["a"].bank][:], ACT.Exp, scale=-1.0, bias=ncols[:, 6 + j:7 + j]).then_inc(evac_a, 1)
                copy_out(t["g"], gT[:, j, :], bank[t["g"].bank][:])
                A(tmp[3], kT7[:, j, :], ACT.Square, scale=col("rw_k_k", j)).then_inc(rp_a, 1)
                act.wait_ge(rp_a, 3 * j + 1)
                act.nop().then_inc(rp_a, 1)
                act.wait_ge(rp_v, 4 * j + 1)
                link(A(tmp[2], tmp[2], ACT.Ln))
                A(tmp[2], tmp[2], ACT.Exp, scale=-0.5).then_inc(rp_a, 1)
                act.wait_ge(rp_v, 4 * j + 3)
                act.wait_ge(acc_full, t["b"].n + 1)
                A(tmp[4], tmp[5], ACT.Exp, scale=-S0)
                A(tmp[5], tmp[5], ACT.Exp, scale=S0)
                A(tmp[3], tmp[0], ACT.Exp, scale=S0).then_inc(rp_p, 1)
            if upto == "rp":
                return
            m = wo_jobs[1][0][0].split
            split_to(splits_until(m + AHEAD, m))
            for c in range(NCH):
                act.wait_ge(rc_t, RC_T.at("tok", c))
                for n, dst in enumerate((BT, KT, VT)):
                    last = A(dst, bank[4 + n][:, 0:384].rearrange("p (j n) -> p j n", j=JP), ACT.Copy)
                last.then_inc(rc_a, 1)
                for l in range(1, 6):
                    act.wait_ge(rc_t, RC_T.at(f"y{l}", c))
                    A(Ym, bank[0][:, 0:384].rearrange("p (j n) -> p j n", j=JP), ACT.Copy).then_inc(rc_a, 1)
                act.wait_ge(rc_t, RC_T.at("u", c))
                A(Um, bank[4][:, 0:384].rearrange("p (j n) -> p j n", j=JP), ACT.Copy).then_inc(rc_a, 1)
            for j in range(JP):
                t0, t1 = gn_tiles[j]
                tile_in(t0)
                if j:
                    act.wait_ge(gn_v, 3 * j)
                A(tmp[0], bank[t0.bank][:], ACT.Copy, scale=-1.0 / HD).then_inc(evac_a, 1)
                act.nop().then_inc(gn_a, 1)
                act.wait_ge(gn_v, 3 * j + 1)
                A(tmp[1], rT[:, j, :], ACT.Square).then_inc(gn_a, 1)
                tile_in(t1)
                A(tmp[2], bank[t1.bank][:], ACT.Ln, scale=1.0 / HD, bias=eps[:, 2:3]).then_inc(evac_a, 1)
                act.wait_ge(evac_a, t1.order + 1)
                A(tmp[2], tmp[2], ACT.Exp, scale=-0.5).then_inc(gn_a, 1)
                act.wait_ge(gn_v, 3 * j + 2)
                A(h_hi[:, j, :], rT[:, j, :], ACT.Copy).then_inc(mix_hi, 1)
            if upto == "gn":
                return
            swiglu_act(ffn[1], wo_jobs[1])
            for k, t in enumerate(mem2_tiles):
                if t.eng == "a":
                    copy_out(t, memT2[:, 2 * k:2 * k + 2, :], bank[t.bank][:].rearrange("p (k m) -> p k m", k=2))
            m = mem2_jobs[0][0].split
            split_to(splits_until(m + AHEAD, m))
            read_out(act, mem2_tiles)
            norm_root(mem2_norm)
            plain(mem2_jobs)
            norm_root(n2a)
            if upto == "b1":
                return
            for t, _, dst, v in z_jobs:
                tile_in(t)
                A(dst, v, ACT.Silu).then_inc(evac_a, 1)
            for t, _, dst, v, c in conv_jobs:
                tile_in(t)
                A(dst, v, ACT.Identity, scale=col("conv_w_2", 18 + c), bias=col("conv_b_2", c)).then_inc(conv_a, 1)
            act.wait_ge(conv_v, 6)
            for c in range(6):
                A(xbc[:, c, :], xbc[:, c, :], ACT.Silu).then_inc(conv_a, 1)
            plain(qkv_jobs)
            A(bcast[:, 44:52], bcast[:, 44:52], ACT.Exp)
            act.wait_ge(gates_ready, 2)
            link(A(small[:, 2, :], small[:, 2, :], ACT.Exp))
            A(small[:, 2, :], small[:, 2, :], ACT.Ln, bias=eps[:, 3:4]).then_inc(sd_a, 1)
            copy_out(bt_tile, Btok, bank[bt_tile.bank][:])
            act.wait_ge(sd_v, 2)
            A(small[:, 3:5, :], small[:, 3:5, :], ACT.Exp).then_inc(sd_a, 1)
            for c in range(TT):
                act.wait_ge(sc_t, SC_T.at("row", c))
                if c:
                    act.wait_ge(sc_v, SC_V.at("ct", c - 1))
                for g in range(2):
                    last = A(ER[g], bank[4 + g][:], ACT.Exp)
                last.then_inc(sc_a, 1)
                act.wait_ge(sc_v, SC_V.at("seg", c))
                for h in range(SH):
                    v = SEG[h // 4][:, (h % 4) * P:(h % 4) * P + P]
                    last = A(v, v, ACT.Exp, bias=small[:, 5, c * 8 + h:c * 8 + h + 1])
                last.then_inc(sc_a, 1)
            act.wait_ge(sd_v, 3)
            norm_root(nssd)
            for u in range(4 * SH):
                js = 3 - u % 4
                v = T1[u % 2][:, js * P:S]
                act.wait_ge(sb_v, 2 * u + 1)
                A(v, v, ACT.Exp).then_inc(sb_a, 1)
                act.wait_ge(sb_a, 3 * u + 1)
                A(v, v, ACT.Ln, bias=eps[:, 3:4]).then_inc(sb_a, 1)
                act.wait_ge(sb_t, 2 * u + 3 if u + 1 < 4 * SH else 2 * u + 2)
                if u >= 4:
                    act.wait_ge(sb_pv, u // 4)
                A(WT[:, js, js * P:S], bank[4 + u % 2][:, js * P:S], ACT.Exp).then_inc(sb_a, 1)
            act.wait_ge(sb_out, SH // 2)
            norm_root(nsb)
            norm_root(n2b, added(wout_jobs))
            plain(xq_jobs)
            attention("xa")
            norm_root(n2c, added(wxo_jobs))
            for t, _, j, v in ff1_jobs:
                tile_in(t)
                if j >= 2:
                    act.wait_ge(evac_v, ff1_jobs[j - 2][0].order + 1)
                A(hraw[0][:, j % 2, :], v, ACT.Relu, scale=FF_SCALE).then_inc(shifted, 1)
                if j:
                    hidden(j - 1, 2 * FT, ff1_jobs[j - 1][0])
            hidden(FFT - 1, 2 * FT, ff1_jobs[-1][0])
            norm_root(n2f, added_split(ff2_halves))
            for i, t in enumerate(out_tiles):
                if t.eng == "a":
                    tt, kh = divmod(i, 2)
                    copy_out(t, out_sb[:, tt, kh * 512:kh * 512 + 512], bank[t.bank][:])

        @block.vector
        def _(dve):
            V = nc.vector
            link = chained(dve, chain_v)

            at = [0]

            def split_to(m):
                while at[0] <= m:
                    w = splits[at[0]]
                    sl = at[0] % NSPLIT
                    dve.wait_ge(split_hi, at[0] + 1)
                    V.tensor_tensor(w_lo[:, sl, 0:w["size"]], wring[:, w["slot"], 0:w["size"]], w_hi[:, sl, 0:w["size"]],
                                    ALU.subtract).then_inc(split_lo, 1)
                    at[0] += 1

            def tile_in(t):
                if t.split is not None:
                    split_to(splits_until(t.split + AHEAD, t.split))
                dve.wait_ge(acc_full, t.n + 1)

            def copy_out(t, dst, v, scale=1.0):
                tile_in(t)
                if isinstance(scale, float) and scale == 1.0:
                    V.tensor_copy(dst, v).then_inc(evac_v, 1)
                else:
                    V.tensor_scalar(dst, v, scale, None, ALU.mult).then_inc(evac_v, 1)

            def plain(jobs):
                for t, _, dst, v, sc in jobs:
                    split_to(splits_until(t.split + AHEAD, t.split))
                    if t.eng == "v":
                        copy_out(t, dst, v, sc)

            def norm_apply(nm):
                dve.wait_ge(rooted, nm["j"] + 1)
                n, pair_ = nm["n"], isinstance(nm["dst"], tuple)

                def rest(k):
                    dve.wait_ge(cast, nm["c"] + k + 1)
                    V.tensor_tensor(nm["dst"][1][:, k, 0:n], ntmp[:, k % 2, 0:n], nm["dst"][0][:, k, 0:n],
                                    ALU.subtract).then_inc(normed, 1)

                for k in range(nm["k"]):
                    dst = ntmp[:, k % 2, 0:n] if pair_ else nm["dst"][:, k, 0:n]
                    if pair_ and k >= 2:
                        dve.wait_ge(normed, nm["c"] + k - 1)
                    V.scalar_tensor_tensor(dst, nm["src"][:, k, 0:n], col(nm["gain"][0], nm["gain"][1] + k),
                                           rsb[:, 0:n], ALU.mult, ALU.mult).then_inc(scaled, 1)
                    if pair_ and k:
                        rest(k - 1)
                if pair_:
                    rest(nm["k"] - 1)

            def add_residual(jobs):
                for t, _, k, v in jobs:
                    tile_in(t)
                    V.tensor_tensor(xT[:, k, :], xT[:, k, :], v, ALU.add).then_inc(evac_v, 1)

            def add_split(halves, scale=1.0):
                for hf, ts, ps, h in halves:
                    for w, _, _ in ps:
                        split_to(splits_until(w["m"] + AHEAD, w["m"]))
                    for c, t in enumerate(ts):
                        tile_in(t)
                        x_ = xT[:, 4 * hf + c, :]
                        V.scalar_tensor_tensor(x_, bank[t.bank][:], scale, x_, ALU.mult, ALU.add).then_inc(evac_v, 1)

            def hidden(j, h0):
                dve.wait_ge(hid_hi, h0 + j + 1)
                V.tensor_tensor(hid[1][:, j, :], hraw[1][:, j % 2, :], hid[0][:, j, :], ALU.subtract).then_inc(hid_lo, 1)

            def attention(name):
                g0, g1 = att_stage[name]

                def shape(g):
                    n = g["n"]
                    N = g["N"]
                    dve.wait_ge(att_scores, n + 1)
                    for w, u in enumerate(g["units"]):
                        ins = V.tensor_tensor_reduce(g["s"][w][:, 0:N], g["s"][w][:, 0:N], u["D"], 1.0, -3.0e38,
                                                     ALU.add, ALU.max, g["st"][:, 0, w:w + 1])
                    link(ins)
                    V.tensor_scalar(g["st"][:, 1, :], g["st"][:, 0, :], -g["slope"], None, ALU.mult).then_inc(att_max, 1)

                def weigh(g):
                    st = g["st"]
                    dve.wait_ge(att_exp, g["n"] + 1)
                    link(V.reciprocal(st[:, 3, :], st[:, 2, :]))
                    if g["gates"] is not None:
                        link(V.tensor_tensor(st[:, 3, :], st[:, 3, :], g["gates"], ALU.mult))
                    for w in range(2):
                        p_ = g["P"][w][:, 0:g["N"]]
                        last = V.tensor_scalar(p_, p_, st[:, 3, w:w + 1], None, ALU.mult)
                    last.then_inc(att_weight, 1)

                def output(g):
                    if g["evac"] is not None:
                        dve.wait_ge(att_hi, g["out0"] + 1)
                        b_, c = g["evac"]
                        V.tensor_tensor(h_lo[:, c, :], b_[:], h_hi[:, c, :], ALU.subtract).then_inc(att_out, 1)

                for i in range(g0, g1 + 3):
                    if i < g1:
                        shape(groups[i])
                    if g0 <= i - 1 < g1:
                        weigh(groups[i - 1])
                    if i - 3 >= g0:
                        output(groups[i - 3])

            tile_in(vec_tile)
            vb = bank[vec_tile.bank]
            V.tensor_copy(cols[0:HD, POS:POS + 64], vb[0:HD, POS:POS + 64])
            link(V.tensor_copy(cols[:, 0:256], vb[:, 0:256]))
            for hf in range(2):
                V.tensor_copy(dskip[hf * HD:hf * HD + HD, :], bcast[hf * HD:hf * HD + HD, 52 + hf:60:2])
            V.tensor_scalar(ncols[:, 0:12], cols[:, vec["rw_w0"]:vec["rw_w0"] + 12], -1.0, None, ALU.mult)
            V.tensor_scalar(omu[:, 0:20], cols[:, vec["rw_mu"]:vec["rw_mu"] + 20], -1.0, 1.0, ALU.mult, ALU.add)
            V.tensor_scalar(omu[:, 20:21], MUC(20), -1.0, 1.0, ALU.mult, ALU.add).then_inc(cols_ready, 1)
            dve.nop().then_inc(evac_v, 1)
            for k, t in enumerate(x_tiles):
                if t.eng == "v":
                    copy_out(t, xT[:, k, :], bank[t.bank][:])
            for k, t in enumerate(mem_tiles):
                if t.eng == "v":
                    copy_out(t, memT[:, 2 * k:2 * k + 2, :], bank[t.bank][:].rearrange("p (k m) -> p k m", k=2))
            split_to(splits_until(AHEAD, 0))
            for l in range(2):
                norm_apply(mem_norm[l])
                plain(mem_jobs[l])
            norm_apply(n1a)
            plain(nsa_jobs)
            t, _, v = gate_job
            tile_in(t)
            V.tensor_tensor(gates[:], v, bcast[:, 0:36].unsqueeze(1).broadcast_to([P, TT, 36]), ALU.add).then_inc(evac_v, 1)
            dve.wait_ge(evac_v, t.order + 1)
            dve.nop().then_inc(gate_exp_in, 1)
            dve.wait_ge(gate_exp, 1)
            link(V.tensor_scalar(gates[:], gates[:], 1.0, None, ALU.add))
            link(V.reciprocal(gates[:], gates[:]))
            if upto == "nsa":
                return
            for j in range(2):
                t = cmp_hid[j]
                tile_in(t)
                h_ = chid[:, j, :]
                link(V.tensor_copy(cbias[:], bank[t.bank][:, 200:201]))
                V.tensor_scalar(h_[:, 0:62], bank[t.bank][:, 0:62], cbias[:], None, ALU.add)
                V.tensor_scalar(h_[:, 62:124], bank[6][:, 0:62], cbias[:], None, ALU.add).then_inc(evac_v, 1)
                dve.wait_ge(evac_v, t.order + 1)
                link(V.tensor_tensor(ctmp[:], h_, h_, ALU.mult))
                link(V.tensor_scalar(ctmp[:], ctmp[:], 0.044715, 1.0, ALU.mult, ALU.add))
                link(V.tensor_tensor(ctmp[:], ctmp[:], h_, ALU.mult))
                V.tensor_scalar(ctmp[:], ctmp[:], -50.0, None, ALU.max).then_inc(gelu_in, 1)
                dve.wait_ge(gelu_exp, j + 1)
                link(V.tensor_scalar(ctmp[:], ctmp[:], 1.0, None, ALU.add))
                link(V.reciprocal(ctmp[:], ctmp[:]))
                ins = V.tensor_tensor(h_, h_, ctmp[:], ALU.mult)
                ins.then_inc(gelu_out, 1)
                dve.wait_ge(gelu_out, j + 1)
            copy_out(cmp_res[0], kcb[:], bank[cmp_res[0].bank][:, 0:2 * NCMP].rearrange("p (c n) -> p c n", c=2))
            copy_out(cmp_res[1], vcb[:], bank[cmp_res[1].bank][0:NCMP, 0:KV].rearrange("p (g d) -> p g d", g=G1))
            dve.wait_ge(consts, 2)
            dve.wait_ge(cmp_s, 1)
            c48 = lambda i: cst[:, i, :]
            bc = lambda i: c48(i).unsqueeze(2).broadcast_to([P, 48, NCMP])
            for i in range(TT):
                for e in range(2):
                    x0 = i * H1 + 6 * e
                    last = V.tensor_tensor(CU[:, x0:x0 + 6, :], bank[2 * i + e][:, 0:6 * NCMP].rearrange("p (x n) -> p x n", x=6),
                                           distc[:, i:i + 1, :].broadcast_to([P, 6, NCMP]), ALU.add)
            link(last)
            link(V.tensor_reduce(c48(0), CU[:], AX.X, ALU.max))
            link(V.tensor_scalar(c48(0), c48(0), -1.0e20, None, ALU.max))
            link(V.tensor_tensor(CU[:], CU[:], bc(0), ALU.subtract))
            cu4 = CU.rearrange("p (i x) n -> p i x n", i=TT)
            V.tensor_tensor(cu4, cu4, cslope[:].unsqueeze(1).unsqueeze(3).broadcast_to([P, TT, H1, NCMP]),
                            ALU.mult).then_inc(cmp_u, 1)
            dve.wait_ge(cmp_e, 1)
            link(V.tensor_reduce(c48(1), CU[:], AX.X, ALU.add))
            link(V.tensor_scalar(c48(1), c48(1), 1.0e-30, None, ALU.max))
            link(V.reciprocal(c48(2), c48(1)))
            for e in range(2):
                w4 = c48(2).rearrange("p (i e a r) -> p i e a r", i=TT, e=2, a=2)[:, :, e]
                last = V.tensor_tensor(w4, w4, gates[:, :, 0:H1].rearrange("p i (a e r) -> p i a e r", a=2, e=2)[:, :, :, e], ALU.mult)
            link(last)
            V.tensor_tensor(CU[:], CU[:], bc(2), ALU.mult).then_inc(cmp_w, 1)
            for x in range(1, H1, 2):
                dve.wait_ge(cmp_t, x + 1)
                V.tensor_copy(PTc[0:NCMP, cmp_head(x), :], bank[x % 8][0:NCMP, :]).then_inc(cmp_ptv, 1)
            m = wo_jobs[0][0][0].split
            split_to(splits_until(m + AHEAD, m))
            attention("nsa")
            add_residual(wo_jobs[0])

            def swiglu_dve(f):
                nm, jobs, halves, h0, then = f
                norm_apply(nm)
                for g_, u_, j in jobs:
                    tile_in(u_[0])
                    dve.wait_ge(evac_a, g_[0].order + 1)
                    if j >= 2:
                        dve.wait_ge(hid_lo, h0 + j - 1)
                    V.tensor_tensor(hraw[1][:, j % 2, :], hraw[0][:, j % 2, :], u_[2], ALU.mult).then_inc(evac_v, 1)
                    if j:
                        hidden(j - 1, h0)
                hidden(FT - 1, h0)
                add_split(halves)
                norm_apply(then)

            if upto == "wo0":
                return
            swiglu_dve(ffn[0])
            if upto == "l0":
                return
            for t, _, dst, v, j, m in shift_jobs:
                split_to(splits_until(t.split + AHEAD, t.split))
                dve.wait_ge(shifted, j + 1)
                V.scalar_tensor_tensor(dst[:, 1:S], v[:, 0:S - 1], MUC(j)[0:m], dst[:, 1:S], ALU.mult, ALU.add).then_inc(evac_v, 1)
            dve.wait_ge(lora_pre, 1)
            V.tensor_scalar(lo3[0:32, :], lo3[0:32, :], 1.0, None, ALU.add)
            link(V.tensor_scalar(lo2, lo2, 1.0, None, ALU.add))
            V.reciprocal(lo3[0:32, :], lo3[0:32, :])
            V.reciprocal(lo2, lo2).then_inc(lora_in, 1)
            attention("mem1")
            t0_, t1_, t2_, t3_, t4_, t5_ = tmp
            dve.wait_ge(consts, 3)
            for j in range(JP):
                t = rp_tiles[j]
                tile_in(t["n"])
                V.tensor_scalar(t2_, bank[t["n"].bank][:], 1.0e-24, None, ALU.max).then_inc(evac_v, 1)
                dve.wait_ge(evac_v, t["n"].order + 1)
                dve.nop().then_inc(rp_v, 1)
                dve.wait_ge(evac_a, t["a"].order + 1)
                link(V.tensor_scalar(t1_, t1_, 1.0, None, ALU.add))
                link(V.reciprocal(t1_, t1_))
                link(V.tensor_scalar(kkT[:, j, :], kT7[:, j, :], col("rw_k_k", j), None, ALU.mult))
                dve.wait_ge(rp_a, 3 * j + 3)
                link(V.tensor_tensor(kkT[:, j, :], kkT[:, j, :], t2_, ALU.mult))
                V.tensor_tensor(bT[:, j, :], kkT[:, j, :], t1_, ALU.mult)
                link(V.tensor_scalar(t2_, t1_, -1.0, col("rw_k_a", j), ALU.add, ALU.mult))
                link(V.scalar_tensor_tensor(kT7[:, j, :], t2_, 1.0, kT7[:, j, :], ALU.add, ALU.mult))
                V.scalar_tensor_tensor(t4_, rT[:, j, :], col("rw_r_k", j), kT7[:, j, :], ALU.mult, ALU.mult).then_inc(rp_v, 1)
                link(V.tensor_scalar(t0_, t0_, 1.0, None, ALU.add))
                link(V.reciprocal(t0_, t0_))
                link(V.tensor_tensor_scan(t5_, keep[:], t0_, 0.0, ALU.mult, ALU.add))
                V.tensor_tensor(t0_, t5_, t0_, ALU.subtract).then_inc(rp_v, 1)
                tile_in(t["b"])
                V.tensor_tensor(bonT[:, j, :], vT7[:, j, :], bank[t["b"].bank][:], ALU.mult).then_inc(evac_v, 1)
                dve.wait_ge(rp_p, j + 1)
                V.tensor_tensor(bT[:, j, :], bT[:, j, :], t4_, ALU.mult)
                V.tensor_tensor(kT7[:, j, :], kT7[:, j, :], t4_, ALU.mult)
                V.tensor_tensor(rT[:, j, :], rT[:, j, :], t5_, ALU.mult)
                V.tensor_copy(pc[:, j, :], t5_[:, CH - 1:S:CH])
                V.scalar_tensor_tensor(kkT[:, j, :], kkT[:, j, :], -1.0, t3_, ALU.mult, ALU.mult).then_inc(rp_v, 1)
                dve.wait_ge(rp_v, 4 * j + 4)
            if upto == "rp":
                return
            m = wo_jobs[1][0][0].split
            split_to(splits_until(m + AHEAD, m))
            w3 = lambda b_: b_[:, 0:384].rearrange("p (j n) -> p j n", j=JP)
            eyes = eye2[:].unsqueeze(1).broadcast_to([P, JP, HD])
            for c in range(NCH):
                cs = slice(c * CH, c * CH + CH)
                dve.wait_ge(rc_t, RC_T.at("gram", c))
                if c:
                    dve.wait_ge(rc_t, RC_T.at("s", c - 1))
                    dve.wait_ge(rc_p, 6 * c)
                cm = causal.unsqueeze(1).broadcast_to([P, 3, P])
                for dst, b0 in ((GA, 0), (GK, 2)):
                    for q_ in range(2):
                        last = V.tensor_tensor(dst[:, 3 * q_:3 * q_ + 3, :],
                                               bank[b0 + q_][:, 0:384].rearrange("p (j n) -> p j n", j=3), cm, ALU.mult)
                last.then_inc(rc_v, 1)
                dve.wait_ge(rc_p, 6 * c + 1)
                dve.wait_ge(rc_t, RC_T.at("eye", c))
                V.tensor_tensor(TTm, ALT[:, 0, :].rearrange("p (j n) -> p j n", j=JP), eyes, ALU.add)
                V.tensor_tensor(Tm, w3(bank[7]), eyes, ALU.add).then_inc(rc_v, 1)
                for l in range(1, 6):
                    dve.wait_ge(rc_t, RC_T.at(f"t{l}", c))
                    dve.wait_ge(rc_v, RC_V.at(f"t{l - 1}", c))
                    if l < 5:
                        V.tensor_tensor(Tm, Tm, w3(bank[1]), ALU.add)
                    V.tensor_tensor(TTm, TTm, w3(bank[2]), ALU.add).then_inc(rc_v, 1)
                dve.wait_ge(rc_t, RC_T.at("x", c))
                V.tensor_copy(Xm, w3(bank[3])).then_inc(rc_v, 1)
                dve.wait_ge(rc_t, RC_T.at("y", c))
                V.tensor_copy(rT[:, :, cs], w3(bank[5])).then_inc(rc_v, 1)
                dve.wait_ge(rc_t, RC_T.at("s", c))
                link(V.tensor_tensor(state[:], state[:], w3(bank[6]), ALU.add))
                V.tensor_tensor(state[:], state[:], pc[:, :, c:c + 1].broadcast_to([P, JP, HD]), ALU.mult).then_inc(rc_v, 1)
                dve.wait_ge(rc_v, RC_V.at("s", c))
            for j in range(JP):
                t0, t1 = gn_tiles[j]
                dve.wait_ge(evac_a, t0.order + 1)
                V.tensor_tensor(rT[:, j, :], rT[:, j, :], t0_, ALU.add).then_inc(gn_v, 1)
                dve.wait_ge(gn_v, 3 * j + 1)
                dve.wait_ge(gn_a, 3 * j + 3)
                link(V.scalar_tensor_tensor(rT[:, j, :], rT[:, j, :], col("rw_lnx_w", j), t2_, ALU.mult, ALU.mult))
                link(V.scalar_tensor_tensor(rT[:, j, :], rT[:, j, :], col("rw_lnx_b", j), bonT[:, j, :], ALU.add, ALU.add))
                V.tensor_tensor(rT[:, j, :], rT[:, j, :], gT[:, j, :], ALU.mult).then_inc(gn_v, 1)
                dve.wait_ge(mix_hi, j + 1)
                V.tensor_tensor(h_lo[:, j, :], rT[:, j, :], h_hi[:, j, :], ALU.subtract).then_inc(gn_v, 1)
            if upto == "gn":
                return
            add_residual(wo_jobs[1])
            swiglu_dve(ffn[1])
            for k, t in enumerate(mem2_tiles):
                if t.eng == "v":
                    copy_out(t, memT2[:, 2 * k:2 * k + 2, :], bank[t.bank][:].rearrange("p (k m) -> p k m", k=2))
            m = mem2_jobs[0][0].split
            split_to(splits_until(m + AHEAD, m))
            norm_apply(mem2_norm)
            plain(mem2_jobs)
            norm_apply(n2a)
            if upto == "b1":
                return
            for t, _, dst, v in z_jobs:
                split_to(splits_until(t.split + AHEAD, t.split))
            for n, (t, _, dst, v, c) in enumerate(conv_jobs):
                split_to(splits_until(t.split + AHEAD, t.split))
                dve.wait_ge(conv_a, n + 1)
                for s_ in (1, 2):
                    link(V.scalar_tensor_tensor(dst[:, s_:S], v[:, 0:S - s_], col("conv_w_2", 6 * (3 - s_) + c), dst[:, s_:S],
                                                ALU.mult, ALU.add))
                V.scalar_tensor_tensor(dst[:, 3:S], v[:, 0:S - 3], col("conv_w_2", c), dst[:, 3:S],
                                       ALU.mult, ALU.add).then_inc(evac_v, 1)
            dve.wait_ge(evac_v, conv_jobs[-1][0].order + 1)
            dve.nop().then_inc(conv_v, 6)
            t, _, v = dt_job
            tile_in(t)
            s8 = lambda i: small[:, i, :]
            s48 = lambda i: small[:, i, :].rearrange("p (c h) -> p c h", c=4)
            V.tensor_tensor(s48(0), v, bcast[:, 36:44].unsqueeze(1).broadcast_to([P, TT, 8]), ALU.add).then_inc(evac_v, 1)
            dve.wait_ge(evac_v, t.order + 1)
            link(V.tensor_scalar(s8(2), s8(0), -1.0, None, ALU.mult))
            link(V.tensor_tensor(s8(2), s8(2), s8(0), ALU.min))
            dve.nop().then_inc(gates_ready, 2)
            plain(qkv_jobs)
            dve.wait_ge(sd_a, 1)
            link(V.tensor_scalar(s8(0), s8(0), 0.0, None, ALU.max))
            link(V.tensor_tensor(s8(0), s8(0), s8(2), ALU.add))
            link(V.tensor_scalar(s8(2), s8(0), -1.0, None, ALU.mult))
            V.tensor_tensor(s48(1), s48(2), bcast[:, 44:52].unsqueeze(1).broadcast_to([P, TT, 8]), ALU.mult).then_inc(sd_v, 1)
            h3 = lambda v_: v_.rearrange("p (h d) -> p h d", h=8)
            for c, t in enumerate(xd_tiles):
                tile_in(t)
                V.tensor_tensor(h3(XD[:, c, :]), h3(bank[t.bank][:]),
                                small[:, 0, c * 8:c * 8 + 8].unsqueeze(2).broadcast_to([P, 8, HD]), ALU.mult).then_inc(evac_v, 1)
            tile_in(ac_tile)
            ab = bank[ac_tile.bank]
            link(V.tensor_scalar(s8(5), ab[:, 0:32], -1.0, None, ALU.mult))
            V.tensor_copy(s8(4), ab[:, 32:64])
            V.tensor_tensor(s8(3), s8(5), ab[:, 32:64], ALU.add).then_inc(evac_v, 1)
            dve.wait_ge(evac_v, ac_tile.order + 1)
            dve.nop().then_inc(sd_v, 1)
            dve.wait_ge(sd_a, 2)
            q4 = lambda v_: v_.rearrange("p (h l) -> p h l", h=4)
            dve.wait_ge(consts, 4)
            for c in range(TT):
                cs = slice(c * P, c * P + P)
                dve.wait_ge(sc_a, SC_A.at("er", c))
                for g in range(2):
                    last = V.tensor_tensor(q4(SEG[g]), q4(bank[4 + g][:]), hide_gt.unsqueeze(1).broadcast_to([P, 4, P]), ALU.add)
                last.then_inc(sc_v, 1)
                V.tensor_tensor(h3(XDD), h3(XD[:, c, :]), small[:, 3, c * 8:c * 8 + 8].unsqueeze(2).broadcast_to([P, 8, HD]),
                                ALU.mult).then_inc(sc_v, 1)
                dve.wait_ge(sc_a, SC_A.at("e", c))
                for g in range(2):
                    last = V.tensor_tensor(q4(MM_[g]), q4(SEG[g]), bank[(6, 2)[g]][:, 0:P].unsqueeze(1).broadcast_to([P, 4, P]),
                                           ALU.mult)
                last.then_inc(sc_v, 1)
                for g in range(2):
                    gs = slice(g * HD, g * HD + HD)
                    last = V.tensor_tensor(q4(CT[gs, :]), q4(ER[g][gs, :]), xbc[gs, 5, cs].unsqueeze(1).broadcast_to([HD, 4, P]),
                                           ALU.mult)
                last.then_inc(sc_v, 1)
                dve.wait_ge(sc_t, SC_T.at("y", c))
                for k in range(4):
                    last = V.scalar_tensor_tensor(yS[:, k, cs], xbc[:, k, cs], dskip[:, k:k + 1],
                                                  bank[(7, 1)[k // 2]][:, (k % 2) * P:(k % 2) * P + P],
                                                  ALU.mult, ALU.add)
                last.then_inc(sc_v, 1)
                dve.wait_ge(sc_t, SC_T.at("st", c))
                for g in range(2):
                    gs = slice(g * HD, g * HD + HD)
                    pv_ = bank[3][gs, 0:256].rearrange("p (h d) -> p h d", h=4)
                    cd = small[gs, 4, c * 8 + 4 * g:c * 8 + 4 * g + 4].unsqueeze(2).broadcast_to([HD, 4, HD])
                    if c == 0:
                        last = V.tensor_copy(SST[gs], pv_)
                    else:
                        link(V.tensor_tensor(SST[gs], SST[gs], cd, ALU.mult))
                        last = V.tensor_tensor(SST[gs], SST[gs], pv_, ALU.add)
                last.then_inc(sc_v, 1)
                dve.wait_ge(sc_v, SC_V.at("st", c))
            for k in range(4):
                last = V.tensor_tensor(yS[:, k, :], yS[:, k, :], zT[:, k, :], ALU.mult)
            last.then_inc(sd_v, 1)
            norm_apply(nssd)
            for u in range(4 * SH):
                h, js = u // 4, 3 - u % 4
                z_ = bank[4 + u % 2][:, js * P:S]
                dve.wait_ge(sb_t, 1 if u == 0 else 2 * u)
                if u >= 2:
                    dve.wait_ge(sb_v, 2 * (u - 2) + 2)
                V.tensor_scalar(T1[u % 2][:, js * P:S], z_, 80.0, None, ALU.min).then_inc(sb_v, 1)
                dve.wait_ge(sb_a, 3 * u + 2)
                if u >= 4:
                    dve.wait_ge(sb_t, 8 * (u // 4))
                link(V.tensor_tensor(SP[:, js, js * P:S], T1[u % 2][:, js * P:S], z_, ALU.max))
                dg = SP[:, js, js * P:js * P + P]
                V.tensor_tensor(dg, dg, triu_s, ALU.mult).then_inc(sb_v, 1)
                if u % 4 == 1 and u // 4 and (u // 4) % 2 == 0:
                    dve.wait_ge(sb_pv, u // 4)
                    V.tensor_copy(yB[:, u // 8 - 1, :], bank[7][:]).then_inc(sb_out, 1)
            dve.wait_ge(sb_pv, SH)
            V.tensor_copy(yB[:, 3, :], bank[7][:]).then_inc(sb_out, 1)
            norm_apply(nsb)
            if upto == "sb":
                return
            add_residual(wout_jobs)
            norm_apply(n2b)
            plain(xq_jobs)
            attention("xa")
            add_residual(wxo_jobs)
            norm_apply(n2c)
            for n, (t, _, j, v) in enumerate(ff1_jobs):
                split_to(splits_until(t.split + AHEAD, t.split))
                dve.wait_ge(shifted, len(shift_jobs) + n + 1)
                if j >= 2:
                    dve.wait_ge(hid_lo, 2 * FT + j - 1)
                V.scalar_tensor_tensor(hraw[1][:, j % 2, :], v, FF_SCALE, hraw[0][:, j % 2, :], ALU.mult,
                                       ALU.mult).then_inc(evac_v, 1)
                if j:
                    hidden(j - 1, 2 * FT)
            hidden(FFT - 1, 2 * FT)
            add_split(ff2_halves, FF_SCALE ** -2)
            norm_apply(n2f)
            for i, t in enumerate(out_tiles):
                if t.eng == "v":
                    tt, kh = divmod(i, 2)
                    copy_out(t, out_sb[:, tt, kh * 512:kh * 512 + 512], bank[t.bank][:])


_OUT = (1, S, D)


def kernel(**inputs):
    import concourse.bacc as bacc
    from concourse.bass_utils import run_bass_kernel_spmd

    nc = bacc.Bacc("TRN2", target_bir_lowering=False, num_devices=1)
    arrays, args = {}, {}
    for name, value in inputs.items():
        v = np.ascontiguousarray(value)
        arrays[f"in_{name}"] = v
        args[name] = nc.dram_tensor(f"in_{name}", v.shape, mybir.dt.from_np(v.dtype), kind="ExternalInput").ap()
    out = nc.dram_tensor("out_x", _OUT, F32, kind="ExternalOutput").ap()
    block_stack(nc, args, out)
    r = run_bass_kernel_spmd(nc, [arrays], core_ids=[0])
    return r.results[0]["out_x"]
```

```python
import math
from contextlib import ExitStack

import numpy as np
import concourse.bass as bass
from concourse import mybir

F32 = mybir.dt.float32
F16 = mybir.dt.float16
BF16 = mybir.dt.bfloat16
ALU = mybir.AluOpType
ACT = mybir.ActivationFunctionType
AX = mybir.AxisListType

P = 128
D = 1024
KC = D // P
S = 512
TT = S // P
M = 256
HD = 64
NEG = -1.0e30

H1 = 12
G1 = 4
R1 = H1 // G1
MIX = H1 * HD
KV = G1 * HD
CB, CS = 32, 16
NCMP = (S - CB) // CS + 1
FH = 2816
FT = FH // P
SLOT = 3 * MIX + 64 + 64 + 160
DECAY = math.exp(-0.5)
CH = 64
NCH = S // CH
JP = H1 // 2
SD = 512
SH = 8
SG = 2
XH = 4
FF = 4096
FFT = FF // P
EPS1, EPS2, EPS_GN = 1e-6, 1e-5, 64e-5

NSLOT = 3
NSPLIT = 3
PANEL = 2048
AHEAD = 2
FF_SCALE = 1.0 / 8
TO_TURN = 3
TO_VALUES = 5
QORDER = (1, 3, 0, 2)
NBANK = 4


def alibi_slopes(n):
    def pow2(m):
        start = 2.0 ** (-8.0 / m)
        return [start ** (i + 1) for i in range(m)]
    c = 2 ** int(math.floor(math.log2(n)))
    s = pow2(c)
    if c < n:
        s = s + pow2(2 * c)[0::2][: n - c]
    return [float(np.float32(v)) for v in s]


class Steps:

    def __init__(self, sem, *names):
        self.sem, self.names = sem, names

    def at(self, name, rnd):
        return rnd * len(self.names) + self.names.index(name) + 1


class Tile:

    def __init__(self, n, eng, order):
        self.n, self.bank, self.eng, self.order = n, n % NBANK, eng, order
        self.split = None


def block_stack(nc, a, out, upto=None):
    ctx = ExitStack()
    with ctx:
        def sb(name, shape, dt=F32):
            return ctx.enter_context(nc.sbuf_tensor(name, shape, dt))

        def sem(name):
            return ctx.enter_context(nc.semaphore(name))

        xT = sb("xT", [P, KC, S])
        h_hi = sb("h_hi", [P, KC, S], F16)
        h_lo = sb("h_lo", [P, KC, S], BF16)
        hT = (h_hi, h_lo)
        wring = sb("wring", [P, NSLOT, PANEL])
        w_hi = sb("w_hi", [P, NSPLIT, PANEL], F16)
        w_lo = sb("w_lo", [P, NSPLIT, PANEL], BF16)
        arena = sb("arena", [P, 54 * S])
        ntmp = sb("ntmp", [P, 2, S])
        ident = sb("ident", [P, P])
        ones = sb("ones", [P, P])
        nones = sb("nones", [P, P])
        blockones = sb("blockones", [P, P])
        eye2 = sb("eye2", [P, HD])
        dist = sb("dist", [P, S])
        distc = sb("distc", [P, TT, NCMP])
        keep = dist
        triu = sb("triu", [P, P])
        masks = sb("masks", [P, 4 * P])
        causal = masks[:, 0:P]
        level = masks[:, P:4 * P].rearrange("p (l n) -> p l n", l=6)
        triu_s, ntril = masks[:, 0:P], masks[:, P:2 * P]
        hide_gt, hide_ge = masks[:, 2 * P:3 * P], masks[:, 3 * P:4 * P]
        qscale = sb("qscale", [P, 6])
        cols = sb("cols", [P, 320])
        ncols = sb("ncols", [P, 16])
        omu = sb("omu", [P, 21])
        eps = sb("eps", [P, 5])
        bcast = sb("bcast", [P, 60])
        dskip = sb("dskip", [P, 4])
        cmp_w2 = sb("cmp_w2", [P, 2, HD])
        stat = sb("stat", [P, 3, 4, 2])
        cst = sb("cst", [P, 3, 48])
        cslope = sb("cslope", [P, 12])
        rsb = sb("rsb", [P, S])
        small = sb("small", [P, 6, 32])
        gates = small[:, :, :].rearrange("p a b -> p (a b)")[:, 0:TT * 36].rearrange("p (t n) -> p t n", t=TT)
        bank = [ctx.enter_context(nc.psum_tensor(f"bank{i}", [P, S], F32)) for i in range(8)]

        def blk(first, n=1, width=S):
            v = arena[:, first * S:first * S + n * width]
            return v.rearrange("p (n w) -> p n w", n=n)

        def parts(first, n, width=S):
            m = n * width // 2
            return tuple(arena[:, first * S + i * m:first * S + (i + 1) * m].bitcast(dt)
                         .rearrange("p (n w) -> p n w", n=n) for i, dt in enumerate((F16, BF16)))

        rows = blk(30)[:, 0, 0:3 * P].rearrange("p (j n) -> p j n", j=3)

        landed = [sem(f"landed{i}") for i in range(NSLOT)]
        panel_read = sem("panel_read")
        acc_full = sem("acc_full")
        evac_v = sem("evac_v")
        evac_a = sem("evac_a")
        consts = sem("consts")
        ident_ready = sem("ident_ready")
        rows_clear = sem("rows_clear")
        vec_in = sem("vec_in")
        cols_ready = sem("cols_ready")
        split_hi = sem("split_hi")
        split_lo = sem("split_lo")
        squared = sem("squared")
        norm_part = sem("norm_part")
        scaled = sem("scaled")
        cast = sem("cast")
        hid_f = sem("hid_f")
        hid_hi = sem("hid_hi")
        hid_lo = sem("hid_lo")
        cmp_s = sem("cmp_s")
        qk_hi = sem("qk_hi")
        kcb_split = sem("kcb_split")
        cmp_u = sem("cmp_u")
        cmp_e = sem("cmp_e")
        cmp_w = sem("cmp_w")
        cmp_t = sem("cmp_t")
        cmp_pt = sem("cmp_pt")
        cmp_ptv = sem("cmp_ptv")
        att_hi = sem("att_hi")
        mix_hi = sem("mix_hi")
        rooted = sem("rooted")
        normed = sem("normed")
        chain_v = sem("chain_v")
        chain_a = sem("chain_a")
        chain_p = sem("chain_p")
        gates_ready = sem("gates_ready")
        gate_exp_in = sem("gate_exp_in")
        gate_exp = sem("gate_exp")
        gelu_in = sem("gelu_in")
        gelu_exp = sem("gelu_exp")
        gelu_out = sem("gelu_out")
        cmp_ready = sem("cmp_ready")
        att_scores = sem("att_scores")
        att_max = sem("att_max")
        att_exp = sem("att_exp")
        att_weight = sem("att_weight")
        att_turned = sem("att_turned")
        att_copied = sem("att_copied")
        att_pv = sem("att_pv")
        att_out = sem("att_out")
        shifted = sem("shifted")
        lora_mid = sem("lora_mid")
        lora_in = sem("lora_in")
        rp_square = sem("rp_square")
        rp_sigma = sem("rp_sigma")
        rp_root = sem("rp_root")
        rp_exp = sem("rp_exp")
        rp_max = sem("rp_max")
        rp_scan = sem("rp_scan")
        rp_rk = sem("rp_rk")
        rp_done = sem("rp_done")
        rc_t = sem("rc_t")
        rc_v = sem("rc_v")
        rc_a = sem("rc_a")
        rc_p = sem("rc_p")
        rs_t = sem("rs_t")
        rs_v = sem("rs_v")
        rs_a = sem("rs_a")
        gn_centred = sem("gn_centred")
        gn_square = sem("gn_square")
        gn_root = sem("gn_root")
        gn_out = sem("gn_out")
        gn_lo = sem("gn_lo")
        sd_v = sem("sd_v")
        sd_a = sem("sd_a")
        sc_t = sem("sc_t")
        sc_v = sem("sc_v")
        sf_t = sem("sf_t")
        sf_v = sem("sf_v")
        ssd_xdd = sem("ssd_xdd")
        ssd_ct = sem("ssd_ct")
        sc_a = sem("sc_a")
        conv_a = sem("conv_a")
        conv_v = sem("conv_v")
        sb_logits = sem("sb_logits")
        sb_sums = sem("sb_sums")
        sb_min = sem("sb_min")
        sb_soft = sem("sb_soft")
        sb_exp = sem("sb_exp")
        sb_ln = sem("sb_ln")
        sb_weight = sem("sb_weight")
        sb_pv = sem("sb_pv")
        sb_out = sem("sb_out")
        out_sent = sem("out_sent")

        tiles, order = [], {"v": 0, "a": 0}

        def tile(eng):
            t = Tile(len(tiles), eng, order[eng])
            order[eng] += 1
            tiles.append(t)
            return t

        panels = []

        splits = []

        def panel(*srcs):
            p = {"slot": len(panels) % NSLOT, "n": len(panels), "until": None}
            before = panels[-NSLOT]["level"] if len(panels) >= NSLOT else 0
            p["parts"] = [(f(wring[:, p["slot"], :]), src) for f, src in srcs]
            p["level"] = before + 16 * len(srcs)
            panels.append(p)
            return p

        def split_panel(k, n, *srcs):
            p = panel(*srcs)
            p.update(m=len(splits), size=k * n, until=(split_lo, len(splits) + 1), read=None)
            sl = p["m"] % NSPLIT
            p["hi"], p["lo"] = (w_[:, sl, 0:k * n].rearrange("p (k n) -> p k n", k=k) for w_ in (w_hi, w_lo))
            splits.append(p)
            return p

        def columns(w, c0, n, k=KC):
            return split_panel(k, n, (lambda s: s[:, 0:k * n].rearrange("p (k n) -> p k n", k=k),
                                      w[0:k * P, c0:c0 + n].rearrange("(k p) n -> p k n", p=P)))

        def until_tile(p, t):
            p["read" if "m" in p else "until"] = (acc_full, t.n + 1)
            if "m" in p:
                t.split = p["m"]

        vec = {}
        vec_dmas = []
        nrow = [0]

        def vrow(name, src, n):
            vec[name] = nrow[0]
            r = 0
            while r < n:
                j, o = divmod(nrow[0] + r, P)
                m = min(n - r, P - o)
                vec_dmas.append((rows[o:o + m, j, :], src[r:r + m, :]))
                r += m
            nrow[0] += n

        for nm in ("norm1", "norm_mem", "norm2"):
            vrow(nm, a[nm].rearrange("l (k p) -> (l k) p", p=P), 2 * KC)
        for nm in ("final_norm", "final_g_2"):
            vrow(nm, a[nm].rearrange("(k p) -> k p", p=P), KC)
        for nm in ("norm_mix_g_2", "norm_xa_g_2", "norm_mem_g_2", "norm_ff_g_2"):
            vrow(nm, a[nm].rearrange("l (k p) -> (l k) p", p=P), KC)
        for nm in ("ssd_norm_g_2", "sb_norm_g_2"):
            vrow(nm, a[nm].rearrange("l (k p) -> (l k) p", p=P), 4)
        vrow("rw_mu", a["rw_mu"][:, 0:20 * P].rearrange("l (k p) -> (l k) p", p=P), 20)
        for nm in ("rw_w0", "rw_a0", "rw_k_k", "rw_k_a", "rw_lnx_w", "rw_lnx_b"):
            vrow(nm, a[nm].rearrange("l (k p) -> (l k) p", p=P), 6)
        vrow("rw_r_k", a["rw_r_k"].rearrange("l (c two) d -> (l c) (two d)", two=2), 6)
        vrow("conv_w_2", a["conv_w_2"].rearrange("l k (c p) -> (l k c) p", p=P), 24)
        vrow("conv_b_2", a["conv_b_2"].rearrange("l (c p) -> (l c) p", p=P), 6)
        NVEC = nrow[0]
        MU20 = NVEC
        j20, o20 = divmod(MU20, P)
        vec_dmas.append((rows[o20:o20 + 1, j20, 0:32], a["rw_mu"][:, 20 * P:SLOT]))
        POS = 256
        for j in range(2):
            for hf in range(2):
                vec_dmas.append((rows[j * CS:j * CS + CS, 2, hf * HD:hf * HD + HD], a["nsa_cmp_pos"][0, j, hf * CS:hf * CS + CS, :]))
        vec_dmas.append((bcast[:, 0:36], a["nsa_gate_b"].rearrange("a n -> (a n)").partition_broadcast(P)))
        vec_dmas.append((bcast[:, 36:44], a["dt_bias_2"].rearrange("a n -> (a n)").partition_broadcast(P)))
        vec_dmas.append((bcast[:, 44:52], a["a_log_2"].rearrange("a n -> (a n)").partition_broadcast(P)))
        vec_dmas.append((bcast[:, 52:60], a["d_skip_2"].rearrange("a n -> (a n)").partition_broadcast(P)))
        vec_dmas.append((cmp_w2[:, :, :], a["nsa_cmp_w2"].rearrange("z j e d -> e (z j) d")))

        def col(name, j, p0=0, p1=P):
            return cols[p0:p1, vec[name] + j:vec[name] + j + 1]

        MUC = lambda j: cols[:, (vec["rw_mu"] + j if j < 20 else MU20):(vec["rw_mu"] + j if j < 20 else MU20) + 1]

        def rows_panel(src, nt):
            p = panel((lambda s: s[:, 0:nt * D].rearrange("p (t d) -> p t d", t=nt),
                       src.rearrange("z (t p) d -> p (z t) d", p=P)))
            p["v"] = wring[:, p["slot"], 0:nt * D].rearrange("p (t d) -> p t d", t=nt)
            return p

        x_panels = [rows_panel(a["x"][:, hf * M:hf * M + M, :], 2) for hf in range(2)]
        x_tiles = [tile("va"[k % 2]) for k in range(KC)]
        for p in x_panels:
            until_tile(p, x_tiles[-1])
        vec_tile = tile("v")
        mem_panel = rows_panel(a["mem"], 2)
        memT = blk(40, KC, M)
        mem_tiles = [tile("va"[k % 2]) for k in range(KC // 2)]
        until_tile(mem_panel, mem_tiles[-1])

        norms, nk = [], [0, 0]

        def norm(src, dst, gain, k, n, epscol):
            nm = dict(src=src, dst=dst, gain=gain, k=k, n=n, eps=epscol, j=len(norms), b=nk[0], c=nk[1])
            nk[0] += k
            nk[1] += k * isinstance(dst, tuple)
            norms.append(nm)
            return nm

        def feature_tile(w, c, width, h, eng, n=S, k=KC, m=P):
            t = tile(eng)
            v = bank[t.bank][0:m, 0:n]
            mm = [(v, [(w[a_][:, kk, c:c + m], h[b_][:, kk, 0:n], w, kk) for kk in range(k)
                       for a_, b_ in (("hi", 0), ("hi", 1), ("lo", 0))])]
            until_tile(w, t)
            return t, mm, v

        def token_tile(w, c, width, h, tts, eng, k=KC):
            t = tile(eng)
            v = bank[t.bank][:, 0:len(tts) * width].rearrange("p (t w) -> p t w", t=len(tts))
            mm = [(v[:, i, :], [(h[b_][:, kk, tt * P:tt * P + P], w[a_][:, kk, c:c + width], w, kk) for kk in range(k)
                                for b_, a_ in ((0, "hi"), (0, "lo"), (1, "hi"))])
                  for i, tt in enumerate(tts)]
            until_tile(w, t)
            return t, mm, v

        mn = parts(32, KC, M)
        kmT = [blk(44 + 2 * l, 2, M) for l in range(2)]
        vm = [blk(45 + 2 * l, 2, M) for l in range(2)]
        mem_norm, mem_jobs = [], []
        for l in range(2):
            mem_norm.append(norm(memT, mn, ("norm_mem", l * KC), KC, M, 0))
            w = columns(a["w_mem_kv"][l], 0, M)
            jobs = []
            for c in range(2):
                t, mm, v = feature_tile(w, c * P, P, mn, "va"[c], n=M)
                jobs.append((t, mm, kmT[l][:, c, :], v, 1.0))
            w = columns(a["w_mem_kv"][l], M, M)
            t, mm, v = token_tile(w, 0, M, mn, range(2), "v")
            jobs.append((t, mm, vm[l][:, :, :], v, 1.0))
            mem_jobs.append(jobs)

        qT = parts(0, 6)
        ksT, kwT, qmT = parts(10, 2), parts(12, 2), blk(14, 2)
        vs, vw = blk(16, 4, KV), blk(18, 4, KV)
        n1a = norm(xT, hT, ("norm1", 0), KC, S, 0)
        wn = a["nsa_w_in"][0]
        nsa_jobs, cmp_jobs = [], []
        cmp_src = [blk(20, 4), blk(48, 4)]
        for j in range(2):
            w = columns(wn, MIX + j * KV, KV)
            for c in range(2):
                t, mm, v = feature_tile(w, c * P, P, hT, "va"[c])
                cmp_jobs.append((t, mm, cmp_src[j], v, c))
        cmp_panels = []
        for j in range(2):
            w = panel(*[((lambda s, hf=hf: s[hf * HD:hf * HD + HD, :].rearrange("p (l e) -> p l e", l=CS)),
                         a["nsa_cmp_w1"][0, j, hf * CS:hf * CS + CS].rearrange("l d e -> d l e")) for hf in range(2)])
            w["v"] = wring[:, w["slot"], :].rearrange("p (l e) -> p l e", l=CS)
            cmp_panels.append(w)
        cmp_hid = [tile("v") for _ in range(2)]
        for j in range(2):
            until_tile(cmp_panels[j], cmp_hid[j])
        slopes = alibi_slopes(H1)
        pair = lambda h: (h // 6) * 3 + h % 3
        for gp in range(2):
            for r in range(3):
                w = split_panel(KC, P, *[
                    ((lambda s, gg=gg: s[:, 0:KC * P].rearrange("p (k g d) -> p k g d", k=KC, g=2)[:, :, gg, :]),
                     wn[:, (3 * (2 * gp + gg) + r) * HD:(3 * (2 * gp + gg) + r + 1) * HD].rearrange("(k p) d -> p k d", p=P))
                    for gg in range(2)])
                t, mm, v = feature_tile(w, 0, P, hT, "v")
                nsa_jobs.append((t, mm, [x[:, gp * 3 + r, :] for x in qT], v, qscale[:, gp * 3 + r:gp * 3 + r + 1]))
        for c0, dst in ((MIX + 2 * KV, ksT), (MIX + 4 * KV, kwT), (MIX + 6 * KV + 36, qmT)):
            w = columns(wn, c0, KV)
            for c in range(2):
                whole = dst is qmT
                t, mm, v = feature_tile(w, c * P, P, hT, "va"[c % 2] if whole else "v")
                nsa_jobs.append((t, mm, dst[:, c, :] if whole else [x[:, c, :] for x in dst], v, HD ** -0.5 if whole else 1.0))
        for c0, v_ in ((MIX + 3 * KV, vs), (MIX + 5 * KV, vw)):
            w = columns(wn, c0, KV)
            for i in range(2):
                t, mm, v = token_tile(w, 0, KV, hT, range(2 * i, 2 * i + 2), "va"[i % 2])
                nsa_jobs.append((t, mm, v_[:, 2 * i:2 * i + 2, :], v, 1.0))
        w = columns(wn, MIX + 6 * KV, 36)
        gate_job = token_tile(w, 0, 36, hT, range(TT), "v")

        cmp_res = [tile("v") for _ in range(2)]
        kcb = blk(26)[:, 0, 0:2 * NCMP].rearrange("p (c n) -> p c n", c=2)
        kcb_parts = [blk(26)[:, 0, 64 + 32 * i:95 + 32 * i].bitcast(dt).rearrange("p (c n) -> p c n", c=2)
                     for i, dt in enumerate((F16, BF16))]
        vcb = blk(27)[0:NCMP, 0, 0:KV].rearrange("p (g d) -> p g d", g=G1)
        cbias = blk(27)[:, 0, KV:KV + 1]
        chid = blk(28)[:, 0, 0:248].rearrange("p (j n) -> p j n", j=2)
        ctmp = blk(28)[:, 0, 256:380]

        cmp_heads = [[6 * a_ + 3 * e + r for a_ in range(2) for r in range(3)] for e in range(2)]
        cmp_head = lambda x: cmp_heads[x // 6][x % 6]
        CU = blk(40, 3)[:, :, :].rearrange("p a w -> p (a w)")[:, 0:48 * NCMP].rearrange("p (x n) -> p x n", x=48)
        PTc = blk(28, 12)

        groups = []
        att_stage = {}
        nout = [0]

        def group(pb, ptb, **k):
            n = len(groups)
            k["n"] = n
            k["s"] = [bank[2 * (n % 2) + w] for w in range(2)]
            k["P"] = [blk(pb[n % 4] + w)[:, 0, :] for w in range(2)]
            k["PT"] = [blk(ptb[n % 3] + w)[:, 0, :] for w in range(2)]
            k["st"] = stat[:, n % 3, :, :]
            k["out0"] = nout[0]
            if k.get("evac") is not None:
                nout[0] += 1
            groups.append(k)

        zeros = sb("zeros", [P, M])
        att_stage["nsa"] = [0]
        for c in range(6):
            ob = bank[6 + c % 2]
            for i in QORDER:
                for hf in range(2):
                    h = 2 * c + hf
                    g = h // R1
                    b0 = HD * (g % 2)
                    q = [x[b0:b0 + HD, pair(h), i * P:i * P + P] for x in qT]
                    N = (i + 1) * P
                    dd = dist[:, (TT - 1 - i) * P:S]
                    o = ob[hf * HD:hf * HD + HD, i * P:i * P + P]
                    group((20, 22, 24, 6), (40, 42, 48), slope=slopes[h], N=N, gates=gates[:, i, H1 + h:3 * H1:H1],
                          first=((ob[hf * HD:hf * HD + HD, :], vcb[:, g, :], PTc[0:NCMP, h, :]) if i == QORDER[0] else None),
                          units=[dict(q=q, k=[x[b0:b0 + HD, g // 2, 0:N] for x in kT_], D=dd, o=o, start=False,
                                      v=[v_[:, t, g * HD:g * HD + HD] for t in range(i + 1)])
                                 for kT_, v_ in ((ksT, vs), (kwT, vw))],
                          evac=(ob, c) if (i == QORDER[-1] and hf == 1) else None, ob=(i == QORDER[0] and hf == 0))

        def mem_groups(l, qm, pb, ptb):
            for c in range(2):
                ob = bank[6 + c % 2]
                for i in range(TT):
                    group(pb, ptb, slope=1.0, N=M, gates=None, first=None, ob=(i == 0),
                          units=[dict(q=qm[hf * HD:hf * HD + HD, c, i * P:i * P + P], k=kmT[l][hf * HD:hf * HD + HD, c, :],
                                      D=zeros[:, :], o=ob[hf * HD:hf * HD + HD, i * P:i * P + P], start=True,
                                      v=[vm[l][:, t, (2 * c + hf) * HD:(2 * c + hf + 1) * HD] for t in range(2)])
                                 for hf in range(2)],
                          evac=(ob, 6 + c) if i == TT - 1 else None)

        mem_groups(0, qmT, (20, 22, 24, 6), (40, 42, 48))
        att_stage["nsa"].append(len(groups))

        def residual(w_dram, h, k):
            jobs = []
            per_panel = PANEL // k
            for c0 in range(0, D, per_panel):
                w = columns(w_dram, c0, per_panel, k)
                for c in range(per_panel // P):
                    t, mm, v = feature_tile(w, c * P, P, h, "v", k=k)
                    jobs.append((t, mm, (c0 // P) + c, v))
            return jobs

        def residual_split(w_dram, h, k):
            halves = []
            for hf in range(2):
                ts = [tile("v") for _ in range(4)]
                ps = []
                for k0 in range(0, k, 4):
                    kk = min(4, k - k0)
                    w = columns(w_dram[k0 * P:(k0 + kk) * P, :], hf * 512, 512, kk)
                    ps.append((w, k0, kk))
                halves.append((hf, ts, ps, h))
            return halves

        wo_jobs = [None, None]
        wo_jobs[0] = residual(a["w_o"][0], hT, KC)
        hid = parts(0, 32)
        hraw = [blk(32, 2), blk(34, 2)]

        def swiglu(l):
            nm = norm(xT, hT, ("norm2", l * KC), KC, S, 0)
            jobs = []
            wi = a["w_ffn_in"][l]
            for b in range(FT):
                w = split_panel(KC, 2 * P, *[
                    ((lambda s, o=o: s.rearrange("p (k n) -> p k n", k=KC)[:, :, o * P:o * P + P]),
                     wi[:, o * FH + b * P:o * FH + b * P + P].rearrange("(k p) n -> p k n", p=P)) for o in range(2)])
                jobs.append((feature_tile(w, 0, P, hT, "a"), feature_tile(w, P, P, hT, "v"), b))
            return [nm, jobs, residual_split(a["w_ffn_out"][l], hid, FT), l * FT]

        ffn = [swiglu(0)]

        rT, kT7, vT7 = blk(0, 6), blk(6, 6), blk(12, 6)
        kkT, bT, bonT = blk(18, 6), blk(24, 6), blk(30, 6)
        lo, lo2, lo3, qm1 = blk(36)[:, 0, :], blk(37)[:, 0, :], blk(38)[:, 0, :], blk(39, 2)
        n1b = norm(xT, hT, ("norm1", KC), KC, S, 0)
        ffn[0].append(n1b)
        wr = a["rw_w_in"][0]
        shift_jobs, qm1_jobs = [], []
        for b in range(10):
            w = columns(wr, b * M, M)
            for c in range(2):
                j = 2 * b + c
                dst = blk(j)[:, 0, :] if j < 18 else (lo if j == 18 else lo2)
                t, mm, v = feature_tile(w, c * P, P, hT, "v")
                shift_jobs.append((t, mm, dst, v, j, P))
        w = columns(wr, 2560, 32)
        t, mm, v = feature_tile(w, 0, 32, hT, "v", m=32)
        shift_jobs.append((t, mm, lo3[0:32, :], v, 20, 32))
        w = columns(wr, 2592, M)
        for c in range(2):
            t, mm, v = feature_tile(w, c * P, P, hT, "a")
            qm1_jobs.append((t, mm, qm1[:, c, :], v, HD ** -0.5))
        lora_panels = [panel((lambda s: s[0:64, 0:MIX], a["rw_w2"][0]),
                             (lambda s: s[64:128, 0:MIX], a["rw_a2"][0]),
                             (lambda s: s[:, MIX:2 * MIX], a["rw_g2"][0, 0:P, :])),
                       panel((lambda s: s[0:32, 0:MIX], a["rw_g2"][0, P:160, :]))]
        lw, lw2 = (wring[:, p["slot"], :] for p in lora_panels)
        att_stage["mem1"] = [len(groups)]
        mem_groups(1, qm1, (18, 20, 22, 30), (24, 26, 28))
        att_stage["mem1"].append(len(groups))
        gT = blk(48, 6)
        rp_tiles = [{} for _ in range(JP)]
        for j in range(JP + 2):
            if j < JP:
                rp_tiles[j].update(w=tile("a"), a=tile("a"), g=tile("a"))
            if j >= 2:
                rp_tiles[j - 2]["b"] = tile("v")
            if j < JP:
                rp_tiles[j]["n"] = tile("v")
        for p in lora_panels:
            until_tile(p, rp_tiles[-1]["g"])
        second = [t_[:, 0:6, :].rearrange("p k s -> p (k s)").bitcast(F32) for t_ in (h_hi, h_lo)]
        tmp = [[blk(41 + i)[:, 0, :] for i in range(6)] + [rsb[:, :]],
               [second[i // 3][:, i % 3 * S:i % 3 * S + S] for i in range(6)] + [blk(47)[:, 0, :]]]
        pc = sb("pc", [P, JP, NCH])
        gn_tiles = [{} for _ in range(JP)]
        gn_tiles[0]["s"] = tile("v")
        for j in range(JP):
            if j + 1 < JP:
                gn_tiles[j + 1]["s"] = tile("v")
            gn_tiles[j]["q"] = tile("a")
        gtmp = [[blk(36 + 2 * (j % 3) + i)[:, 0, :] for i in range(2)] for j in range(JP)]
        jn = lambda v: v.rearrange("p (j n) -> p j n", j=JP)
        o_ = 36 * S
        own = [arena[:, o_ + i * 384:o_ + (i + 1) * 384] for i in range(11)]
        GA = [jn(arena[:, o_:o_ + 768]), jn(second[0][:, 0:768])]
        GK = [jn(arena[:, o_ + 768:o_ + 1536]), jn(second[0][:, 768:1536])]
        BT, KT, VT, TTf = ([jn(own[4 + i]), jn(second[1][:, i * 384:i * 384 + 384])] for i in range(4))
        Ym, Xm, Um = (jn(own[8 + i]) for i in range(3))
        o_ += 11 * 384
        T2 = arena[:, o_:o_ + 768].rearrange("p (h w n) -> p h w n", h=2, w=2)
        o_ += 768
        NALT = 3
        ALT = arena[:, o_:o_ + NALT * 384].rearrange("p (a n) -> p a n", a=NALT)
        state = sb("state", [P, JP, HD])
        wo_jobs[1] = residual(a["w_o"][1], hT, KC)
        ffn.append(swiglu(1))
        n1f = norm(xT, xT, ("final_norm", 0), KC, S, 0)
        ffn[1].append(n1f)

        mem2_panel = rows_panel(a["mem_2"], 2)
        memT2, mn2 = blk(40, KC, M), parts(36, KC, M)
        mem2_tiles = [tile("va"[k % 2]) for k in range(KC // 2)]
        until_tile(mem2_panel, mem2_tiles[-1])
        mem2_norm = norm(memT2, mn2, ("norm_mem_g_2", 0), KC, M, 1)
        kxT, vx = blk(44, 4, M), blk(46, 2)
        mem2_jobs = []
        for b in range(2):
            w = columns(a["w_xk_2"][0], b * M, M)
            for c in range(2):
                t, mm, v = feature_tile(w, c * P, P, mn2, "va"[c % 2], n=M)
                mem2_jobs.append((t, mm, kxT[:, 2 * b + c, :], v, 1.0))
        for b in range(2):
            w = columns(a["w_xv_2"][0], b * M, M)
            t, mm, v = token_tile(w, 0, M, mn2, range(2), "va"[b % 2])
            mem2_jobs.append((t, mm, vx[:, :, b * M:b * M + M], v, 1.0))
        n2a = norm(xT, hT, ("norm_mix_g_2", 0), KC, S, 1)
        zT, xbc, q2, k2, v2 = blk(0, 4), blk(4, 6), blk(10, 4), blk(14, 4), blk(18, 4)
        wi2 = a["w_in_2"][0]
        z_jobs, conv_jobs, qkv_jobs = [], [], []
        for b in range(2):
            w = columns(wi2, b * M, M)
            for c in range(2):
                t, mm, v = feature_tile(w, c * P, P, hT, "a")
                z_jobs.append((t, mm, zT[:, 2 * b + c, :], v))
        for b in range(3):
            w = columns(wi2, 512 + b * M, M)
            for c in range(2):
                t, mm, v = feature_tile(w, c * P, P, hT, "v")
                conv_jobs.append((t, mm, xbc[:, 2 * b + c, :], v, 2 * b + c))
        w = columns(wi2, 1280, 8)
        dt_job = token_tile(w, 0, 8, hT, range(TT), "v")
        for c0, dst, sc in ((1288, q2, HD ** -0.5), (1800, k2, 1.0)):
            for b in range(2):
                w = columns(wi2, c0 + b * M, M)
                for c in range(2):
                    t, mm, v = feature_tile(w, c * P, P, hT, "va"[c % 2])
                    qkv_jobs.append((t, mm, dst[:, 2 * b + c, :], v, sc))
        for b in range(2):
            w = columns(wi2, 2312 + b * M, M)
            for i in range(2):
                t, mm, v = token_tile(w, 0, M, hT, range(2 * i, 2 * i + 2), "va"[i % 2])
                qkv_jobs.append((t, mm, v2[:, 2 * i:2 * i + 2, b * M:b * M + M], v, 1.0))
        XD, Btok = blk(24, 4), blk(28)[:, 0, :]
        xd_tiles = [tile("v") for _ in range(4)]
        bt_tile = tile("a")
        ac_tile = tile("v")
        SEG = [blk(29)[:, 0, :], blk(30)[:, 0, :]]
        MM_ = [[blk(31)[:, 0, :], blk(32)[:, 0, :]], [blk(48)[:, 0, :], blk(49)[:, 0, :]]]
        ER = [blk(33)[:, 0, :], blk(34)[:, 0, :]]
        CT = [blk(35)[:, 0, :], blk(50)[:, 0, :]]
        XDD = [blk(22)[:, 0, :], blk(51)[:, 0, :]]
        SST = state[:, 0:4, :]
        yS = blk(36, 4)
        nssd = norm(yS, (h_hi[:, 0:4, :], h_lo[:, 0:4, :]), ("ssd_norm_g_2", 0), 4, S, 1)
        SP, WT = blk(24, 4), blk(28, 4)
        T1 = [blk(22)[:, 0, :], blk(23)[:, 0, :]]
        yB = blk(40, 4)
        nsb = norm(yB, (h_hi[:, 4:8, :], h_lo[:, 4:8, :]), ("sb_norm_g_2", 0), 4, S, 1)
        wout_jobs = residual(a["w_out_2"][0], hT, KC)
        n2b = norm(xT, hT, ("norm_xa_g_2", 0), KC, S, 1)
        qx = blk(0, 4)
        xq_jobs = []
        for b in range(2):
            w = columns(a["w_xq_2"][0], b * M, M)
            for c in range(2):
                t, mm, v = feature_tile(w, c * P, P, hT, "va"[c % 2])
                xq_jobs.append((t, mm, qx[:, 2 * b + c, :], v, P ** -0.5))
        att_stage["xa"] = [len(groups)]
        for h in range(XH):
            ob = bank[6 + h % 2]
            for i2 in range(2):
                group((8, 10, 12, 20), (14, 16, 18), slope=1.0, N=M, gates=None, first=None, ob=(i2 == 0),
                      units=[dict(q=qx[:, h, i * P:i * P + P], k=kxT[:, h, :], D=zeros[:, :], o=ob[:, i * P:i * P + P],
                                  start=True, v=[vx[:, t, h * P:h * P + P] for t in range(2)])
                             for i in (2 * i2, 2 * i2 + 1)],
                      evac=(ob, h) if i2 == 1 else None)
        att_stage["xa"].append(len(groups))
        wxo_jobs = residual(a["w_xo_2"][0], hT, 4)
        n2c = norm(xT, hT, ("norm_ff_g_2", 0), KC, S, 1)
        ff1_jobs = []
        for b in range(16):
            w = columns(a["w_ff1_2"][0], b * M, M)
            for c in range(2):
                t, mm, v = feature_tile(w, c * P, P, hT, "v")
                ff1_jobs.append((t, mm, 2 * b + c, v))
        ff2_halves = residual_split(a["w_ff2_2"][0], hid, FFT)
        yT = blk(36, 8)
        n2f = norm(xT, yT, ("final_g_2", 0), KC, S, 1)
        out_sb = blk(0, 4, D)
        out_tiles = [(tile("va"[i % 2]), i % TT, i // TT) for i in range(2 * TT)]

        nread = 0
        for halves in (ffn[0][2], ffn[1][2], ff2_halves):
            for hf, ts, ps, h in halves:
                for w, k0, kk in ps:
                    if w is ps[-1][0]:
                        until_tile(w, ts[-1])
                    else:
                        nread += 1
                        w["read"] = (panel_read, nread)

        def read_out(eng, ts):
            for e, s_ in (("v", evac_v), ("a", evac_a)):
                n = [t.order for t in ts if t.eng == e]
                if n:
                    eng.wait_ge(s_, max(n) + 1)

        def done(t):
            return evac_v if t.eng == "v" else evac_a

        def splits_until(m, now):
            while m >= len(splits):
                m -= 1
            while m > now and splits[m]["n"] - splits[now]["n"] != m - now:
                m -= 1
            return m

        def chained(eng, s_):
            n = [0]

            def link(ins):
                n[0] += 1
                ins.then_inc(s_, 1)
                eng.wait_ge(s_, n[0])
            return link

        RC_T = Steps(rc_t, "ga", "gk", "tokb", "tokk", "tokv", "eye",
                     *[f"{x}{l}{h}" for l in range(1, 6) for x in "yt" for h in range(2)])
        RC_V = Steps(rc_v, "ga", "gk", "t0", *[f"t{l}{h}" for l in range(1, 6) for h in range(2)])
        RC_A = Steps(rc_a, "tokb", "tokk", "tokv", *[f"y{l}{h}" for l in range(1, 6) for h in range(2)])
        RS_T = Steps(rs_t, "x", "u", "y", "s")
        RS_V = Steps(rs_v, "x", "y", "s")
        SF_T = Steps(sf_t, "y", "st")
        SC_V = Steps(sc_v, "seg", "m")
        SF_V = Steps(sf_v, "y", "st")
        SC_A = Steps(sc_a, "er", "e")
        jobs_of = lambda jobs: [j[0] for j in jobs]

        block = ctx.enter_context(nc.Block())

        @block.sync
        def _(sp):
            for p in panels:
                if p is mem_panel:
                    sp.wait_ge(rows_clear, 1)
                    for dst, src in vec_dmas:
                        sp.dma_start(dst, src).then_inc(vec_in, 16)
                if p["n"] >= NSLOT:
                    sp.wait_ge(*panels[p["n"] - NSLOT]["until"])
                for dst, src in p["parts"]:
                    sp.dma_start(dst, src).then_inc(landed[p["slot"]], 16)
            o = out.rearrange("z (t p) d -> p (z t) d", p=P)
            for tt in range(TT):
                read_out(sp, [t for t, tt_, _ in out_tiles if tt_ == tt])
                sp.dma_start(o[:, tt, :], out_sb[:, tt, :]).then_inc(out_sent, 16)
            sp.wait_ge(out_sent, 16 * TT)

        @block.gpsimd
        def _(pool):
            link = chained(pool, chain_p)
            ms = nc.gpsimd.memset
            aff = nc.gpsimd.affine_select

            def fill(t, value, *conds):
                link(ms(t, value))
                for pat, base, cm, other in conds:
                    link(aff(out=t, in_=t, compare_op=ALU.is_ge, fill=other, base=base, pattern=pat, channel_multiplier=cm))

            link(ms(ident[:], 0.0))
            link(aff(out=ident[:], in_=ident[:], compare_op=ALU.not_equal, fill=1.0, base=0, pattern=[[-1, P]],
                     channel_multiplier=1))
            pool.nop().then_inc(ident_ready, 1)
            link(ms(rows[:], 0.0))
            pool.nop().then_inc(rows_clear, 1)
            link(ms(ones[:], 1.0))
            link(ms(nones[:], -1.0))
            for i, e in enumerate((EPS1, EPS2, EPS_GN, 1.0, 1e-24)):
                link(ms(eps[:, i:i + 1], e))
            for gp in range(2):
                for r in range(3):
                    for gg in range(2):
                        h = 3 * (2 * gp + gg) + r
                        x = 6 * gg + 3 * gp + r
                        link(ms(cslope[:, x:x + 1], slopes[h]))
                        link(ms(qscale[gg * HD:gg * HD + HD, gp * 3 + r:gp * 3 + r + 1], HD ** -0.5 / slopes[h]))
            pool.nop().then_inc(consts, 1)
            link(ms(zeros[:], 0.0))
            link(ms(blockones[:], 0.0))
            for hf in range(2):
                s_ = slice(hf * HD, hf * HD + HD)
                link(ms(blockones[s_, s_], 1.0))
                link(ms(eye2[s_, :], 0.0))
                link(aff(out=eye2[s_, :], in_=eye2[s_, :], compare_op=ALU.not_equal, fill=1.0, base=0,
                         pattern=[[-1, HD]], channel_multiplier=1))
                fill(causal[s_, 0:HD], 1.0, ([[1, HD]], -1, -1, 0.0))
                fill(causal[s_, HD:P], 1.0, ([[1, HD]], 0, -1, 0.0))
                for l in range(6):
                    m = 1 << l
                    nb = HD // (2 * m)
                    v = level[s_, l, :].rearrange("p (b o w) -> p b o w", b=nb, o=2)
                    link(ms(level[s_, l, :], 0.0))
                    link(ms(v[:, :, 1, :], 1.0))
                    for pat, base, cm in (([[-2 * m, nb], [0, m]], 0, 1), ([[2 * m, nb], [0, m]], m - 1, -1)):
                        link(aff(out=v[:, :, 1, :], in_=v[:, :, 1, :], compare_op=ALU.is_ge, fill=0.0, base=base,
                                 pattern=pat, channel_multiplier=cm))
            link(nc.gpsimd.iota(dist[:], pattern=[[1, S]], base=-(S - P), channel_multiplier=-1,
                                allow_small_or_imprecise_dtypes=True))
            link(aff(out=dist[:], in_=dist[:], compare_op=ALU.is_ge, fill=NEG, base=S - P, pattern=[[-1, S]],
                     channel_multiplier=1))
            link(nc.gpsimd.iota(distc[:], pattern=[[-P, TT], [CS, NCMP]], base=CB - 1, channel_multiplier=-1,
                                allow_small_or_imprecise_dtypes=True))
            link(aff(out=distc[:], in_=distc[:], compare_op=ALU.is_ge, fill=NEG, base=-(CB - 1),
                     pattern=[[P, TT], [-CS, NCMP]], channel_multiplier=1))
            fill(triu[:], 1.0, ([[1, P]], 0, -1, 0.0))
            link(ms(state[:], 0.0))
            pool.nop().then_inc(consts, 1)
            pool.wait_ge(att_max, att_stage["nsa"][1])
            link(ms(keep[:], 1.0))
            link(ms(keep[:, 0:S:CH], 0.0))
            pool.nop().then_inc(consts, 1)
            for c in range(NCH):
                pool.wait_ge(rc_v, RC_V.at("ga", c))
                if c:
                    pool.wait_ge(rc_t, RC_T.at("y51", c - 1))
                for l in range(6):
                    if l == NALT:
                        pool.wait_ge(rc_v, RC_V.at("t0", c))
                    if l >= NALT:
                        pool.wait_ge(rc_t, RC_T.at(("eye", "y11", "y21")[l - NALT], c))
                    nc.gpsimd.tensor_tensor(jn(ALT[:, l % NALT, :]), GA[c % 2][:, :, 0:HD],
                                            level[:, l:l + 1, :].broadcast_to([P, JP, HD]), ALU.mult).then_inc(rc_p, 1)
            pool.wait_ge(rc_p, 6 * NCH)
            fill(triu_s, 1.0, ([[1, P]], -1, -1, 0.0))
            fill(ntril, -1.0, ([[-1, P]], 0, 1, 0.0))
            fill(hide_gt, 0.0, ([[1, P]], 0, -1, NEG))
            fill(hide_ge, 0.0, ([[1, P]], -1, -1, NEG))
            pool.nop().then_inc(consts, 1)
            read_out(pool, xd_tiles)
            pool.wait_ge(sd_a, 2)
            for c in range(TT):
                cs = slice(c * P, c * P + P)
                if c >= 2:
                    pool.wait_ge(sf_t, SF_T.at("st", c - 2))
                nc.gpsimd.tensor_tensor(XDD[c % 2].rearrange("p (h d) -> p h d", h=8), XD[:, c, :].rearrange("p (h d) -> p h d", h=8),
                                        small[:, 3, c * 8:c * 8 + 8].unsqueeze(2).broadcast_to([P, 8, HD]),
                                        ALU.mult).then_inc(ssd_xdd, 1)
                pool.wait_ge(ssd_xdd, c + 1)
                pool.wait_ge(sc_a, SC_A.at("er", c))
                for g in range(2):
                    gs = slice(g * HD, g * HD + HD)
                    last = nc.gpsimd.tensor_tensor(CT[c % 2][gs, :].rearrange("p (h l) -> p h l", h=4),
                                                   ER[g][gs, :].rearrange("p (h l) -> p h l", h=4),
                                                   xbc[gs, 5, cs].unsqueeze(1).broadcast_to([HD, 4, P]), ALU.mult)
                last.then_inc(ssd_ct, 1)
                pool.wait_ge(ssd_ct, c + 1)

        @block.tensor
        def _(pe):
            mm = nc.tensor.matmul
            seen = set()

            def opened(t):
                if t.n >= NBANK:
                    read_out(pe, [tiles[t.n - NBANK]])

            def arrived(w):
                if w["n"] not in seen:
                    seen.add(w["n"])
                    if "m" in w:
                        pe.wait_ge(split_lo, w["m"] + 1)
                    else:
                        pe.wait_ge(landed[w["slot"]], w["level"])

            def products(t, sums, nm=None):
                opened(t)
                for v, prods in sums:
                    for i, p in enumerate(prods):
                        if p[2] is not None:
                            arrived(p[2])
                        if nm is not None and (nm["j"], p[3]) not in seen:
                            seen.add((nm["j"], p[3]))
                            if p[3] < nm["k"]:
                                pe.wait_ge(nm.get("sem", normed), nm["c"] + p[3] + 1)
                        last = mm(v, p[0], p[1], start=(i == 0), stop=(i == len(prods) - 1))
                last.then_inc(acc_full, 1)

            def turned(t, views):
                opened(t)
                for v, src in views:
                    last = nc.tensor.transpose(v, src, ident[0:src.shape[0], 0:src.shape[0]])
                last.then_inc(acc_full, 1)

            def norm_sum(nm, ks=None):
                for k in (range(nm["k"]) if ks is None else ks):
                    pe.wait_ge(squared, nm["b"] + k + 1)
                    mm(bank[4][:, 0:nm["n"]], ones[:], ntmp[:, k % 2, 0:nm["n"]], start=(k == 0),
                       stop=(k == nm["k"] - 1)).then_inc(norm_part, 1)

            def gemm(jobs, nm=None, then=None):
                for n, j in enumerate(jobs):
                    products(j[0], j[1], nm)
                    if then is not None and n:
                        norm_sum(then, [n - 1])
                if then is not None:
                    norm_sum(then, [len(jobs) - 1])

            def split_sum(halves, h0, then):
                for hf, ts, ps, h in halves:
                    for t in ts:
                        opened(t)
                    for w, k0, kk in ps:
                        arrived(w)
                        if hf == 0:
                            pe.wait_ge(hid_lo, h0 + k0 + kk)
                        for c, t in enumerate(ts):
                            for k in range(kk):
                                for i, (a_, b_) in enumerate((("hi", 0), ("hi", 1), ("lo", 0))):
                                    last = mm(bank[t.bank][:], w[a_][:, k, c * P:c * P + P], h[b_][:, k0 + k, :],
                                              start=(k0 + k == 0 and i == 0), stop=(w is ps[-1][0] and k == kk - 1 and i == 2))
                            if w is ps[-1][0]:
                                last.then_inc(acc_full, 1)
                        if w is not ps[-1][0]:
                            last.then_inc(panel_read, 1)
                        if hf == 1 and w is ps[0][0]:
                            norm_sum(then, range(4))
                norm_sum(then, range(4, 8))

            def scored(o, q, k):
                if not isinstance(q, list):
                    return mm(o, q, k, start=True, stop=True)
                mm(o, q[0], k[0], start=True, stop=False)
                mm(o, q[0], k[1], start=False, stop=False)
                return mm(o, q[1], k[0], start=False, stop=True)

            def attention(name):
                g0, g1 = att_stage[name]

                def scores(g):
                    n = g["n"]
                    if n >= 2:
                        pe.wait_ge(att_exp, n - 1)
                    for w, u in enumerate(g["units"]):
                        last = scored(g["s"][w][:, 0:g["N"]], u["q"], u["k"])
                    last.then_inc(att_scores, 1)

                def turn(g):
                    n = g["n"]
                    pe.wait_ge(att_weight, n + 1)
                    if n:
                        pe.wait_ge(att_copied, n)
                    for w in range(2):
                        for t in range(g["N"] // P):
                            last = nc.tensor.transpose(bank[4 + w][:, t * P:t * P + P], g["P"][w][:, t * P:t * P + P], ident[:])
                    last.then_inc(att_turned, 1)

                def values(g):
                    n = g["n"]
                    pe.wait_ge(att_copied, n + 1)
                    if g["ob"] and g["out0"] >= 2:
                        pe.wait_ge(att_out, g["out0"] - 1)
                    more = dict(skip_group_check=True)
                    if g["first"] is not None:
                        mm(*g["first"], start=True, stop=False, **more)
                    for w, u in enumerate(g["units"]):
                        for t, v in enumerate(u["v"]):
                            last = mm(u["o"], v, g["PT"][w][:, t * P:t * P + P], start=(u["start"] and t == 0),
                                      stop=(t == len(u["v"]) - 1), **more)
                    last.then_inc(att_pv, 1)

                for i in range(g0, g1 + TO_VALUES):
                    if i < g1:
                        scores(groups[i])
                    if i - TO_VALUES >= g0:
                        values(groups[i - TO_VALUES])
                    if g0 <= i - TO_TURN < g1:
                        turn(groups[i - TO_TURN])

            pe.wait_ge(ident_ready, 1)
            arrived(x_panels[0])
            arrived(x_panels[1])
            for k, t in enumerate(x_tiles):
                turned(t, [(bank[t.bank][:, tt * P:tt * P + P], x_panels[tt // 2]["v"][:, tt % 2, k * P:k * P + P]) for tt in range(TT)])
            pe.wait_ge(vec_in, 16 * len(vec_dmas))
            vb = bank[vec_tile.bank]
            turned(vec_tile, [(vb[:, 0:P], rows[:, 0, :]), (vb[:, P:2 * P], rows[:, 1, :]),
                              (vb[:, POS:POS + 2 * CS], rows[0:2 * CS, 2, :])])
            pe.wait_ge(consts, 1)
            arrived(mem_panel)
            for k, t in enumerate(mem_tiles):
                turned(t, [(bank[t.bank][:, (2 * kk + tt) * P:(2 * kk + tt) * P + P],
                            mem_panel["v"][:, tt, (2 * k + kk) * P:(2 * k + kk) * P + P]) for kk in range(2) for tt in range(2)])
            for l in range(2):
                norm_sum(mem_norm[l])
                gemm(mem_jobs[l], mem_norm[l])
            norm_sum(n1a)
            gemm(cmp_jobs, n1a)
            pe.wait_ge(cols_ready, 1)
            for j in range(2):
                w, t = cmp_panels[j], cmp_hid[j]
                opened(t)
                arrived(w)
                read_out(pe, jobs_of(cmp_jobs[2 * j:2 * j + 2]))
                for l in range(CS):
                    mm(bank[t.bank][:, 0:G1 * NCMP].rearrange("p (g n) -> p g n", g=G1), w["v"][:, l, :],
                       cmp_src[j][:, :, l:l + CS * (NCMP - 1) + 1:CS], start=(l == 0), stop=(l == CS - 1))
                for l in range(CS):
                    last = mm(bank[t.bank][:, 200:201], w["v"][:, l, :],
                              cols[:, POS + j * CS + l:POS + j * CS + l + 1], start=(l == 0), stop=(l == CS - 1))
                last.then_inc(acc_full, 1)
            gemm(nsa_jobs)
            gemm([gate_job])
            if upto == "nsa":
                return
            read_out(pe, jobs_of(nsa_jobs))
            for j in range(2):
                t = cmp_res[j]
                opened(t)
                pe.wait_ge(gelu_out, j + 1)
                hv = chid[:, j, :].rearrange("p (c b n) -> p c b n", b=2, c=2)
                if j == 0:
                    for b in range(2):
                        last = mm(bank[t.bank][b * HD:b * HD + HD, 0:2 * NCMP].rearrange("p (c n) -> p c n", c=2),
                                  cmp_w2[:, 0, :], hv[:, :, b, :], start=True, stop=True)
                else:
                    for g in range(G1):
                        last = mm(bank[t.bank][0:NCMP, g * HD:g * HD + HD], hv[:, g // 2, g % 2, :], cmp_w2[:, 1, :],
                                  start=True, stop=True)
                last.then_inc(acc_full, 1)
            read_out(pe, cmp_res)
            pe.wait_ge(consts, 2)
            pe.wait_ge(kcb_split, 1)
            for i in range(TT):
                for e in range(2):
                    for x, h in enumerate(cmp_heads[e]):
                        hs = slice(e * HD, e * HD + HD)
                        last = scored(bank[2 * i + e][:, x * NCMP:x * NCMP + NCMP],
                                      [q[hs, pair(h), i * P:i * P + P] for q in qT], [k[hs, h // 6, :] for k in kcb_parts])
            last.then_inc(cmp_s, 1)
            pe.wait_ge(cmp_w, 1)
            for x in range(H1):
                if x >= 8:
                    pe.wait_ge((cmp_pt, cmp_ptv)[x % 2], (x - 8) // 2 + 1)
                for i in range(TT):
                    last = nc.tensor.transpose(bank[x % 8][0:NCMP, i * P:i * P + P], CU[:, i * H1 + x, :], ident[:])
                last.then_inc(cmp_t, 1)
            pe.wait_ge(cmp_pt, 6)
            pe.wait_ge(cmp_ptv, 6)
            attention("nsa")
            pe.wait_ge(att_out, groups[att_stage["nsa"][1] - 1]["out0"] + 1)
            gemm(wo_jobs[0], then=ffn[0][0])

            def swiglu_pe(f):
                nm, jobs, halves, h0, then = f
                for g_, u_, j in jobs:
                    products(g_[0], g_[1], nm)
                    products(u_[0], u_[1])
                split_sum(halves, h0, then)

            if upto == "wo0":
                return
            swiglu_pe(ffn[0])
            if upto == "l0":
                return
            gemm(shift_jobs, n1b)
            gemm(qm1_jobs)
            read_out(pe, jobs_of(qm1_jobs))
            read_out(pe, jobs_of(shift_jobs[-4:]))
            attention("mem1")
            arrived(lora_panels[0])
            arrived(lora_panels[1])
            pe.wait_ge(lora_in, 2)
            for j in range(JP + 2):
                if j < JP:
                    t = rp_tiles[j]
                    s_ = slice(j * P, j * P + P)
                    b_ = lambda n: bank[t[n].bank][:]
                    products(t["w"], [(b_("w"), [(lw[0:64, s_], lo[0:64, :], None)])])
                    products(t["a"], [(b_("a"), [(lw[64:128, s_], lo[64:128, :], None)])])
                    products(t["g"], [(b_("g"), [(lw[:, MIX + j * P:MIX + j * P + P], lo2, None),
                                                 (lw2[0:32, j * P:j * P + P], lo3[0:32, :], None)])])
                if j >= 2:
                    t = rp_tiles[j - 2]["b"]
                    pe.wait_ge(rp_rk, j - 1)
                    products(t, [(bank[t.bank][:], [(blockones[:], tmp[j % 2][4], None)])])
                if j < JP:
                    t = rp_tiles[j]["n"]
                    pe.wait_ge(rp_square, j + 1)
                    products(t, [(bank[t.bank][:], [(blockones[:], tmp[j % 2][3], None)])])
            if upto == "rp":
                return
            read_out(pe, [rp_tiles[-1]["b"]])
            pe.wait_ge(rp_done, JP)
            halves2 = [slice(0, HD), slice(HD, P)]

            def small_mm(out_bank, lf, rf, pairs=range(JP), j0=0, c0=0):
                for j in pairs:
                    for hs in halves2:
                        o = c0 + (j - j0) * HD
                        last = mm(out_bank[hs, o:o + HD], lf(hs, j), rf(hs, j), start=True, stop=True)
                return last

            AR = arena[:, 0:24 * S].rearrange("p (w j t) -> p w j t", w=4, j=6)
            half = [range(0, 3), range(3, 6)]
            Tg = lambda w_: (lambda hs, j: T2[hs, j // 3, w_, j % 3 * HD:j % 3 * HD + HD])

            def gram(c, name, src, b0):
                for j in range(JP):
                    for hs in halves2:
                        o = bank[b0 + j // 3][hs, (j % 3) * P:(j % 3) * P + P]
                        cs = slice(c * CH, c * CH + CH)
                        mm(o[:, 0:HD], src[hs, j, cs], AR[hs, 3, j, cs], start=True, stop=True)
                        last = mm(o[:, HD:P], src[hs, j, cs], AR[hs, 0, j, cs], start=True, stop=True)
                last.then_inc(rc_t, 1)

            def tok(c, src, b_):
                cs = slice(c * CH, c * CH + CH)
                small_mm(b_, lambda hs, j: src[hs, j, cs], lambda hs, j: ident[hs, hs]).then_inc(rc_t, 1)

            for c in range(NCH + 1):
                prep, d = c < NCH, c - 1
                e = d % 2
                ds = slice(d * CH, d * CH + CH)
                if d >= 0:
                    pe.wait_ge(rc_a, RC_A.at("tokv", d))
                    if d:
                        pe.wait_ge(rs_v, RS_V.at("s", d - 1))
                    for j in range(JP):
                        for hs in halves2:
                            o = bank[6][hs, j * HD:j * HD + HD]
                            mm(o, GK[e][hs, j, 0:HD], VT[e][hs, j, :], start=True, stop=False)
                            last = mm(o, kkT[hs, j, ds], state[hs, j, :], start=False, stop=True)
                    last.then_inc(rs_t, 1)
                if prep:
                    gram(c, "ga", bT, 0)
                if d >= 0:
                    pe.wait_ge(rs_v, RS_V.at("x", d))
                    pe.wait_ge(rc_v, RC_V.at("t51", d))
                    small_mm(bank[7], lambda hs, j: TTf[e][hs, j, :], lambda hs, j: Xm[hs, j, :]).then_inc(rs_t, 1)
                if prep:
                    gram(c, "gk", kT7, 2)
                if d >= 0:
                    pe.wait_ge(rs_a, d + 1)
                    for j in range(JP):
                        for hs in halves2:
                            o = bank[6][hs, j * HD:j * HD + HD]
                            mm(o, state[hs, j, :], rT[hs, j, ds], start=True, stop=False)
                            mm(o, VT[e][hs, j, :], GK[e][hs, j, HD:P], start=False, stop=False)
                            last = mm(o, Um[hs, j, :], GA[e][hs, j, HD:P], start=False, stop=True)
                    last.then_inc(rs_t, 1)
                if prep:
                    tok(c, bT, bank[4])
                    tok(c, kT7, bank[5])
                if d >= 0:
                    for j in range(JP):
                        for hs in halves2:
                            o = bank[7][hs, j * HD:j * HD + HD]
                            mm(o, KT[e][hs, j, :], VT[e][hs, j, :], start=True, stop=False)
                            last = mm(o, BT[e][hs, j, :], Um[hs, j, :], start=False, stop=True)
                    last.then_inc(rs_t, 1)
                if not prep:
                    break
                pe.wait_ge(rc_a, RC_A.at("tokb", c))
                tok(c, vT7, bank[4])
                Al = lambda l: (lambda hs, j: ALT[hs, l % NALT, j * HD:j * HD + HD])
                pe.wait_ge(rc_a, RC_A.at("tokk", c))
                pe.wait_ge(rc_p, 6 * c + 1)
                small_mm(bank[5], Al(0), lambda hs, j: eye2[hs, :]).then_inc(rc_t, 1)
                for l in range(1, 6):
                    pe.wait_ge(rc_p, 6 * c + l + 1)
                    for h in range(2):
                        pe.wait_ge(rc_v, RC_V.at(f"t{l - 1}{h}" if l > 1 else "t0", c))
                        small_mm(bank[h], Al(l), Tg(0), half[h], 3 * h).then_inc(rc_t, 1)
                    for h in range(2):
                        Y = lambda hs, j: Ym[hs, j, :]
                        pe.wait_ge(rc_a, RC_A.at(f"y{l}{h}", c))
                        if l < 5:
                            small_mm(bank[2 + h], Tg(1), Y, half[h], 3 * h)
                        small_mm(bank[2 + h], Y, Tg(1), half[h], 3 * h, 192).then_inc(rc_t, 1)
            pe.wait_ge(rs_v, RS_V.at("y", NCH - 1))
            gn_sum = lambda t, v: products(t, [(bank[t.bank][:], [(blockones[:], v, None)])])
            gn_sum(gn_tiles[0]["s"], rT[:, 0, :])
            for j in range(JP):
                if j + 1 < JP:
                    gn_sum(gn_tiles[j + 1]["s"], rT[:, j + 1, :])
                pe.wait_ge(gn_square, j + 1)
                gn_sum(gn_tiles[j]["q"], gtmp[j][0])
            pe.wait_ge(att_out, groups[att_stage["mem1"][1] - 1]["out0"] + 1)
            if upto == "gn":
                return
            gemm(wo_jobs[1], dict(j="gn", c=0, k=JP, sem=gn_lo), then=ffn[1][0])
            swiglu_pe(ffn[1])
            arrived(mem2_panel)
            for k, t in enumerate(mem2_tiles):
                turned(t, [(bank[t.bank][:, (2 * kk + tt) * P:(2 * kk + tt) * P + P],
                            mem2_panel["v"][:, tt, (2 * k + kk) * P:(2 * k + kk) * P + P]) for kk in range(2) for tt in range(2)])
            norm_sum(mem2_norm)
            gemm(mem2_jobs, mem2_norm)
            norm_sum(n2a)
            if upto == "b1":
                return
            gemm(z_jobs, n2a)
            gemm(conv_jobs)
            gemm([dt_job])
            gemm(qkv_jobs)
            pe.wait_ge(conv_a, 12)
            for c, t in enumerate(xd_tiles):
                turned(t, [(bank[t.bank][:, k * P:k * P + P], xbc[:, k, c * P:c * P + P]) for k in range(4)])
            turned(bt_tile, [(bank[bt_tile.bank][:, c * P:c * P + P], xbc[:, 4, c * P:c * P + P]) for c in range(4)])
            pe.wait_ge(sd_v, 1)
            opened(ac_tile)
            mm(bank[ac_tile.bank][:, 0:32], triu[:], small[:, 1, :], start=True, stop=True)
            mm(bank[ac_tile.bank][:, 32:64], ones[:], small[:, 1, :], start=True, stop=True).then_inc(acc_full, 1)
            read_out(pe, xd_tiles + [bt_tile])
            pe.wait_ge(sd_v, 2)
            read_out(pe, [ac_tile])
            def ssd_rows(c):
                cs = slice(c * P, c * P + P)
                if c:
                    pe.wait_ge(sc_v, SC_V.at("m", c - 1))
                for h in range(SH):
                    mm(bank[4 + h // 4][:, (h % 4) * P:(h % 4) * P + P],
                       small[:, 1, c * 8 + h:c * 8 + h + 1].broadcast_to([P, P]), triu[:], start=True, stop=True)
                for g in range(SG):
                    gs = slice(g * HD, g * HD + HD)
                    last = mm(bank[(6, 2)[g]][:, 0:P], xbc[gs, 4, cs], xbc[gs, 5, cs], start=True, stop=True)
                last.then_inc(sc_t, 1)

            ssd_rows(0)
            for c in range(TT):
                if c + 1 < TT:
                    ssd_rows(c + 1)
                pe.wait_ge(sc_v, SC_V.at("m", c))
                pe.wait_ge(ssd_ct, c + 1)
                if c:
                    pe.wait_ge(sf_v, SF_V.at("st", c - 1))
                for h in range(SH):
                    g = h // 4
                    gs = slice(g * HD, g * HD + HD)
                    o = bank[(7, 1)[g]][(h % 2) * HD:(h % 2) * HD + HD, (h // 2 % 2) * P:(h // 2 % 2) * P + P]
                    last = mm(o, XD[:, c, h * HD:h * HD + HD], MM_[c % 2][g][:, (h % 4) * P:(h % 4) * P + P], start=True, stop=(c == 0))
                    if c:
                        last = mm(o, SST[gs, h % 4, :], CT[c % 2][gs, (h % 4) * P:(h % 4) * P + P], start=False, stop=True)
                last.then_inc(sf_t, 1)
                pe.wait_ge(ssd_xdd, c + 1)
                for g in range(SG):
                    last = mm(bank[3][g * HD:g * HD + HD, 0:256], Btok[:, c * P + g * HD:c * P + g * HD + HD],
                              XDD[c % 2][:, g * 256:g * 256 + 256], start=True, stop=True)
                last.then_inc(sf_t, 1)
            pe.wait_ge(sf_v, SF_V.at("st", TT - 1))
            norm_sum(nssd)
            read_out(pe, jobs_of(qkv_jobs))
            nu = 4 * SH
            pe.wait_ge(consts, 4)
            pe.wait_ge(rooted, nssd["j"] + 1)

            def logits(u):
                h, js = u // 4, 3 - u % 4
                hs = slice((h % 2) * HD, (h % 2) * HD + HD)
                if u >= 3:
                    pe.wait_ge(sb_weight, u - 2)
                mm(bank[4 + u % 3][:, js * P:S], k2[hs, h // 2, js * P:js * P + P], q2[hs, h // 2, js * P:S],
                   start=True, stop=True).then_inc(sb_logits, 1)

            def later(u):
                h, js = u // 4, 3 - u % 4
                b_ = bank[4 + u % 3]
                pe.wait_ge(sb_soft, u + 1)
                more = dict(start=False, stop=False, skip_group_check=True)
                mm(b_[:, js * P:js * P + P], ident[:], hide_ge, **more)
                for jj in range(js + 1, 4):
                    mm(b_[:, jj * P:S], nones[:], SP[:, jj, jj * P:S], **more)
                more["stop"] = True
                mm(b_[:, js * P:S], ntril, SP[:, js, js * P:S], **more).then_inc(sb_sums, 1)

            def sb_values(h):
                pe.wait_ge(sb_weight, 4 * h + 4)
                if h >= 2 and h % 2 == 0:
                    pe.wait_ge(sb_out, h // 2)
                for js in range(4):
                    last = mm(bank[7][(h % 2) * HD:(h % 2) * HD + HD, js * P:S], v2[:, js, h * HD:h * HD + HD],
                              WT[:, js, js * P:S], start=(js == 0), stop=(js == 3))
                last.then_inc(sb_pv, 1)

            logits(0)
            for u in range(nu):
                if u + 1 < nu:
                    logits(u + 1)
                later(u)
                if u % 4 == 0 and u:
                    sb_values(u // 4 - 1)
            sb_values(SH - 1)
            norm_sum(nsb)
            if upto == "sb":
                return
            gemm(wout_jobs, dict(j="y", c=nsb["c"] - 4, k=KC), then=n2b)
            gemm(xq_jobs, n2b)
            read_out(pe, jobs_of(xq_jobs))
            attention("xa")
            pe.wait_ge(att_out, nout[0])
            gemm(wxo_jobs, then=n2c)
            gemm(ff1_jobs, n2c)
            split_sum(ff2_halves, 2 * FT, n2f)
            for t, tt, kh in out_tiles:
                pe.wait_ge(scaled, n2f["b"] + 4 * kh + 4)
                turned(t, [(bank[t.bank][:, k * P:k * P + P], yT[:, kh * 4 + k, tt * P:tt * P + P]) for k in range(4)])

        @block.scalar
        def _(act):
            A = nc.scalar.activation
            link = chained(act, chain_a)
            at = [0]

            def split_to(m):
                while at[0] <= m:
                    w = splits[at[0]]
                    act.wait_ge(landed[w["slot"]], w["level"])
                    if at[0] >= NSPLIT:
                        act.wait_ge(*splits[at[0] - NSPLIT]["read"])
                    A(w_hi[:, at[0] % NSPLIT, 0:w["size"]], wring[:, w["slot"], 0:w["size"]], ACT.Copy).then_inc(split_hi, 1)
                    at[0] += 1

            def tile_in(t):
                if t.split is not None:
                    split_to(splits_until(t.split + AHEAD, t.split))
                act.wait_ge(acc_full, t.n + 1)

            def copy_out(t, dst, v, scale=1.0):
                tile_in(t)
                A(dst, v, ACT.Copy if isinstance(scale, float) else ACT.Identity, scale=scale).then_inc(evac_a, 1)

            def norm_root(nm, ready=None):
                n = nm["n"]
                if nm["c"]:
                    act.wait_ge(normed, nm["c"])
                for k in range(nm["k"]):
                    if ready is not None:
                        ready(k)
                    if k >= 2:
                        act.wait_ge(norm_part, nm["b"] + k - 1)
                    A(ntmp[:, k % 2, 0:n], nm["src"][:, k, 0:n], ACT.Square).then_inc(squared, 1)
                act.wait_ge(norm_part, nm["b"] + nm["k"])
                if nm["b"]:
                    act.wait_ge(scaled, nm["b"])
                link(A(rsb[:, 0:n], bank[4][:, 0:n], ACT.Ln, scale=1.0 / (nm["k"] * P), bias=eps[:, nm["eps"]:nm["eps"] + 1]))
                A(rsb[:, 0:n], rsb[:, 0:n], ACT.Exp, scale=-0.5).then_inc(rooted, 1)
                if isinstance(nm["dst"], tuple):
                    for k in range(nm["k"]):
                        act.wait_ge(scaled, nm["b"] + k + 1)
                        A(nm["dst"][0][:, k, 0:n], ntmp[:, k % 2, 0:n], ACT.Copy).then_inc(cast, 1)

            def added(jobs):
                def ready(k):
                    t = jobs[k][0]
                    split_to(splits_until(t.split + AHEAD, t.split))
                    act.wait_ge(evac_v, t.order + 1)
                return ready

            def added_split(halves):
                def ready(k):
                    if k % 4 == 0:
                        for w, _, _ in halves[k // 4][2]:
                            split_to(splits_until(w["m"] + AHEAD, w["m"]))
                    act.wait_ge(evac_v, halves[k // 4][1][k % 4].order + 1)
                return ready

            def plain(jobs):
                for t, _, dst, v, sc in jobs:
                    split_to(splits_until(t.split + AHEAD, t.split))
                    if isinstance(dst, list):
                        tile_in(t)
                        A(dst[0], v, ACT.Copy if isinstance(sc, float) else ACT.Identity, scale=sc).then_inc(qk_hi, 1)
                    elif t.eng == "a":
                        copy_out(t, dst, v, sc)

            def attention(name):
                g0, g1 = att_stage[name]

                def probs(g):
                    n = g["n"]
                    if n >= 4:
                        act.wait_ge(att_turned, n - 3)
                    act.wait_ge(att_max, n + 1)
                    for w in range(2):
                        last = A(g["P"][w][:, 0:g["N"]], g["s"][w][:, 0:g["N"]], ACT.Exp, scale=g["slope"],
                                 bias=g["st"][:, 1, w:w + 1], accum_out=g["st"][:, 2, w:w + 1])
                    last.then_inc(att_exp, 1)

                def copy(g):
                    n = g["n"]
                    act.wait_ge(att_turned, n + 1)
                    if n >= 3:
                        act.wait_ge(att_pv, n - 2)
                    for w in range(2):
                        last = A(g["PT"][w][:, 0:g["N"]], bank[4 + w][:, 0:g["N"]], ACT.Copy)
                    last.then_inc(att_copied, 1)

                def output(g):
                    if g["evac"] is not None:
                        act.wait_ge(att_pv, g["n"] + 1)
                        A(h_hi[:, g["evac"][1], :], g["evac"][0][:], ACT.Copy).then_inc(att_hi, 1)

                for i in range(g0, g1 + TO_VALUES):
                    if i < g1:
                        probs(groups[i])
                    if g0 <= i - TO_TURN < g1:
                        copy(groups[i - TO_TURN])
                    if i - TO_VALUES >= g0:
                        output(groups[i - TO_VALUES])

            def exp_ln():
                nc.scalar.preload_act_table_set("natural_log_exp_and_others")

            def spread(jobs):
                for t, _, dst, v, c in jobs:
                    split_to(splits_until(t.split + AHEAD, t.split))
                    if t.eng == "a":
                        tile_in(t)
                        for g in range(2):
                            gs = slice(g * HD, g * HD + HD)
                            A(dst[0:HD, 2 * c + g, :], v[gs, :], ACT.Copy)
                            last = A(dst[HD:P, 2 * c + g, 0:S - CS], v[gs, CS:S], ACT.Copy)
                        last.then_inc(evac_a, 1)

            exp_ln()
            for k, t in enumerate(x_tiles):
                if t.eng == "a":
                    copy_out(t, xT[:, k, :], bank[t.bank][:])
            for k, t in enumerate(mem_tiles):
                if t.eng == "a":
                    copy_out(t, memT[:, 2 * k:2 * k + 2, :], bank[t.bank][:].rearrange("p (k m) -> p k m", k=2))
            read_out(act, mem_tiles + x_tiles)
            split_to(splits_until(AHEAD, 0))
            for l in range(2):
                if l:
                    read_out(act, jobs_of(mem_jobs[0]))
                norm_root(mem_norm[l])
                plain(mem_jobs[l])
            norm_root(n1a)
            spread(cmp_jobs)
            split_to(nsa_jobs[0][0].split)
            for j in range(2):
                act.wait_ge(gelu_in, j + 1)
                A(ctmp[:], ctmp[:], ACT.Exp, scale=-2.0 * math.sqrt(2.0 / math.pi)).then_inc(gelu_exp, 1)
            plain(nsa_jobs)
            split_to(splits_until(gate_job[0].split + AHEAD, gate_job[0].split))
            act.wait_ge(gate_exp_in, 1)
            A(gates[:], gates[:], ACT.Exp, scale=-1.0).then_inc(gate_exp, 1)
            if upto == "nsa":
                return
            act.wait_ge(cmp_u, 1)
            A(CU[:], CU[:], ACT.Exp).then_inc(cmp_e, 1)
            for x in range(0, H1, 2):
                act.wait_ge(cmp_t, x + 1)
                A(PTc[0:NCMP, cmp_head(x), :], bank[x % 8][0:NCMP, :], ACT.Copy).then_inc(cmp_pt, 1)
            m = wo_jobs[0][0][0].split
            split_to(splits_until(m + AHEAD, m))
            attention("nsa")

            def hidden(j, h0, tile_):
                act.wait_ge(evac_v, tile_.order + 1)
                A(hid[0][:, j, :], hraw[1][:, j % 2, :], ACT.Copy).then_inc(hid_hi, 1)

            def swiglu_act(f, jw):
                nm, jobs, halves, h0, then = f
                norm_root(nm, added(jw))
                for g_, u_, j in jobs:
                    tile_in(g_[0])
                    if j >= 2:
                        act.wait_ge(evac_v, jobs[j - 2][1][0].order + 1)
                    A(hraw[0][:, j % 2, :], g_[2], ACT.Silu).then_inc(evac_a, 1)
                    if j:
                        hidden(j - 1, h0, jobs[j - 1][1][0])
                hidden(FT - 1, h0, jobs[FT - 1][1][0])
                exp_ln()
                norm_root(then, added_split(halves))

            if upto == "wo0":
                return
            swiglu_act(ffn[0], wo_jobs[0])
            if upto == "l0":
                return
            for t, _, dst, v, j, m in shift_jobs:
                tile_in(t)
                A(dst, v, ACT.Identity, scale=omu[0:m, j:j + 1]).then_inc(shifted, 1)
            act.wait_ge(evac_v, shift_jobs[-1][0].order + 1)
            plain(qm1_jobs)
            A(lo[0:64, :], lo[0:64, :], ACT.Tanh).then_inc(lora_in, 1)
            exp_ln()
            low = (lo2, lo3[0:32, :])
            for v in low:
                last = A(v, v, ACT.Exp, scale=-1.0)
            link(last)
            for v in low:
                last = A(v, v, ACT.Ln, bias=eps[0:v.shape[0], 3:4])
            link(last)
            for v in low:
                last = A(v, v, ACT.Exp, scale=-1.0)
            last.then_inc(lora_in, 1)
            attention("mem1")
            S0 = -DECAY

            def rp_squares(j):
                if j >= 2:
                    act.wait_ge(rp_done, j - 1)
                A(tmp[j % 2][3], kT7[:, j, :], ACT.Square, scale=col("rw_k_k", j)).then_inc(rp_square, 1)

            def rp_sigmoids(j):
                t, t_ = rp_tiles[j], tmp[j % 2]
                for i, (n, c0) in enumerate((("w", 0), ("a", 6))):
                    tile_in(t[n])
                    A(t_[i], bank[t[n].bank][:], ACT.Exp, scale=-1.0, bias=ncols[:, c0 + j:c0 + j + 1]).then_inc(evac_a, 1)
                act.wait_ge(evac_a, t["a"].order + 1)
                for i in range(2):
                    last = A(t_[i], t_[i], ACT.Ln, bias=eps[:, 3:4])
                link(last)
                for i in range(2):
                    last = A(t_[i], t_[i], ACT.Exp, scale=-1.0)
                last.then_inc(rp_sigma, 1)
                copy_out(t["g"], gT[:, j, :], bank[t["g"].bank][:])
                act.wait_ge(rp_max, j + 1)
                link(A(t_[2], t_[2], ACT.Ln))
                A(t_[2], t_[2], ACT.Exp, scale=-0.5).then_inc(rp_root, 1)

            rp_squares(0)
            rp_sigmoids(0)
            for j in range(JP):
                t_ = tmp[j % 2]
                if j + 1 < JP:
                    rp_squares(j + 1)
                act.wait_ge(rp_scan, j + 1)
                A(t_[6], t_[5], ACT.Exp, scale=-S0)
                A(t_[5], t_[5], ACT.Exp, scale=S0)
                A(t_[3], t_[0], ACT.Exp, scale=S0).then_inc(rp_exp, 1)
                if j + 1 < JP:
                    rp_sigmoids(j + 1)
            if upto == "rp":
                return
            m = wo_jobs[1][0][0].split
            split_to(splits_until(m + AHEAD, m))
            for c in range(NCH + 1):
                if c:
                    act.wait_ge(rs_t, RS_T.at("u", c - 1))
                    A(Um, jn(bank[7][:, 0:384]), ACT.Copy).then_inc(rs_a, 1)
                if c == NCH:
                    break
                for nm_, dst, b_ in (("tokb", BT, 4), ("tokk", KT, 5), ("tokv", VT, 4)):
                    act.wait_ge(rc_t, RC_T.at(nm_, c))
                    A(dst[c % 2], jn(bank[b_][:, 0:384]), ACT.Copy).then_inc(rc_a, 1)
                for l in range(1, 6):
                    for h in range(2):
                        act.wait_ge(rc_t, RC_T.at(f"y{l}{h}", c))
                        A(Ym[:, 3 * h:3 * h + 3, :], bank[h][:, 0:192].rearrange("p (j n) -> p j n", j=3),
                          ACT.Copy).then_inc(rc_a, 1)
            def gn_squares(j):
                act.wait_ge(gn_centred, j + 1)
                A(gtmp[j][0], rT[:, j, :], ACT.Square).then_inc(gn_square, 1)

            def gn_high(j):
                act.wait_ge(gn_out, j + 1)
                A(h_hi[:, j, :], rT[:, j, :], ACT.Copy).then_inc(mix_hi, 1)

            gn_squares(0)
            for j in range(JP):
                if j + 1 < JP:
                    gn_squares(j + 1)
                t = gn_tiles[j]["q"]
                tile_in(t)
                A(gtmp[j][1], bank[t.bank][:], ACT.Ln, scale=1.0 / HD, bias=eps[:, 2:3]).then_inc(evac_a, 1)
                act.wait_ge(evac_a, t.order + 1)
                A(gtmp[j][1], gtmp[j][1], ACT.Exp, scale=-0.5).then_inc(gn_root, 1)
                if j:
                    gn_high(j - 1)
            gn_high(JP - 1)
            if upto == "gn":
                return
            swiglu_act(ffn[1], wo_jobs[1])
            for k, t in enumerate(mem2_tiles):
                if t.eng == "a":
                    copy_out(t, memT2[:, 2 * k:2 * k + 2, :], bank[t.bank][:].rearrange("p (k m) -> p k m", k=2))
            m = mem2_jobs[0][0].split
            split_to(splits_until(m + AHEAD, m))
            read_out(act, mem2_tiles)
            norm_root(mem2_norm)
            plain(mem2_jobs)
            norm_root(n2a)
            if upto == "b1":
                return
            for t, _, dst, v in z_jobs:
                tile_in(t)
                A(dst, v, ACT.Silu).then_inc(evac_a, 1)
            for t, _, dst, v, c in conv_jobs:
                tile_in(t)
                A(dst, v, ACT.Identity, scale=col("conv_w_2", 18 + c), bias=col("conv_b_2", c)).then_inc(conv_a, 1)
            act.wait_ge(conv_v, 6)
            for c in range(6):
                A(xbc[:, c, :], xbc[:, c, :], ACT.Silu).then_inc(conv_a, 1)
            exp_ln()
            plain(qkv_jobs)
            A(bcast[:, 44:52], bcast[:, 44:52], ACT.Exp)
            act.wait_ge(gates_ready, 2)
            link(A(small[:, 2, :], small[:, 2, :], ACT.Exp))
            A(small[:, 2, :], small[:, 2, :], ACT.Ln, bias=eps[:, 3:4]).then_inc(sd_a, 1)
            copy_out(bt_tile, Btok, bank[bt_tile.bank][:])
            act.wait_ge(sd_v, 2)
            A(small[:, 3:5, :], small[:, 3:5, :], ACT.Exp).then_inc(sd_a, 1)
            for c in range(TT):
                act.wait_ge(sc_t, c + 1)
                if c:
                    act.wait_ge(ssd_ct, c)
                for g in range(2):
                    last = A(ER[g], bank[4 + g][:], ACT.Exp)
                last.then_inc(sc_a, 1)
                act.wait_ge(sc_v, SC_V.at("seg", c))
                for h in range(SH):
                    v = SEG[h // 4][:, (h % 4) * P:(h % 4) * P + P]
                    last = A(v, v, ACT.Exp, bias=small[:, 5, c * 8 + h:c * 8 + h + 1])
                last.then_inc(sc_a, 1)
            act.wait_ge(sd_v, 3)
            norm_root(nssd)
            def soft(u):
                v = T1[u % 2][:, (3 - u % 4) * P:S]
                act.wait_ge(sb_min, u + 1)
                A(v, v, ACT.Exp).then_inc(sb_exp, 1)
                act.wait_ge(sb_exp, u + 1)
                A(v, v, ACT.Ln, bias=eps[:, 3:4]).then_inc(sb_ln, 1)

            soft(0)
            for u in range(4 * SH):
                js = 3 - u % 4
                if u + 1 < 4 * SH:
                    soft(u + 1)
                act.wait_ge(sb_sums, u + 1)
                if u >= 4:
                    act.wait_ge(sb_pv, u // 4)
                A(WT[:, js, js * P:S], bank[4 + u % 3][:, js * P:S], ACT.Exp).then_inc(sb_weight, 1)
            act.wait_ge(sb_out, SH // 2)
            norm_root(nsb)
            norm_root(n2b, added(wout_jobs))
            plain(xq_jobs)
            attention("xa")
            norm_root(n2c, added(wxo_jobs))
            for t, _, j, v in ff1_jobs:
                tile_in(t)
                if j >= 2:
                    act.wait_ge(evac_v, ff1_jobs[j - 2][0].order + 1)
                A(hraw[0][:, j % 2, :], v, ACT.Relu, scale=FF_SCALE).then_inc(shifted, 1)
                if j:
                    hidden(j - 1, 2 * FT, ff1_jobs[j - 1][0])
            hidden(FFT - 1, 2 * FT, ff1_jobs[-1][0])
            norm_root(n2f, added_split(ff2_halves))
            for t, tt, kh in out_tiles:
                if t.eng == "a":
                    copy_out(t, out_sb[:, tt, kh * 512:kh * 512 + 512], bank[t.bank][:])

        @block.vector
        def _(dve):
            V = nc.vector
            link = chained(dve, chain_v)

            at, nqk = [0], [0]

            def split_to(m):
                while at[0] <= m:
                    w = splits[at[0]]
                    sl = at[0] % NSPLIT
                    dve.wait_ge(split_hi, at[0] + 1)
                    V.tensor_tensor(w_lo[:, sl, 0:w["size"]], wring[:, w["slot"], 0:w["size"]], w_hi[:, sl, 0:w["size"]],
                                    ALU.subtract).then_inc(split_lo, 1)
                    at[0] += 1

            def tile_in(t):
                if t.split is not None:
                    split_to(splits_until(t.split + AHEAD, t.split))
                dve.wait_ge(acc_full, t.n + 1)

            def copy_out(t, dst, v, scale=1.0):
                tile_in(t)
                if isinstance(scale, float) and scale == 1.0:
                    V.tensor_copy(dst, v).then_inc(evac_v, 1)
                else:
                    V.tensor_scalar(dst, v, scale, None, ALU.mult).then_inc(evac_v, 1)

            def plain(jobs):
                for t, _, dst, v, sc in jobs:
                    split_to(splits_until(t.split + AHEAD, t.split))
                    if isinstance(dst, list):
                        nqk[0] += 1
                        dve.wait_ge(qk_hi, nqk[0])
                        V.scalar_tensor_tensor(dst[1], v, sc, dst[0], ALU.mult, ALU.subtract).then_inc(evac_v, 1)
                    elif t.eng == "v":
                        copy_out(t, dst, v, sc)

            def norm_apply(nm):
                dve.wait_ge(rooted, nm["j"] + 1)
                n, pair_ = nm["n"], isinstance(nm["dst"], tuple)

                def rest(k):
                    dve.wait_ge(cast, nm["c"] + k + 1)
                    V.tensor_tensor(nm["dst"][1][:, k, 0:n], ntmp[:, k % 2, 0:n], nm["dst"][0][:, k, 0:n],
                                    ALU.subtract).then_inc(normed, 1)

                for k in range(nm["k"]):
                    dst = ntmp[:, k % 2, 0:n] if pair_ else nm["dst"][:, k, 0:n]
                    if pair_ and k >= 2:
                        dve.wait_ge(normed, nm["c"] + k - 1)
                    V.scalar_tensor_tensor(dst, nm["src"][:, k, 0:n], col(nm["gain"][0], nm["gain"][1] + k),
                                           rsb[:, 0:n], ALU.mult, ALU.mult).then_inc(scaled, 1)
                    if pair_ and k:
                        rest(k - 1)
                if pair_:
                    rest(nm["k"] - 1)

            def add_residual(jobs):
                for t, _, k, v in jobs:
                    tile_in(t)
                    V.tensor_tensor(xT[:, k, :], xT[:, k, :], v, ALU.add).then_inc(evac_v, 1)

            def add_split(halves, scale=1.0):
                for hf, ts, ps, h in halves:
                    for w, _, _ in ps:
                        split_to(splits_until(w["m"] + AHEAD, w["m"]))
                    for c, t in enumerate(ts):
                        tile_in(t)
                        x_ = xT[:, 4 * hf + c, :]
                        V.scalar_tensor_tensor(x_, bank[t.bank][:], scale, x_, ALU.mult, ALU.add).then_inc(evac_v, 1)

            def hidden(j, h0):
                dve.wait_ge(hid_hi, h0 + j + 1)
                V.tensor_tensor(hid[1][:, j, :], hraw[1][:, j % 2, :], hid[0][:, j, :], ALU.subtract).then_inc(hid_lo, 1)

            def attention(name):
                g0, g1 = att_stage[name]

                def shape(g):
                    n = g["n"]
                    N = g["N"]
                    dve.wait_ge(att_scores, n + 1)
                    for w, u in enumerate(g["units"]):
                        ins = V.tensor_tensor_reduce(g["s"][w][:, 0:N], g["s"][w][:, 0:N], u["D"], 1.0, -3.0e38,
                                                     ALU.add, ALU.max, g["st"][:, 0, w:w + 1])
                    link(ins)
                    V.tensor_scalar(g["st"][:, 1, :], g["st"][:, 0, :], -g["slope"], None, ALU.mult).then_inc(att_max, 1)

                def weigh(g):
                    st = g["st"]
                    dve.wait_ge(att_exp, g["n"] + 1)
                    link(V.reciprocal(st[:, 3, :], st[:, 2, :]))
                    if g["gates"] is not None:
                        link(V.tensor_tensor(st[:, 3, :], st[:, 3, :], g["gates"], ALU.mult))
                    for w in range(2):
                        p_ = g["P"][w][:, 0:g["N"]]
                        last = V.tensor_scalar(p_, p_, st[:, 3, w:w + 1], None, ALU.mult)
                    last.then_inc(att_weight, 1)

                def output(g):
                    if g["evac"] is not None:
                        dve.wait_ge(att_hi, g["out0"] + 1)
                        b_, c = g["evac"]
                        V.tensor_tensor(h_lo[:, c, :], b_[:], h_hi[:, c, :], ALU.subtract).then_inc(att_out, 1)

                for i in range(g0, g1 + TO_VALUES):
                    if i < g1:
                        shape(groups[i])
                    if g0 <= i - 1 < g1:
                        weigh(groups[i - 1])
                    if i - TO_VALUES >= g0:
                        output(groups[i - TO_VALUES])

            for k, t in enumerate(x_tiles):
                if t.eng == "v":
                    copy_out(t, xT[:, k, :], bank[t.bank][:])
            tile_in(vec_tile)
            link(V.tensor_copy(cols[:, 0:POS + 2 * CS], bank[vec_tile.bank][:, 0:POS + 2 * CS]))
            for hf in range(2):
                V.tensor_copy(dskip[hf * HD:hf * HD + HD, :], bcast[hf * HD:hf * HD + HD, 52 + hf:60:2])
            V.tensor_scalar(ncols[:, 0:12], cols[:, vec["rw_w0"]:vec["rw_w0"] + 12], -1.0, None, ALU.mult)
            V.tensor_scalar(omu[:, 0:20], cols[:, vec["rw_mu"]:vec["rw_mu"] + 20], -1.0, 1.0, ALU.mult, ALU.add)
            V.tensor_scalar(omu[:, 20:21], MUC(20), -1.0, 1.0, ALU.mult, ALU.add).then_inc(cols_ready, 1)
            dve.nop().then_inc(evac_v, 1)
            for k, t in enumerate(mem_tiles):
                if t.eng == "v":
                    copy_out(t, memT[:, 2 * k:2 * k + 2, :], bank[t.bank][:].rearrange("p (k m) -> p k m", k=2))
            split_to(splits_until(AHEAD, 0))
            for l in range(2):
                norm_apply(mem_norm[l])
                plain(mem_jobs[l])
            norm_apply(n1a)
            for t, _, dst, v, c in cmp_jobs:
                split_to(splits_until(t.split + AHEAD, t.split))
                if t.eng == "v":
                    tile_in(t)
                    for g in range(2):
                        gs = slice(g * HD, g * HD + HD)
                        V.tensor_copy(dst[0:HD, 2 * c + g, :], v[gs, :])
                        last = V.tensor_copy(dst[HD:P, 2 * c + g, 0:S - CS], v[gs, CS:S])
                    last.then_inc(evac_v, 1)
            split_to(nsa_jobs[0][0].split)
            for j in range(2):
                t = cmp_hid[j]
                tile_in(t)
                h_ = chid[:, j, :]
                link(V.tensor_copy(cbias[:], bank[t.bank][:, 200:201]))
                V.tensor_scalar(h_, bank[t.bank][:, 0:G1 * NCMP], cbias[:], None, ALU.add).then_inc(evac_v, 1)
                dve.wait_ge(evac_v, t.order + 1)
                link(V.tensor_tensor(ctmp[:], h_, h_, ALU.mult))
                link(V.tensor_scalar(ctmp[:], ctmp[:], 0.044715, 1.0, ALU.mult, ALU.add))
                link(V.tensor_tensor(ctmp[:], ctmp[:], h_, ALU.mult))
                V.tensor_scalar(ctmp[:], ctmp[:], -50.0, None, ALU.max).then_inc(gelu_in, 1)
                dve.wait_ge(gelu_exp, j + 1)
                link(V.tensor_scalar(ctmp[:], ctmp[:], 1.0, None, ALU.add))
                link(V.reciprocal(ctmp[:], ctmp[:]))
                ins = V.tensor_tensor(h_, h_, ctmp[:], ALU.mult)
                ins.then_inc(gelu_out, 1)
                dve.wait_ge(gelu_out, j + 1)
            plain(nsa_jobs)
            t, _, v = gate_job
            tile_in(t)
            V.tensor_tensor(gates[:], v, bcast[:, 0:36].unsqueeze(1).broadcast_to([P, TT, 36]), ALU.add).then_inc(evac_v, 1)
            dve.wait_ge(evac_v, t.order + 1)
            dve.nop().then_inc(gate_exp_in, 1)
            dve.wait_ge(gate_exp, 1)
            link(V.tensor_scalar(gates[:], gates[:], 1.0, None, ALU.add))
            link(V.reciprocal(gates[:], gates[:]))
            if upto == "nsa":
                return
            copy_out(cmp_res[0], kcb[:], bank[cmp_res[0].bank][:, 0:2 * NCMP].rearrange("p (c n) -> p c n", c=2))
            dve.wait_ge(evac_v, cmp_res[0].order + 1)
            link(V.tensor_copy(kcb_parts[0], kcb[:]))
            V.tensor_tensor(kcb_parts[1], kcb[:], kcb_parts[0], ALU.subtract).then_inc(kcb_split, 1)
            copy_out(cmp_res[1], vcb[:], bank[cmp_res[1].bank][0:NCMP, 0:KV].rearrange("p (g d) -> p g d", g=G1))
            dve.wait_ge(consts, 2)
            dve.wait_ge(cmp_s, 1)
            c48 = lambda i: cst[:, i, :]
            bc = lambda i: c48(i).unsqueeze(2).broadcast_to([P, 48, NCMP])
            for i in range(TT):
                for e in range(2):
                    x0 = i * H1 + 6 * e
                    last = V.tensor_tensor(CU[:, x0:x0 + 6, :], bank[2 * i + e][:, 0:6 * NCMP].rearrange("p (x n) -> p x n", x=6),
                                           distc[:, i:i + 1, :].broadcast_to([P, 6, NCMP]), ALU.add)
            link(last)
            link(V.tensor_reduce(c48(0), CU[:], AX.X, ALU.max))
            link(V.tensor_scalar(c48(0), c48(0), -1.0e20, None, ALU.max))
            link(V.tensor_tensor(CU[:], CU[:], bc(0), ALU.subtract))
            cu4 = CU.rearrange("p (i x) n -> p i x n", i=TT)
            V.tensor_tensor(cu4, cu4, cslope[:].unsqueeze(1).unsqueeze(3).broadcast_to([P, TT, H1, NCMP]),
                            ALU.mult).then_inc(cmp_u, 1)
            dve.wait_ge(cmp_e, 1)
            link(V.tensor_reduce(c48(1), CU[:], AX.X, ALU.add))
            link(V.tensor_scalar(c48(1), c48(1), 1.0e-30, None, ALU.max))
            link(V.reciprocal(c48(2), c48(1)))
            for e in range(2):
                w4 = c48(2).rearrange("p (i e a r) -> p i e a r", i=TT, e=2, a=2)[:, :, e]
                last = V.tensor_tensor(w4, w4, gates[:, :, 0:H1].rearrange("p i (a e r) -> p i a e r", a=2, e=2)[:, :, :, e], ALU.mult)
            link(last)
            V.tensor_tensor(CU[:], CU[:], bc(2), ALU.mult).then_inc(cmp_w, 1)
            for x in range(1, H1, 2):
                dve.wait_ge(cmp_t, x + 1)
                V.tensor_copy(PTc[0:NCMP, cmp_head(x), :], bank[x % 8][0:NCMP, :]).then_inc(cmp_ptv, 1)
            m = wo_jobs[0][0][0].split
            split_to(splits_until(m + AHEAD, m))
            attention("nsa")
            add_residual(wo_jobs[0])

            def swiglu_dve(f):
                nm, jobs, halves, h0, then = f
                norm_apply(nm)
                for g_, u_, j in jobs:
                    tile_in(u_[0])
                    dve.wait_ge(evac_a, g_[0].order + 1)
                    if j >= 2:
                        dve.wait_ge(hid_lo, h0 + j - 1)
                    V.tensor_tensor(hraw[1][:, j % 2, :], hraw[0][:, j % 2, :], u_[2], ALU.mult).then_inc(evac_v, 1)
                    if j:
                        hidden(j - 1, h0)
                hidden(FT - 1, h0)
                add_split(halves)
                norm_apply(then)

            if upto == "wo0":
                return
            swiglu_dve(ffn[0])
            if upto == "l0":
                return
            for t, _, dst, v, j, m in shift_jobs:
                split_to(splits_until(t.split + AHEAD, t.split))
                dve.wait_ge(shifted, j + 1)
                V.scalar_tensor_tensor(dst[:, 1:S], v[:, 0:S - 1], MUC(j)[0:m], dst[:, 1:S], ALU.mult, ALU.add).then_inc(evac_v, 1)
            attention("mem1")
            dve.wait_ge(consts, 3)

            def rp_bound(j):
                t = rp_tiles[j]["n"]
                tile_in(t)
                V.tensor_scalar(tmp[j % 2][2], bank[t.bank][:], 1.0e-24, None, ALU.max).then_inc(evac_v, 1)
                dve.wait_ge(evac_v, t.order + 1)
                dve.nop().then_inc(rp_max, 1)

            def rp_bonus(j):
                t = rp_tiles[j]["b"]
                tile_in(t)
                V.tensor_tensor(bonT[:, j, :], vT7[:, j, :], bank[t.bank][:], ALU.mult).then_inc(evac_v, 1)

            rp_bound(0)
            for j in range(JP):
                t0_, t1_, t2_, t3_, t4_, t5_, t6_ = tmp[j % 2]
                dve.wait_ge(rp_sigma, j + 1)
                link(V.tensor_tensor_scan(t5_, keep[:], t0_, 0.0, ALU.mult, ALU.add))
                V.tensor_tensor(t0_, t5_, t0_, ALU.subtract).then_inc(rp_scan, 1)
                dve.wait_ge(rp_root, j + 1)
                link(V.scalar_tensor_tensor(kkT[:, j, :], kT7[:, j, :], col("rw_k_k", j), t2_, ALU.mult, ALU.mult))
                V.tensor_tensor(bT[:, j, :], kkT[:, j, :], t1_, ALU.mult)
                link(V.tensor_scalar(t2_, t1_, -1.0, col("rw_k_a", j), ALU.add, ALU.mult))
                link(V.scalar_tensor_tensor(kT7[:, j, :], t2_, 1.0, kT7[:, j, :], ALU.add, ALU.mult))
                V.scalar_tensor_tensor(t4_, rT[:, j, :], col("rw_r_k", j), kT7[:, j, :], ALU.mult, ALU.mult).then_inc(rp_rk, 1)
                if j:
                    rp_bonus(j - 1)
                if j + 1 < JP:
                    rp_bound(j + 1)
                dve.wait_ge(rp_rk, j + 1)
                dve.wait_ge(rp_exp, j + 1)
                V.tensor_tensor(bT[:, j, :], bT[:, j, :], t6_, ALU.mult)
                V.tensor_tensor(kT7[:, j, :], kT7[:, j, :], t6_, ALU.mult)
                V.tensor_tensor(rT[:, j, :], rT[:, j, :], t5_, ALU.mult)
                V.tensor_copy(pc[:, j, :], t5_[:, CH - 1:S:CH])
                V.scalar_tensor_tensor(kkT[:, j, :], kkT[:, j, :], -1.0, t3_, ALU.mult, ALU.mult).then_inc(rp_done, 1)
            rp_bonus(JP - 1)
            dve.wait_ge(rp_done, JP)
            if upto == "rp":
                return
            m = wo_jobs[1][0][0].split
            split_to(splits_until(m + AHEAD, m))
            h3_ = lambda v: v.rearrange("p (h j n) -> p h j n", h=2, j=3)
            eyes = eye2[:].unsqueeze(1).unsqueeze(1).broadcast_to([P, 2, 3, HD])
            cm = causal.unsqueeze(1).broadcast_to([P, 3, P])

            def mask(c, name, dst, b0):
                dve.wait_ge(rc_t, RC_T.at(name, c))
                for q_ in range(2):
                    last = V.tensor_tensor(dst[:, 3 * q_:3 * q_ + 3, :],
                                           bank[b0 + q_][:, 0:384].rearrange("p (j n) -> p j n", j=3), cm, ALU.mult)
                last.then_inc(rc_v, 1)

            for c in range(NCH + 1):
                prep, d = c < NCH, c - 1
                ds = slice(d * CH, d * CH + CH)
                if d >= 0:
                    dve.wait_ge(rs_t, RS_T.at("x", d))
                    V.tensor_copy(Xm, jn(bank[6][:, 0:384])).then_inc(rs_v, 1)
                if prep:
                    if c >= 2:
                        dve.wait_ge(rc_p, 6 * (c - 1))
                    mask(c, "ga", GA[c % 2], 0)
                    mask(c, "gk", GK[c % 2], 2)
                if d >= 0:
                    dve.wait_ge(rs_t, RS_T.at("y", d))
                    V.tensor_copy(rT[:, :, ds], jn(bank[6][:, 0:384])).then_inc(rs_v, 1)
                    dve.wait_ge(rs_t, RS_T.at("s", d))
                    link(V.tensor_tensor(state[:], state[:], jn(bank[7][:, 0:384]), ALU.add))
                    V.tensor_tensor(state[:], state[:], pc[:, :, d:d + 1].broadcast_to([P, JP, HD]), ALU.mult).then_inc(rs_v, 1)
                    dve.wait_ge(rs_v, RS_V.at("s", d))
                if not prep:
                    break
                dve.wait_ge(rc_p, 6 * c + 1)
                dve.wait_ge(rc_t, RC_T.at("eye", c))
                V.tensor_tensor(T2[:, :, 1, :].rearrange("p h (j n) -> p h j n", j=3),
                                h3_(ALT[:, 0, :]), eyes, ALU.add)
                V.tensor_tensor(T2[:, :, 0, :].rearrange("p h (j n) -> p h j n", j=3),
                                h3_(bank[5][:, 0:384]), eyes, ALU.add).then_inc(rc_v, 1)
                for l in range(1, 6):
                    for h in range(2):
                        dve.wait_ge(rc_t, RC_T.at(f"t{l}{h}", c))
                        dve.wait_ge(rc_v, RC_V.at(f"t{l - 1}{h}" if l > 1 else "t0", c))
                        b_ = bank[2 + h]
                        if l < 5:
                            t_ = T2[:, h, :, :].rearrange("p w n -> p (w n)")
                            V.tensor_tensor(t_, t_, b_[:, 0:384], ALU.add).then_inc(rc_v, 1)
                        else:
                            V.tensor_tensor(TTf[c % 2][:, 3 * h:3 * h + 3, :],
                                            T2[:, h, 1, :].rearrange("p (j n) -> p j n", j=3),
                                            b_[:, 192:384].rearrange("p (j n) -> p j n", j=3), ALU.add).then_inc(rc_v, 1)
            def gn_centre(j):
                t = gn_tiles[j]["s"]
                tile_in(t)
                V.scalar_tensor_tensor(rT[:, j, :], bank[t.bank][:], -1.0 / HD, rT[:, j, :], ALU.mult, ALU.add).then_inc(evac_v, 1)
                dve.wait_ge(evac_v, t.order + 1)
                dve.nop().then_inc(gn_centred, 1)

            def gn_rest(j):
                dve.wait_ge(mix_hi, j + 1)
                V.tensor_tensor(h_lo[:, j, :], rT[:, j, :], h_hi[:, j, :], ALU.subtract).then_inc(gn_lo, 1)

            gn_centre(0)
            for j in range(JP):
                if j + 1 < JP:
                    gn_centre(j + 1)
                dve.wait_ge(gn_root, j + 1)
                link(V.scalar_tensor_tensor(rT[:, j, :], rT[:, j, :], col("rw_lnx_w", j), gtmp[j][1], ALU.mult, ALU.mult))
                link(V.scalar_tensor_tensor(rT[:, j, :], rT[:, j, :], col("rw_lnx_b", j), bonT[:, j, :], ALU.add, ALU.add))
                V.tensor_tensor(rT[:, j, :], rT[:, j, :], gT[:, j, :], ALU.mult).then_inc(gn_out, 1)
                if j:
                    gn_rest(j - 1)
            gn_rest(JP - 1)
            if upto == "gn":
                return
            add_residual(wo_jobs[1])
            swiglu_dve(ffn[1])
            for k, t in enumerate(mem2_tiles):
                if t.eng == "v":
                    copy_out(t, memT2[:, 2 * k:2 * k + 2, :], bank[t.bank][:].rearrange("p (k m) -> p k m", k=2))
            m = mem2_jobs[0][0].split
            split_to(splits_until(m + AHEAD, m))
            norm_apply(mem2_norm)
            plain(mem2_jobs)
            norm_apply(n2a)
            if upto == "b1":
                return
            for t, _, dst, v in z_jobs:
                split_to(splits_until(t.split + AHEAD, t.split))
            for n, (t, _, dst, v, c) in enumerate(conv_jobs):
                split_to(splits_until(t.split + AHEAD, t.split))
                dve.wait_ge(conv_a, n + 1)
                for s_ in (1, 2):
                    link(V.scalar_tensor_tensor(dst[:, s_:S], v[:, 0:S - s_], col("conv_w_2", 6 * (3 - s_) + c), dst[:, s_:S],
                                                ALU.mult, ALU.add))
                V.scalar_tensor_tensor(dst[:, 3:S], v[:, 0:S - 3], col("conv_w_2", c), dst[:, 3:S],
                                       ALU.mult, ALU.add).then_inc(evac_v, 1)
            dve.wait_ge(evac_v, conv_jobs[-1][0].order + 1)
            dve.nop().then_inc(conv_v, 6)
            t, _, v = dt_job
            tile_in(t)
            s8 = lambda i: small[:, i, :]
            s48 = lambda i: small[:, i, :].rearrange("p (c h) -> p c h", c=4)
            V.tensor_tensor(s48(0), v, bcast[:, 36:44].unsqueeze(1).broadcast_to([P, TT, 8]), ALU.add).then_inc(evac_v, 1)
            dve.wait_ge(evac_v, t.order + 1)
            link(V.tensor_scalar(s8(2), s8(0), -1.0, None, ALU.mult))
            link(V.tensor_tensor(s8(2), s8(2), s8(0), ALU.min))
            dve.nop().then_inc(gates_ready, 2)
            plain(qkv_jobs)
            dve.wait_ge(sd_a, 1)
            link(V.tensor_scalar(s8(0), s8(0), 0.0, None, ALU.max))
            link(V.tensor_tensor(s8(0), s8(0), s8(2), ALU.add))
            link(V.tensor_scalar(s8(2), s8(0), -1.0, None, ALU.mult))
            V.tensor_tensor(s48(1), s48(2), bcast[:, 44:52].unsqueeze(1).broadcast_to([P, TT, 8]), ALU.mult).then_inc(sd_v, 1)
            h3 = lambda v_: v_.rearrange("p (h d) -> p h d", h=8)
            for c, t in enumerate(xd_tiles):
                tile_in(t)
                V.tensor_tensor(h3(XD[:, c, :]), h3(bank[t.bank][:]),
                                small[:, 0, c * 8:c * 8 + 8].unsqueeze(2).broadcast_to([P, 8, HD]), ALU.mult).then_inc(evac_v, 1)
            tile_in(ac_tile)
            ab = bank[ac_tile.bank]
            link(V.tensor_scalar(s8(5), ab[:, 0:32], -1.0, None, ALU.mult))
            V.tensor_copy(s8(4), ab[:, 32:64])
            V.tensor_tensor(s8(3), s8(5), ab[:, 32:64], ALU.add).then_inc(evac_v, 1)
            dve.wait_ge(evac_v, ac_tile.order + 1)
            dve.nop().then_inc(sd_v, 1)
            dve.wait_ge(sd_a, 2)
            q4 = lambda v_: v_.rearrange("p (h l) -> p h l", h=4)
            dve.wait_ge(consts, 4)
            def ssd_prep(c):
                cs = slice(c * P, c * P + P)
                dve.wait_ge(sc_a, SC_A.at("er", c))
                if c:
                    dve.wait_ge(sc_v, SC_V.at("m", c - 1))
                for g in range(2):
                    last = V.tensor_tensor(q4(SEG[g]), q4(bank[4 + g][:]), hide_gt.unsqueeze(1).broadcast_to([P, 4, P]), ALU.add)
                last.then_inc(sc_v, 1)
                dve.wait_ge(sc_a, SC_A.at("e", c))
                for g in range(2):
                    last = V.tensor_tensor(q4(MM_[c % 2][g]), q4(SEG[g]), bank[(6, 2)[g]][:, 0:P].unsqueeze(1).broadcast_to([P, 4, P]),
                                           ALU.mult)
                last.then_inc(sc_v, 1)

            def ssd_finish(c):
                cs = slice(c * P, c * P + P)
                dve.wait_ge(sf_t, SF_T.at("y", c))
                for k in range(4):
                    last = V.scalar_tensor_tensor(yS[:, k, cs], xbc[:, k, cs], dskip[:, k:k + 1],
                                                  bank[(7, 1)[k // 2]][:, (k % 2) * P:(k % 2) * P + P],
                                                  ALU.mult, ALU.add)
                last.then_inc(sf_v, 1)
                dve.wait_ge(sf_t, SF_T.at("st", c))
                for g in range(2):
                    gs = slice(g * HD, g * HD + HD)
                    pv_ = bank[3][gs, 0:256].rearrange("p (h d) -> p h d", h=4)
                    cd = small[gs, 4, c * 8 + 4 * g:c * 8 + 4 * g + 4].unsqueeze(2).broadcast_to([HD, 4, HD])
                    if c == 0:
                        last = V.tensor_copy(SST[gs], pv_)
                    else:
                        link(V.tensor_tensor(SST[gs], SST[gs], cd, ALU.mult))
                        last = V.tensor_tensor(SST[gs], SST[gs], pv_, ALU.add)
                last.then_inc(sf_v, 1)
                dve.wait_ge(sf_v, SF_V.at("st", c))

            ssd_prep(0)
            for c in range(TT):
                if c + 1 < TT:
                    ssd_prep(c + 1)
                ssd_finish(c)
            for k in range(4):
                last = V.tensor_tensor(yS[:, k, :], yS[:, k, :], zT[:, k, :], ALU.mult)
            last.then_inc(sd_v, 1)
            norm_apply(nssd)
            def bounded(u):
                js = 3 - u % 4
                dve.wait_ge(sb_logits, u + 1)
                if u >= 2:
                    dve.wait_ge(sb_soft, u - 1)
                V.tensor_scalar(T1[u % 2][:, js * P:S], bank[4 + u % 3][:, js * P:S], 80.0, None, ALU.min).then_inc(sb_min, 1)

            for u in range(4 * SH):
                h, js = u // 4, 3 - u % 4
                z_ = bank[4 + u % 3][:, js * P:S]
                if u == 0:
                    bounded(0)
                dve.wait_ge(sb_ln, u + 1)
                if u >= 4:
                    dve.wait_ge(sb_sums, 4 * (u // 4))
                link(V.tensor_tensor(SP[:, js, js * P:S], T1[u % 2][:, js * P:S], z_, ALU.max))
                dg = SP[:, js, js * P:js * P + P]
                V.tensor_tensor(dg, dg, triu_s, ALU.mult).then_inc(sb_soft, 1)
                if u + 1 < 4 * SH:
                    bounded(u + 1)
                if u % 4 == 3 and u // 4 and (u // 4) % 2 == 0:
                    dve.wait_ge(sb_pv, u // 4)
                    V.tensor_copy(yB[:, u // 8 - 1, :], bank[7][:]).then_inc(sb_out, 1)
            dve.wait_ge(sb_pv, SH)
            V.tensor_copy(yB[:, 3, :], bank[7][:]).then_inc(sb_out, 1)
            norm_apply(nsb)
            if upto == "sb":
                return
            add_residual(wout_jobs)
            norm_apply(n2b)
            plain(xq_jobs)
            attention("xa")
            add_residual(wxo_jobs)
            norm_apply(n2c)
            for n, (t, _, j, v) in enumerate(ff1_jobs):
                split_to(splits_until(t.split + AHEAD, t.split))
                dve.wait_ge(shifted, len(shift_jobs) + n + 1)
                if j >= 2:
                    dve.wait_ge(hid_lo, 2 * FT + j - 1)
                V.scalar_tensor_tensor(hraw[1][:, j % 2, :], v, FF_SCALE, hraw[0][:, j % 2, :], ALU.mult,
                                       ALU.mult).then_inc(evac_v, 1)
                if j:
                    hidden(j - 1, 2 * FT)
            hidden(FFT - 1, 2 * FT)
            add_split(ff2_halves, FF_SCALE ** -2)
            norm_apply(n2f)
            for t, tt, kh in out_tiles:
                if t.eng == "v":
                    copy_out(t, out_sb[:, tt, kh * 512:kh * 512 + 512], bank[t.bank][:])


_OUT = (1, S, D)


def kernel(**inputs):
    import concourse.bacc as bacc
    from concourse.bass_utils import run_bass_kernel_spmd

    nc = bacc.Bacc("TRN2", target_bir_lowering=False, num_devices=1)
    arrays, args = {}, {}
    for name, value in inputs.items():
        v = np.ascontiguousarray(value)
        arrays[f"in_{name}"] = v
        args[name] = nc.dram_tensor(f"in_{name}", v.shape, mybir.dt.from_np(v.dtype), kind="ExternalInput").ap()
    out = nc.dram_tensor("out_x", _OUT, F32, kind="ExternalOutput").ap()
    block_stack(nc, args, out)
    r = run_bass_kernel_spmd(nc, [arrays], core_ids=[0])
    return r.results[0]["out_x"]
```
